# Optimizing a Trainium2 kernel written in Bass

```python
import math
import jax, jax.numpy as jnp
from jax import lax
import numpy as np

D_MODEL = 1024
BATCH = 1
SEQ = 256
DEPTH = 2

D_FF = 2816
EPS = 1e-6
Q_BLOCK = 128
NEG_INF = -1e30

MLA_HEADS = 8
MLA_NOPE_DIM = 64
MLA_ROPE_DIM = 32
MLA_V_DIM = 64
MLA_Q_RANK = 256
MLA_KV_RANK = 128
ROPE_BASE = 10000.0

DIFF_HEADS = 8
DIFF_HEAD_DIM = 32

POOL_WINDOWS = (2, 4, 8, 16)
POOL_GROUP = 128
POOL_WIDTH = POOL_GROUP * len(POOL_WINDOWS)

N_BRANCH = 3
BRANCH_WIDTH = 512

DIFF_QK = DIFF_HEADS * 2 * DIFF_HEAD_DIM
DIFF_V = DIFF_HEADS * 2 * DIFF_HEAD_DIM
GATE_WIDTH = N_BRANCH * D_MODEL
IN_SPLITS = (MLA_Q_RANK, MLA_KV_RANK, MLA_ROPE_DIM, DIFF_QK, DIFF_QK, DIFF_V, POOL_WIDTH, GATE_WIDTH)
IN_WIDTH = sum(IN_SPLITS)


def rmsnorm(x, g):
    xf = x.astype(jnp.float32)
    y = xf * lax.rsqrt(jnp.mean(xf * xf, axis=-1, keepdims=True) + EPS)
    return (y * g.astype(jnp.float32)).astype(x.dtype)

def swiglu(x, w_gate, w_up, w_down):
    return (jax.nn.silu(x @ w_gate) * (x @ w_up)) @ w_down

def rope(x, pos):
    half = x.shape[-1] // 2
    inv_freq = ROPE_BASE ** (-jnp.arange(half, dtype=jnp.float32) / half)
    ang = pos.astype(jnp.float32)[:, :, None, None] * inv_freq
    cos, sin = jnp.cos(ang), jnp.sin(ang)
    xf = x.astype(jnp.float32)
    x1, x2 = xf[..., :half], xf[..., half:]
    return jnp.concatenate([x1 * cos - x2 * sin, x2 * cos + x1 * sin], axis=-1).astype(x.dtype)

def sweep_query_blocks(fn, *qs):
    b, s = qs[0].shape[:2]
    nb = s // Q_BLOCK
    blocked = tuple(jnp.moveaxis(q.reshape((b, nb, Q_BLOCK) + q.shape[2:]), 1, 0) for q in qs)
    starts = jnp.arange(nb, dtype=jnp.int32) * Q_BLOCK
    out = lax.map(lambda a: fn(a[0], *a[1]), (starts, blocked))
    out = jnp.moveaxis(out, 0, 1)
    return out.reshape((b, s) + out.shape[3:])

def causal_mask(start, s):
    q_idx = start + jnp.arange(Q_BLOCK, dtype=jnp.int32)
    k_idx = jnp.arange(s, dtype=jnp.int32)
    return k_idx[None, :] <= q_idx[:, None]

def mla_mixer(c_q, c_kv, k_rope_raw, pos, q_norm, w_uq, kv_norm, w_ukv):
    b, s, _ = c_q.shape
    q = (rmsnorm(c_q, q_norm) @ w_uq).reshape(b, s, MLA_HEADS, MLA_NOPE_DIM + MLA_ROPE_DIM)
    q_nope, q_rope = q[..., :MLA_NOPE_DIM], rope(q[..., MLA_NOPE_DIM:], pos)
    kv = (rmsnorm(c_kv, kv_norm) @ w_ukv).reshape(b, s, MLA_HEADS, MLA_NOPE_DIM + MLA_V_DIM)
    k_nope, v = kv[..., :MLA_NOPE_DIM], kv[..., MLA_NOPE_DIM:]
    k_rope = rope(k_rope_raw[:, :, None, :], pos)[:, :, 0]
    scale = (MLA_NOPE_DIM + MLA_ROPE_DIM) ** -0.5

    def block(start, qn, qr):
        sc = jnp.einsum('bqhd,bkhd->bhqk', qn, k_nope) + jnp.einsum('bqhd,bkd->bhqk', qr, k_rope)
        sc = jnp.where(causal_mask(start, s), sc.astype(jnp.float32) * scale, NEG_INF)
        p = jax.nn.softmax(sc, axis=-1).astype(v.dtype)
        return jnp.einsum('bhqk,bkhd->bqhd', p, v)

    o = sweep_query_blocks(block, q_nope, q_rope)
    return o.reshape(b, s, MLA_HEADS * MLA_V_DIM)

def diff_mixer(q, k, v, pos, lq1, lk1, lq2, lk2, subln, lambda_init):
    b, s, _ = q.shape
    q = q.reshape(b, s, DIFF_HEADS, 2, DIFF_HEAD_DIM)
    k = k.reshape(b, s, DIFF_HEADS, 2, DIFF_HEAD_DIM)
    v = v.reshape(b, s, DIFF_HEADS, 2 * DIFF_HEAD_DIM)
    f32 = jnp.float32
    lam = (jnp.exp(jnp.sum(lq1.astype(f32) * lk1.astype(f32)))
           - jnp.exp(jnp.sum(lq2.astype(f32) * lk2.astype(f32))) + lambda_init)
    slopes = jnp.exp2(-8.0 * jnp.arange(1, DIFF_HEADS + 1, dtype=f32) / DIFF_HEADS)
    scale = DIFF_HEAD_DIM ** -0.5

    def block(start, qb, pb):
        sc = jnp.einsum('bqhmd,bkhmd->bmhqk', qb, k).astype(f32) * scale
        dist = jnp.abs(pb[:, :, None] - pos[:, None, :]).astype(f32)
        sc = sc - slopes[None, None, :, None, None] * dist[:, None, None]
        sc = jnp.where(causal_mask(start, s), sc, NEG_INF)
        p = jax.nn.softmax(sc, axis=-1)
        a = (p[:, 0] - lam * p[:, 1]).astype(v.dtype)
        return jnp.einsum('bhqk,bkhd->bqhd', a, v)

    o = sweep_query_blocks(block, q, pos)
    o = rmsnorm(o, subln) * (1.0 - lambda_init)
    return o.reshape(b, s, DIFF_HEADS * 2 * DIFF_HEAD_DIM)

def pool_mixer(p, pool_w, pool_b, pool_scale):
    b, s, _ = p.shape
    pf = p.astype(jnp.float32)
    cs = jnp.cumsum(pf, axis=1)
    t = jnp.arange(s, dtype=jnp.int32)
    outs = []
    for g, w in enumerate(POOL_WINDOWS):
        sl = slice(g * POOL_GROUP, (g + 1) * POOL_GROUP)
        c = cs[..., sl]
        prev = jnp.pad(c, ((0, 0), (w, 0), (0, 0)))[:, :s]
        cnt = jnp.minimum(t + 1, w).astype(jnp.float32)[None, :, None]
        outs.append((c - prev) / cnt - pf[..., sl])
    pooled = jnp.stack(outs, axis=2).astype(p.dtype)
    y = jnp.einsum('bsgc,gcd->bsgd', pooled, pool_w) + pool_b
    return y.reshape(b, s, POOL_WIDTH) * pool_scale

def first_inputs(seed: int = 0) -> dict:
    key = jax.random.key(seed)
    ks = iter(jax.random.split(key, 40))
    f32 = jnp.float32

    def dense(shape, fan_in):
        return jax.random.normal(next(ks), shape, f32) * fan_in ** -0.5

    def gain(shape):
        return 1.0 + 0.02 * jax.random.normal(next(ks), shape, f32)

    x = jax.random.normal(next(ks), (BATCH, SEQ, D_MODEL), f32)
    offset = jax.random.randint(next(ks), (BATCH, 1), 0, 1024, dtype=jnp.int32)
    positions = (jnp.arange(SEQ, dtype=jnp.int32)[None, :] + offset).astype(jnp.int32)
    return {
        "x": x,
        "positions": positions,
        "ffn1_norm": gain((DEPTH, D_MODEL)),
        "ffn1_w_gate": dense((DEPTH, D_MODEL, D_FF), D_MODEL),
        "ffn1_w_up": dense((DEPTH, D_MODEL, D_FF), D_MODEL),
        "ffn1_w_down": dense((DEPTH, D_FF, D_MODEL), D_FF),
        "mix_norm": gain((DEPTH, D_MODEL)),
        "w_in": dense((DEPTH, D_MODEL, IN_WIDTH), D_MODEL),
        "mla_q_norm": gain((DEPTH, MLA_Q_RANK)),
        "mla_w_uq": dense((DEPTH, MLA_Q_RANK, MLA_HEADS * (MLA_NOPE_DIM + MLA_ROPE_DIM)), MLA_Q_RANK),
        "mla_kv_norm": gain((DEPTH, MLA_KV_RANK)),
        "mla_w_ukv": dense((DEPTH, MLA_KV_RANK, MLA_HEADS * (MLA_NOPE_DIM + MLA_V_DIM)), MLA_KV_RANK),
        "diff_lambda_q1": 0.1 * jax.random.normal(next(ks), (DEPTH, DIFF_HEAD_DIM), f32),
        "diff_lambda_k1": 0.1 * jax.random.normal(next(ks), (DEPTH, DIFF_HEAD_DIM), f32),
        "diff_lambda_q2": 0.1 * jax.random.normal(next(ks), (DEPTH, DIFF_HEAD_DIM), f32),
        "diff_lambda_k2": 0.1 * jax.random.normal(next(ks), (DEPTH, DIFF_HEAD_DIM), f32),
        "diff_subln": gain((DEPTH, 2 * DIFF_HEAD_DIM)),
        "pool_w": dense((DEPTH, len(POOL_WINDOWS), POOL_GROUP, POOL_GROUP), POOL_GROUP),
        "pool_b": 0.01 * jax.random.normal(next(ks), (DEPTH, len(POOL_WINDOWS), POOL_GROUP), f32),
        "pool_scale": 1.0 + 0.05 * jax.random.normal(next(ks), (DEPTH, POOL_WIDTH), f32),
        "w_branch": dense((DEPTH, N_BRANCH, BRANCH_WIDTH, D_MODEL), BRANCH_WIDTH),
        "w_out": dense((DEPTH, D_MODEL, D_MODEL), D_MODEL),
        "ffn2_norm": gain((DEPTH, D_MODEL)),
        "ffn2_w_gate": dense((DEPTH, D_MODEL, D_FF), D_MODEL),
        "ffn2_w_up": dense((DEPTH, D_MODEL, D_FF), D_MODEL),
        "ffn2_w_down": dense((DEPTH, D_FF, D_MODEL), D_FF),
        "final_norm": gain((D_MODEL,)),
    }

def first_block(x, positions, ffn1_norm, ffn1_w_gate, ffn1_w_up, ffn1_w_down, mix_norm, w_in,
              mla_q_norm, mla_w_uq, mla_kv_norm, mla_w_ukv,
              diff_lambda_q1, diff_lambda_k1, diff_lambda_q2, diff_lambda_k2, diff_subln,
              pool_w, pool_b, pool_scale, w_branch, w_out,
              ffn2_norm, ffn2_w_gate, ffn2_w_up, ffn2_w_down, final_norm):
    b, s, d = x.shape
    split_idx = [int(v) for v in np.cumsum(IN_SPLITS)[:-1]]
    h = x
    for l in range(DEPTH):
        h = h + 0.5 * swiglu(rmsnorm(h, ffn1_norm[l]), ffn1_w_gate[l], ffn1_w_up[l], ffn1_w_down[l])

        u = rmsnorm(h, mix_norm[l])
        z = u @ w_in[l]
        c_q, c_kv, k_rope, dq, dk, dv, p_in, z_gate = jnp.split(z, split_idx, axis=-1)

        y_mla = mla_mixer(c_q, c_kv, k_rope, positions,
                          mla_q_norm[l], mla_w_uq[l], mla_kv_norm[l], mla_w_ukv[l])
        lambda_init = 0.8 - 0.6 * math.exp(-0.3 * l)
        y_diff = diff_mixer(dq, dk, dv, positions, diff_lambda_q1[l], diff_lambda_k1[l],
                            diff_lambda_q2[l], diff_lambda_k2[l], diff_subln[l], lambda_init)
        y_pool = pool_mixer(p_in, pool_w[l], pool_b[l], pool_scale[l])

        branches = jnp.stack([y_mla, y_diff, y_pool], axis=2)
        branches = jnp.einsum('bsnc,ncd->bsnd', branches, w_branch[l])
        gates = jax.nn.sigmoid(z_gate.reshape(b, s, N_BRANCH, d))
        merged = jnp.sum(gates * branches, axis=2)
        h = h + merged @ w_out[l]

        h = h + 0.5 * swiglu(rmsnorm(h, ffn2_norm[l]), ffn2_w_gate[l], ffn2_w_up[l], ffn2_w_down[l])
    return rmsnorm(h, final_norm)


GLA_HEADS = 4
GLA_DK = 128
GLA_DV = 128
GLA_QK = GLA_HEADS * GLA_DK
GLA_V = GLA_HEADS * GLA_DV
GLA_GATE_RANK = 16
GLA_GATE_NORM = 16.0
GLA_CHUNK = 64
GMLP_GROUPS = 4
GMLP_GROUP_CH = 128
GMLP_WIDTH = GMLP_GROUPS * GMLP_GROUP_CH
GMLP_CHUNK = 128
MOBA_HEADS = 4
MOBA_HD = 128
MOBA_W = MOBA_HEADS * MOBA_HD
MOBA_BLOCK = 256
MOBA_TOPK = 3
MOBA_QBLOCK = 64
ROPE_THETA = 500000.0
ROPE_DIMS = MOBA_HD // 4
BRANCH_W = 512
D_FF_2 = 4 * D_MODEL
IN_COLS = 2 * GLA_QK + 2 * GLA_V + GLA_GATE_RANK + 2 * GMLP_WIDTH + 3 * MOBA_W + N_BRANCH * D_MODEL
DEEPNORM_ALPHA = (2 * DEPTH) ** 0.25
DEEPNORM_BETA = (8 * DEPTH) ** -0.25
LN_EPS = 1e-5
RMS_EPS = 1e-6


def layer_norm(x, g, b):
    xf = x.astype(jnp.float32)
    mu = jnp.mean(xf, axis=-1, keepdims=True)
    xc = xf - mu
    var = jnp.mean(xc * xc, axis=-1, keepdims=True)
    return (xc * lax.rsqrt(var + LN_EPS) * g + b).astype(x.dtype)

def partial_rope(t, positions):
    half = ROPE_DIMS // 2
    inv = 1.0 / (ROPE_THETA ** (jnp.arange(half, dtype=jnp.float32) * (2.0 / ROPE_DIMS)))
    ang = positions.astype(jnp.float32)[:, :, None] * inv
    cos = jnp.cos(ang)[:, :, None, :]
    sin = jnp.sin(ang)[:, :, None, :]
    tr = t[..., :ROPE_DIMS].astype(jnp.float32)
    x1, x2 = tr[..., :half], tr[..., half:]
    rot = jnp.concatenate([x1 * cos - x2 * sin, x2 * cos + x1 * sin], axis=-1)
    return jnp.concatenate([rot.astype(t.dtype), t[..., ROPE_DIMS:]], axis=-1)

def gla_branch(q, k, v, g, lr, w_gate_up, b_gate, norm_w):
    B, S, _ = q.shape
    H, DK, DV, C = GLA_HEADS, GLA_DK, GLA_DV, GLA_CHUNK
    nC = S // C
    f32 = jnp.float32

    def heads(t, d):
        return t.astype(f32).reshape(B, nC, C, H, d).transpose(0, 3, 1, 2, 4)

    log_a = jax.nn.log_sigmoid((lr @ w_gate_up + b_gate).astype(f32)) / GLA_GATE_NORM
    bcum = jnp.cumsum(heads(log_a, DK), axis=3)
    qh = heads(q, DK) * (DK ** -0.5)
    kh = heads(k, DK)
    vh = heads(v, DV)
    q_dec = qh * jnp.exp(bcum)
    k_inv = kh * jnp.exp(-bcum)
    causal = jnp.tril(jnp.ones((C, C), dtype=bool))
    attn = jnp.where(causal, jnp.einsum('bhntd,bhnsd->bhnts', q_dec, k_inv), 0.0)
    o_intra = jnp.einsum('bhnts,bhnsv->bhntv', attn, vh)
    b_end = bcum[:, :, :, -1:, :]
    kv_chunk = jnp.einsum('bhnsd,bhnsv->bhndv', kh * jnp.exp(b_end - bcum), vh)
    decay = jnp.exp(b_end[:, :, :, 0, :])

    def step(state, inp):
        kv_n, dec_n = inp
        return dec_n[..., None] * state + kv_n, state

    _, states = lax.scan(step, jnp.zeros((B, H, DK, DV), f32),
                         (jnp.moveaxis(kv_chunk, 2, 0), jnp.moveaxis(decay, 2, 0)))
    states = jnp.moveaxis(states, 0, 2)
    o = o_intra + jnp.einsum('bhntd,bhndv->bhntv', q_dec, states)
    o = o.transpose(0, 2, 3, 1, 4).reshape(B, S, H, DV)
    o = o * lax.rsqrt(jnp.mean(o * o, axis=-1, keepdims=True) + RMS_EPS) * norm_w
    o = o.reshape(B, S, H * DV) * jax.nn.silu(g.astype(f32))
    return o.astype(q.dtype)

def gmlp_branch(z, ln_g, ln_b, w_s, b_s):
    B, S, _ = z.shape
    G, CH, C = GMLP_GROUPS, GMLP_GROUP_CH, GMLP_CHUNK
    z = jax.nn.gelu(z, approximate=False)
    u, v = jnp.split(z, 2, axis=-1)
    v = layer_norm(v, ln_g, ln_b).reshape(B, S // C, C, G, CH)
    w = w_s * jnp.tril(jnp.ones((C, C), dtype=w_s.dtype))
    vs = jnp.einsum('gts,bnsgc->bntgc', w, v) + b_s.T[None, None, :, :, None]
    return u * vs.reshape(B, S, GMLP_WIDTH)

def moba_branch(q, k, v, positions):
    B, S, _ = q.shape
    H, HD, BLK, QB = MOBA_HEADS, MOBA_HD, MOBA_BLOCK, MOBA_QBLOCK
    f32 = jnp.float32
    qh = partial_rope(q.reshape(B, S, H, HD), positions).transpose(0, 2, 1, 3)
    kh = partial_rope(k.reshape(B, S, H, HD), positions).transpose(0, 2, 1, 3)
    vh = v.reshape(B, S, H, HD).transpose(0, 2, 1, 3)
    n_blk = -(-S // BLK)
    s_pad = n_blk * BLK
    pad = ((0, 0), (0, 0), (0, s_pad - S), (0, 0))
    kh = jnp.pad(kh, pad)
    vh = jnp.pad(vh, pad)
    k_blocks = kh.reshape(B, H, n_blk, BLK, HD)
    v_blocks = vh.reshape(B, H, n_blk, BLK, HD)
    k_mean = jnp.mean(k_blocks.astype(f32), axis=3)
    own_blk = jnp.arange(S) // BLK
    fully_past = jnp.arange(n_blk)[None, :] < own_blk[:, None]
    gate = jnp.where(fully_past, jnp.einsum('bhsd,bhnd->bhsn', qh.astype(f32), k_mean), -jnp.inf)
    n_sel = min(MOBA_TOPK, n_blk)
    _, sel = lax.top_k(gate, n_sel)
    nQ = S // QB
    q_c = jnp.moveaxis(qh.reshape(B, H, nQ, QB, HD), 2, 0)
    sel_c = jnp.moveaxis(sel.reshape(B, H, nQ, QB, n_sel), 2, 0)
    starts = jnp.arange(nQ, dtype=jnp.int32) * QB
    gather = jax.vmap(jax.vmap(lambda blocks, ids: blocks[ids]))
    scale = HD ** -0.5

    def attend(args):
        qb, sb, start = args
        t = start + jnp.arange(QB)
        blk_start = (start // BLK) * BLK
        kg = gather(k_blocks, sb)
        vg = gather(v_blocks, sb)
        s_g = jnp.einsum('bhqd,bhqjkd->bhqjk', qb, kg).astype(f32) * scale
        valid = jnp.arange(n_sel)[None, :] < (t // BLK)[:, None]
        s_g = jnp.where(valid[:, :, None], s_g, -jnp.inf).reshape(B, H, QB, n_sel * BLK)
        k_own = lax.dynamic_slice_in_dim(kh, blk_start, BLK, axis=2)
        v_own = lax.dynamic_slice_in_dim(vh, blk_start, BLK, axis=2)
        s_o = jnp.einsum('bhqd,bhkd->bhqk', qb, k_own).astype(f32) * scale
        s_o = jnp.where((blk_start + jnp.arange(BLK))[None, :] <= t[:, None], s_o, -jnp.inf)
        p = jax.nn.softmax(jnp.concatenate([s_g, s_o], axis=-1), axis=-1).astype(vh.dtype)
        p_g = p[..., :n_sel * BLK].reshape(B, H, QB, n_sel, BLK)
        return (jnp.einsum('bhqjk,bhqjkd->bhqd', p_g, vg)
                + jnp.einsum('bhqk,bhkd->bhqd', p[..., n_sel * BLK:], v_own))

    out = lax.map(attend, (q_c, sel_c, starts))
    out = jnp.moveaxis(out, 0, 2).reshape(B, H, S, HD)
    return out.transpose(0, 2, 1, 3).reshape(B, S, MOBA_W)

def mixer_sublayer(x, positions, w_in, w_gate_up, b_gate, gla_norm_w, gmlp_ln_g, gmlp_ln_b,
                   gmlp_w_s, gmlp_b_s, w_branch, w_out):
    sizes = [GLA_QK, GLA_QK, GLA_V, GLA_V, GLA_GATE_RANK, 2 * GMLP_WIDTH,
             MOBA_W, MOBA_W, MOBA_W, N_BRANCH * D_MODEL]
    offsets = [int(o) for o in np.cumsum(sizes)[:-1]]
    proj = x @ w_in
    gq, gk, gv, gg, glr, gz, mq, mk, mv, gl = jnp.split(proj, offsets, axis=-1)
    a = gla_branch(gq, gk, gv, gg, glr, w_gate_up, b_gate, gla_norm_w) @ w_branch[0]
    b = gmlp_branch(gz, gmlp_ln_g, gmlp_ln_b, gmlp_w_s, gmlp_b_s) @ w_branch[1]
    c = moba_branch(mq, mk, mv, positions) @ w_branch[2]
    ga, gb, gc = jnp.split(jax.nn.sigmoid(gl), N_BRANCH, axis=-1)
    return (ga * a + gb * b + gc * c) @ w_out

def second_inputs(seed: int = 0) -> dict:
    key = jax.random.key(seed)
    ks = jax.random.split(key, 20)
    L, D = DEPTH, D_MODEL
    nrm = lambda k, shape, s: jax.random.normal(k, shape, jnp.float32) * s
    offset = jax.random.randint(ks[1], (BATCH, 1), 0, 1024, dtype=jnp.int32)
    return {
        'x': nrm(ks[0], (BATCH, SEQ, D), 1.0),
        'positions': offset + jnp.arange(SEQ, dtype=jnp.int32)[None, :],
        'w_in': nrm(ks[2], (L, D, IN_COLS), D ** -0.5),
        'w_gate_up': nrm(ks[3], (L, GLA_GATE_RANK, GLA_QK), GLA_GATE_RANK ** -0.5),
        'b_gate': nrm(ks[4], (L, GLA_QK), 0.1),
        'gla_norm_w': 1.0 + nrm(ks[5], (L, GLA_DV), 0.02),
        'gmlp_ln_g': 1.0 + nrm(ks[6], (L, GMLP_WIDTH), 0.02),
        'gmlp_ln_b': nrm(ks[7], (L, GMLP_WIDTH), 0.02),
        'gmlp_w_s': nrm(ks[8], (L, GMLP_GROUPS, GMLP_CHUNK, GMLP_CHUNK), 0.5 * GMLP_CHUNK ** -0.5),
        'gmlp_b_s': 1.0 + nrm(ks[9], (L, GMLP_GROUPS, GMLP_CHUNK), 0.1),
        'w_branch': nrm(ks[10], (L, N_BRANCH, BRANCH_W, D), BRANCH_W ** -0.5),
        'w_out': nrm(ks[11], (L, D, D), DEEPNORM_BETA * D ** -0.5),
        'ln1_g': 1.0 + nrm(ks[12], (L, D), 0.02),
        'ln1_b': nrm(ks[13], (L, D), 0.02),
        'w_ff1': nrm(ks[14], (L, D, D_FF_2), D ** -0.5),
        'w_ff2': nrm(ks[15], (L, D_FF_2, D), DEEPNORM_BETA * D_FF_2 ** -0.5),
        'ln2_g': 1.0 + nrm(ks[16], (L, D), 0.02),
        'ln2_b': nrm(ks[17], (L, D), 0.02),
    }

def second_block(x, positions, w_in, w_gate_up, b_gate, gla_norm_w, gmlp_ln_g, gmlp_ln_b, gmlp_w_s,
              gmlp_b_s, w_branch, w_out, ln1_g, ln1_b, w_ff1, w_ff2, ln2_g, ln2_b):
    for l in range(DEPTH):
        mix = mixer_sublayer(x, positions, w_in[l], w_gate_up[l], b_gate[l], gla_norm_w[l],
                             gmlp_ln_g[l], gmlp_ln_b[l], gmlp_w_s[l], gmlp_b_s[l], w_branch[l], w_out[l])
        x = layer_norm(DEEPNORM_ALPHA * x + mix, ln1_g[l], ln1_b[l])
        ff = jnp.square(jax.nn.relu(x @ w_ff1[l])) @ w_ff2[l]
        x = layer_norm(DEEPNORM_ALPHA * x + ff, ln2_g[l], ln2_b[l])
    return x


def setup_inputs(seed=0):
    out = dict(first_inputs(seed))
    for name, value in second_inputs(seed + 1).items():
        if name != "x":
            out[name + "_2"] = value
    return out


def reference(
    x, positions, ffn1_norm, ffn1_w_gate, ffn1_w_up, ffn1_w_down, mix_norm, w_in, mla_q_norm,
    mla_w_uq, mla_kv_norm, mla_w_ukv, diff_lambda_q1, diff_lambda_k1, diff_lambda_q2,
    diff_lambda_k2, diff_subln, pool_w, pool_b, pool_scale, w_branch, w_out, ffn2_norm,
    ffn2_w_gate, ffn2_w_up, ffn2_w_down, final_norm, positions_2, w_in_2, w_gate_up_2, b_gate_2,
    gla_norm_w_2, gmlp_ln_g_2, gmlp_ln_b_2, gmlp_w_s_2, gmlp_b_s_2, w_branch_2, w_out_2,
    ln1_g_2, ln1_b_2, w_ff1_2, w_ff2_2, ln2_g_2, ln2_b_2,
):
    x = first_block(
        x, positions, ffn1_norm, ffn1_w_gate, ffn1_w_up, ffn1_w_down, mix_norm, w_in,
        mla_q_norm, mla_w_uq, mla_kv_norm, mla_w_ukv, diff_lambda_q1, diff_lambda_k1,
        diff_lambda_q2, diff_lambda_k2, diff_subln, pool_w, pool_b, pool_scale, w_branch, w_out,
        ffn2_norm, ffn2_w_gate, ffn2_w_up, ffn2_w_down, final_norm,
    )
    return second_block(
        x, positions_2, w_in_2, w_gate_up_2, b_gate_2, gla_norm_w_2, gmlp_ln_g_2, gmlp_ln_b_2,
        gmlp_w_s_2, gmlp_b_s_2, w_branch_2, w_out_2, ln1_g_2, ln1_b_2, w_ff1_2, w_ff2_2,
        ln2_g_2, ln2_b_2,
    )


_drawn_inputs = setup_inputs


def setup_inputs(seed=0):
    import zlib

    import numpy as np

    out = dict(_drawn_inputs(seed))
    spreads = {}
    factors = {'ffn1_norm': 3.92,
     'mla_q_norm': 8.0,
     'mla_kv_norm': 8.0,
     'diff_subln': 4.971,
     'pool_b': 7.507,
     'ffn2_norm': 5.323,
     'b_gate_2': 7.532,
     'gla_norm_w_2': 27.726,
     'gmlp_ln_g_2': 52.151,
     'gmlp_ln_b_2': 47.922,
     'gmlp_b_s_2': 3.007}
    for name, (base, spread) in spreads.items():
        noise = np.random.default_rng([zlib.crc32(name.encode()), seed]).standard_normal(out[name].shape)
        drawn = base * np.exp(spread * noise) if base else spread * noise
        out[name] = __import__('jax').numpy.asarray(drawn.astype(out[name].dtype))
    for name, factor in factors.items():
        out[name] = (out[name] * factor).astype(out[name].dtype)
    return out
```

```python
import math
from collections import deque
from contextlib import ExitStack

import numpy as np
import concourse.bass as bass
from concourse import mybir

F32 = mybir.dt.float32
F32R = mybir.dt.float32r
I32 = mybir.dt.int32
U32 = mybir.dt.uint32
ALU = mybir.AluOpType
ACT = mybir.ActivationFunctionType
AXX = mybir.AxisListType.X

P = 128
D = 1024
S = 256
L = 2
FF1 = 2816
FF2 = 4096
IN1 = 5536
IN2 = 7696
EPS = 1e-6
LN_EPS = 1e-5
ALPHA = (2 * L) ** 0.25
BIG = 1e30
TWO_PI = (6.28125, 0.0019350051879882812, 3.0199158306745e-07)
MAGIC = 12582912.0

NRAW, NW = 3, 4
UCOLS = 2048


class Ops:

    def activation(self, *a, **k):
        return lambda e: e.activation(*a, **k)

    def matmul(self, *a, **k):
        return lambda e: e.matmul(*a, **k)

    def transpose(self, *a, **k):
        return lambda e: e.transpose(*a, **k)

    def memset(self, *a, **k):
        return lambda e: e.memset(*a, **k)

    def tensor_copy(self, *a, **k):
        return lambda e: e.tensor_copy(*a, **k)

    def tensor_tensor(self, *a, **k):
        return lambda e: e.tensor_tensor(*a, **k)

    def tensor_scalar(self, *a, **k):
        return lambda e: e.tensor_scalar(*a, **k)

    def scalar_tensor_tensor(self, *a, **k):
        return lambda e: e.scalar_tensor_tensor(*a, **k)

    def tensor_tensor_scan(self, *a, **k):
        return lambda e: e.tensor_tensor_scan(*a, **k)

    def tensor_reduce(self, *a, **k):
        return lambda e: e.tensor_reduce(*a, **k)

    def reciprocal(self, *a, **k):
        return lambda e: e.reciprocal(*a, **k)

    def copy_predicated(self, *a, **k):
        return lambda e: e.copy_predicated(*a, **k)

    def bn_stats(self, *a, **k):
        return lambda e: e.bn_stats(*a, **k)

    def bn_aggr(self, *a, **k):
        return lambda e: e.bn_aggr(*a, **k)

    def dma_start(self, *a, **k):
        return lambda e: e.dma_start(*a, **k)


OPS = Ops()


class Queue:

    def __init__(self, sem):
        self.sem, self.count, self.items = sem, 0, []

    def put(self, fn, *waits, inc=True):
        self.count += inc
        self.items.append((waits, fn(OPS), self.sem if inc else None, 1))
        return (self.sem, self.count)

    def dma(self, out, in_, sem, value, *waits):
        self.items.append((waits, OPS.dma_start(out, in_), sem, 16))
        return (sem, value)

    def last(self):
        return (self.sem, self.count)

    def issue(self, eng):
        seen = {}
        for waits, ins, sem, by in self.items:
            for s, v in waits:
                if v > seen.get(s.name, 0):
                    eng.wait_ge(s, v)
                    seen[s.name] = v
            r = ins(eng)
            if sem is not None:
                r.then_inc(sem, by)


class Buf:

    def __init__(self, ap):
        self.ap, self.free = ap, []

    def __getitem__(self, k):
        return self.ap[k]


def constants():
    ident = np.eye(P, dtype=np.float32)
    q = np.arange(P)
    mask = np.zeros((P, 384), np.float32)
    mask[:, 0:128] = np.where(np.arange(128)[None] <= q[:, None], 0.0, -BIG)
    mask[:, 128:384] = np.where(np.arange(256)[None] <= q[:, None] + 128, 0.0, -BIG)
    half = np.arange(16, dtype=np.float64)
    f1 = (10000.0 ** (-half / 16)).astype(np.float32)
    f2 = (1.0 / (500000.0 ** (half * (2.0 / 32)))).astype(np.float32)
    freq = np.broadcast_to(np.stack([f1, f1, f2, f2]).reshape(1, 64), (P, 64))
    pool = np.zeros((256, 4, 256), np.float64)
    for g, w in enumerate((2, 4, 8, 16)):
        for t in range(256):
            lo = max(0, t - w + 1)
            pool[lo:t + 1, g, t] += 1.0 / (t + 1 - lo)
            pool[t, g, t] -= 1.0
    pool = pool.astype(np.float32)
    p0 = pool[0:128].reshape(P, 1024)
    p1 = pool[128:256, :, 128:256].reshape(P, 512)
    s = q[:, None]
    t = q[None, :]
    tril = (s <= t).astype(np.float32)
    chunk = ((s <= t) & (s // 64 == t // 64)).astype(np.float32)
    scan = np.broadcast_to((np.arange(S) % 64 != 0).astype(np.float32), (P, S))
    return {
        "c_ident": ident, "c_mask": mask, "c_freq": np.ascontiguousarray(freq),
        "c_pool": np.ascontiguousarray(np.concatenate([p0, p1], 1)),
        "c_tril": np.concatenate([tril, chunk], 1),
        "c_scan": np.ascontiguousarray(scan),
    }


class Turned:

    def __init__(self, name, h, l):
        self.name, self.h, self.l, self.ready, self.used = name, h, l, {}, {}


class Net:
    def __init__(self, nc, A, out, ctx):
        self.nc, self.A, self.out, self.ctx = nc, A, out, ctx
        self.s_eng = [self.sem(n) for n in ("s_pe", "s_act", "s_dve", "s_pool", "s_sp")]
        self.s_raw = [self.sem(f"s_raw{i}") for i in range(NRAW)]
        self.s_out = self.sem("s_out")
        self.s_ld = {}
        self.memory()

    def reset(self, plan):
        self.plan = plan
        self.units = []
        self.pe, self.act, self.dve, self.pool, self.sp = (Queue(s) for s in self.s_eng)
        for e in self.s_ld.values():
            e[1] = 0
        for b in self.pb + self.gain:
            b.free = []
        self.gain_n = self.n_side = self.n_split = 0
        self.split_tok, self.raw_free, self.done_tok = {}, {}, {}
        self.lanes = [deque() for _ in range(4)]

    def sem(self, name):
        return self.ctx.enter_context(self.nc.semaphore(name))

    def at(self, name, off, shape, dt=F32):
        n = 1
        for x in shape[1:]:
            n *= x
        assert off + 4 * n <= self.top, name
        return self.nc.alloc_sbuf_tensor_at(name, shape, dt, offset=off)

    def memory(self):
        nc = self.nc
        base = (nc.sbuf_base + 63) // 64 * 64
        self.top = nc.sbuf_usable_end
        off = [base]

        def take(nbytes):
            o = off[0]
            off[0] += (nbytes + 31) // 32 * 32
            assert off[0] <= self.top, (off[0], self.top)
            return o

        A = self.at
        self.h = A("h", take(8192), [P, 2, D])
        o_xn = take(8192)
        self.xn = A("xn", o_xn, [P, 2, D])
        self.xh = A("xh", take(8192), [P, 8, S], F32R)
        self.xl = A("xl", take(8192), [P, 8, S], F32R)
        o_m = take(24576)
        self.mh = A("mh", o_m, [P, 12, S], F32R)
        self.ml = A("ml", o_m + 12288, [P, 12, S], F32R)
        self.raw = [A(f"raw{i}", take(8192), [P, UCOLS]) for i in range(NRAW)]
        self.wh = [A(f"wh{i}", take(8192), [P, UCOLS], F32R) for i in range(NW)]
        self.wl = [A(f"wl{i}", take(8192), [P, UCOLS], F32R) for i in range(NW)]
        self.gain = [Buf(A(f"gain{i}", take(4096), [P, D])) for i in range(2)]
        self.ident = A("ident", take(512), [P, P])
        self.ones = A("ones", take(512), [P, P])
        self.mask = A("mask", take(1536), [P, 384])
        self.dist = A("dist", take(1536), [P, 384])
        self.cs = A("cs", take(512), [P, 2, 2, 2, 16])
        self.half_pi = A("half_pi", take(4), [P, 1])
        self.one = A("one", take(4), [P, 1])
        self.nhalf = A("nhalf", take(4), [P, 1])
        self.lam = A("lam", take(8), [P, 2])
        self.bn = A("bn", take(128), [P, 2, 16])
        self.epsc = A("epsc", take(32), [P, 8])
        self.st = A("st", take(256), [P, 64])
        o_ck = take(512)
        o_r = take(0)
        n_r = self.top - o_r
        self.left = n_r
        r = [o_r]

        def rt(nbytes):
            o = r[0]
            r[0] += (nbytes + 31) // 32 * 32
            assert r[0] <= self.top, (r[0] - self.top)
            return o

        self.sg = [A(f"sg{t}", rt(2048), [P, 512]) for t in range(2)]
        self.mn = [A(f"mn{t}", rt(2048), [P, 512]) for t in range(2)]
        r[0] = o_r
        o_g = [rt(8192), rt(8192)]
        self.G = [A(f"G{i}", o_g[i], [P, 2, D]) for i in range(2)]
        o_lane = [rt(3584) for _ in range(3)]
        self.lS = [[A(f"lS{i}{j}", o_lane[i] + 1536 * j, [P, 384]) for j in range(2)] for i in range(3)]
        self.lQ = [A(f"lQ{i}", o_lane[i] + 1536, [P, 512]) for i in range(3)]
        self.lG = [A(f"lG{i}", o_lane[i], [P, 7, P]) for i in range(3)]
        self.pos_i = A("pos_i", o_lane[1], [P, S], I32)
        self.pos_c = A("pos_c", o_lane[1] + 1024, [P, 4], I32)
        self.pos_f = A("pos_f", o_lane[1] + 1088, [P, 4])
        self.pos_r = A("pos_r", o_lane[1] + 1536, [P, S])
        self.lams = A("lams", o_lane[0], [P, 2 * 128])
        self.lamt = A("lamt", o_lane[0] + 1024, [P, 32])
        self.ang = A("ang", o_lane[2], [P, 64])
        self.angk = A("angk", o_lane[2] + 256, [P, 64])
        self.freq = A("freq", o_lane[2] + 512, [P, 64])
        self.tril = A("tril", o_g[1] + 4096, [P, P])
        self.lane_free = [[] for _ in range(3)]
        self.scan = A("scan", rt(1024), [P, S])
        o_r2 = r[0]
        self.dqT = A("dqT", o_m, [P, 4, S])
        self.dkT = A("dkT", o_m + 4096, [P, 4, S])
        self.dv = A("dv", o_m + 8192, [P, 2, 512])
        self.v = A("v", o_m + 12288, [P, 2, 512])
        self.yph = A("yph", o_m + 16384, [P, 4, S], F32R)
        self.ypl = A("ypl", o_m + 20480, [P, 4, S], F32R)
        self.pin = A("pin", rt(4096), [P, 2, 512])
        self.q = A("q", rt(6144), [P, 2, 8, 96])
        o_kt = rt(8192)
        self.kT = A("kT", o_kt, [P, 8, S])
        self.pc = A("pc", o_kt, [P, 1536])
        self.pw = A("pw", o_kt + 6144, [P, 4, P])
        self.rope_tmp = A("rope_tmp", o_xn, [P, 512])
        self.sq = A("sq", o_m + 20480, [P, 2, 512])
        self.ch = A("ch", o_xn, [P, 3, S], F32R)
        self.cl = A("cl", o_xn + 3072, [P, 3, S], F32R)
        self.cn = A("cn", o_xn + 6144, [P, 384])
        self.pT = A("pT", o_g[1], [P, 4, S])
        self.gq = A("gq", rt(1536), [P, 384])
        self.sub = A("sub", rt(256), [P, 64])
        self.kr = A("kr", rt(768), [P, 2, 96])
        self.pbs = A("pbs", rt(32), [P, 8])
        self.left1 = self.top - r[0]
        r[0] = o_r2
        self.gqT = A("gqT", o_m, [P, 4, S])
        self.gkT = A("gkT", o_m + 4096, [P, 4, S])
        self.ggT = A("ggT", o_m + 8192, [P, 4, S])
        self.gv = A("gv", o_m + 12288, [P, 2, 512])
        o_bl, o_be = rt(4096), rt(4096)
        self.bigL = A("bigL", o_bl, [P, 4, S])
        self.bigE = A("bigE", o_be, [P, 4, S])
        self.lng = A("lng", o_bl, [P, 2, 512])
        self.ws = A("ws", o_be, [P, 4, P])
        self.wsT = A("wsT", o_be + 2048, [P, 4, P])
        self.zu = A("zu", o_xn, [P, 2, 512])
        self.zv = A("zv", o_xn + 4096, [P, 2, 512])
        self.mq = A("mq", rt(4096), [P, 2, 4, P])
        self.mk = A("mk", rt(4096), [P, 2, 4, P])
        self.mv = A("mv", rt(4096), [P, 2, 512])
        self.wgu = A("wgu", rt(2048), [P, 512])
        self.gp = A("gp", rt(64), [P, 9])
        self.chunk = A("chunk", o_ck, [P, P], U32)
        self.lr = A("lr", rt(128), [P, 2, 16])
        self.lrT = A("lrT", o_xn, [P, S])
        self.left2 = self.top - r[0]
        self.pb = [Buf(self.ctx.enter_context(nc.psum_tensor(f"pb{i}", [P, 512], F32))) for i in range(8)]
        self.main = [[self.pb[0], self.pb[1]], [self.pb[2], self.pb[3]]]

    def fetch(self, j):
        if self.plan is None or j >= len(self.plan):
            return
        name, ix, k0, kt, n0, n = self.plan[j]
        src = self.A[name]
        for i in ix:
            src = src[i]
        src = src[k0:k0 + P * kt, n0:n0 + n].rearrange("(k p) n -> p k n", p=P)
        dst = self.raw[j % NRAW][:, 0:kt * n].rearrange("p (k n) -> p k n", n=n)
        self.sp.dma(dst, src, self.s_raw[j % NRAW], None, *self.raw_free.get(j - NRAW, []))

    def split(self, j):
        name, ix, k0, kt, n0, n = self.plan[j]
        c = kt * n
        raw = self.raw[j % NRAW][:, 0:c]
        hi, lo = self.wh[j % NW], self.wl[j % NW]
        landed = (self.s_raw[j % NRAW], 16 * (j // NRAW + 1))
        free = self.done_tok.get(j - NW, [])
        a = self.act.put(lambda e: e.activation(hi[:, 0:c], raw, ACT.Copy), landed, *free)
        v = self.dve.put(lambda e: e.tensor_tensor(lo[:, 0:c], raw, hi[:, 0:c].bitcast(F32), ALU.subtract),
                         a, *free)
        self.split_tok[j] = [a, v]
        self.raw_free[j] = [a, v]
        self.fetch(j + NRAW)

    def advance(self):
        if self.plan is None:
            return
        while self.n_split < len(self.plan) and (self.n_split < NW or self.n_split - NW in self.done_tok):
            self.split(self.n_split)
            self.n_split += 1

    def take(self, key):
        self.units.append(key)
        return len(self.units) - 1

    def weights(self, j):
        _, _, _, kt, _, n = self.plan[j]
        hi, lo = self.wh[j % NW], self.wl[j % NW]
        self.advance()
        assert j < self.n_split
        return tuple(w[:, 0:kt * n].rearrange("p (k n) -> p k n", n=n) for w in (hi, lo))

    def pump(self):
        for lane in self.lanes:
            if lane:
                try:
                    next(lane[0])
                except StopIteration:
                    lane.popleft()

    def drain(self, n=None):
        lanes = self.lanes if n is None else [self.lanes[n]]
        while any(lanes):
            for lane in lanes:
                if lane:
                    try:
                        next(lane[0])
                    except StopIteration:
                        lane.popleft()

    def tick(self):
        self.advance()
        self.pump()

    def side(self):
        self.n_side += 1
        return self.pb[4 + self.n_side % 4]

    def fence(self):
        return [self.pe.last(), self.act.last(), self.dve.last()]

    def ld(self, key, dst, src, *waits):
        if key not in self.s_ld:
            self.s_ld[key] = [self.sem("s_" + key), 0]
        e = self.s_ld[key]
        e[1] += 16
        return self.sp.dma(dst, src, e[0], e[1], *waits)

    def need(self, X, slots, ts):
        out = []
        for s in slots:
            for t in ts:
                while (s, t) not in X.ready:
                    assert any(self.lanes), (X.name, s, t)
                    self.pump()
                out += X.ready[(s, t)]
        return out

    def group(self, jobs):
        idx = [self.take(j["key"]) for j in jobs]
        if self.plan is None:
            return self.dry(jobs)
        for t in range(2):
            for j, job in zip(idx, jobs):
                X, slots = job["X"], job["slots"]
                wh, wl = self.weights(j)
                waits = list(self.split_tok[j]) + self.need(X, slots, [t])
                if job["first"]:
                    for b, _, _ in job["segs"]:
                        waits += self.main[t][b].free
                cols = slice(t * P, t * P + P)
                n = 0
                total = len(slots) * len(job["segs"]) * 3
                for k, slot in enumerate(slots):
                    for x, w in ((X.h, wl), (X.h, wh), (X.l, wh)):
                        for b, c0, c1 in job["segs"]:
                            n += 1
                            tok = self.pe.put(
                                lambda e, o=self.main[t][b][:, 0:c1 - c0], x=x[:, slot, cols],
                                w=w[:, k, c0:c1], st=(job["first"] and k == 0 and x is X.h and w is wl),
                                sp=(job["last"] and n > total - len(job["segs"])):
                                e.matmul(o, x, w, start=st, stop=sp),
                                *waits, inc=(n == total))
                            waits = []
                for s in slots:
                    X.used[(s, t)] = [tok]
                if t == 1:
                    self.done_tok[j] = [tok]
                if job["last"]:
                    job["epi"](t, tok)
                self.tick()

    def dry(self, jobs):
        for t in range(2):
            for job in jobs:
                for s in job["slots"]:
                    job["X"].used[(s, t)] = []
                if job["last"]:
                    job["epi"](t, (self.pe.sem, 0))
                self.pump()

    def turned_group(self, X, keys, b, epi):
        idx = [self.take(k) for k in keys]
        if self.plan is None:
            epi((self.pe.sem, 0))
            return
        banks = [self.main[0][b], self.main[1][b]]
        kk = 0
        for u, j in enumerate(idx):
            kt = keys[u][3]
            wh, wl = self.weights(j)
            slots = list(range(kk, kk + kt))
            waits = list(self.split_tok[j]) + self.need(X, slots, [0, 1])
            if u == 0:
                waits += banks[0].free + banks[1].free
            for k in range(kt):
                for f in range(4):
                    fs = slice(f * P, f * P + P)
                    o = banks[f // 2][:, (f % 2) * S:(f % 2) * S + S]
                    for n, (w, x) in enumerate(((wl, X.h), (wh, X.h), (wh, X.l))):
                        end = k == kt - 1 and f == 3 and n == 2
                        tok = self.pe.put(
                            lambda e, o=o, w=w[:, k, fs], x=x[:, kk + k, :],
                            st=(u == 0 and k == 0 and n == 0 and f % 2 == 0),
                            sp=(u == len(idx) - 1 and k == kt - 1 and n == 2):
                            e.matmul(o, w, x, start=st, stop=sp, skip_group_check=True),
                            *waits, inc=end)
                        waits = []
            for s in slots:
                X.used[(s, 0)] = X.used[(s, 1)] = [tok]
            self.done_tok[j] = [tok]
            if u < len(idx) - 1:
                self.tick()
            kk += kt
        epi(tok)
        self.tick()

    def turn(self, X, slot0, t, srcs, *waits):
        n = len(srcs)
        bank = self.side()
        w = list(waits) + bank.free
        for i, s in enumerate(srcs):
            tok = self.pe.put(lambda e, i=i, s=s: e.transpose(bank[:, i * P:i * P + P], s, self.ident[:, :]),
                              *(w if i == 0 else []), inc=(i == n - 1))
        war = [x for i in range(n) for x in X.used.get((slot0 + i, t), [])]
        hi = X.h[:, slot0:slot0 + n, t * P:t * P + P]
        lo = X.l[:, slot0:slot0 + n, t * P:t * P + P]
        src = bank[:, 0:n * P].rearrange("p (k n) -> p k n", n=P)
        a = self.act.put(lambda e: e.activation(hi, src, ACT.Copy), tok, *war)
        v = self.dve.put(lambda e: e.tensor_tensor(lo, src, hi.bitcast(F32), ALU.subtract), a)
        bank.free = [a, v]
        for i in range(n):
            X.ready[(slot0 + i, t)] = [a, v]
        return tok

    def rsqrt(self, out, x, eps, *waits):
        p = self.pool.put(lambda e: e.tensor_scalar(out, x, eps, None, ALU.add), *waits)
        half = self.nhalf[:, :].broadcast_to([P, out.shape[1]])
        return self.pool.put(lambda e: e.tensor_tensor(out, out, half, ALU.pow), p, self.memset_tok)

    def gain_load(self, vec):
        g = self.gain[self.gain_n % 2]
        self.gain_n += 1
        tok = self.ld(f"gain{(self.gain_n - 1) % 2}", g[:, :], vec.partition_broadcast(P), *g.free)
        return g, tok

    def add(self, t, tok, coef=0.5):
        for b in range(2):
            o = self.h[:, t, b * 512:b * 512 + 512]
            v = self.dve.put(lambda e, b=b, o=o: e.scalar_tensor_tensor(
                o, self.main[t][b][:, :], coef, o, ALU.mult, ALU.add), tok, *self.h_tok[t])
            self.main[t][b].free = [v]
        self.h_tok[t] = [v]

    def rms(self, t, gain, final=False):
        g, gt = gain
        ms, rs = self.st[:, 48 + 2 * t:49 + 2 * t], self.st[:, 49 + 2 * t:50 + 2 * t]
        x, h = self.xn[:, t, :], self.h[:, t, :]
        a = self.act.put(lambda e: e.activation(x, h, ACT.Square, scale=1.0 / 32, accum_out=ms),
                         *self.h_tok[t], *self.xn_free[t])
        v = self.rsqrt(rs, ms, EPS, a)
        o = h if final else x
        v = self.dve.put(lambda e: e.scalar_tensor_tensor(o, h, rs, g[:, :], ALU.mult, ALU.mult), v, gt)
        g.free = g.free + [v] if t else [v]
        self.xn_free[t] = [v]
        if final:
            self.h_tok[t] = [v]
        return o, v

    def layer_norm(self, t, gg, gb):
        bs = self.bn[:, t, 0:12]
        mv = self.bn[:, t, 12:14]
        rs = self.bn[:, t, 14:15]
        h = self.h[:, t, :]
        for i in range(2):
            v = self.dve.put(lambda e, i=i: e.bn_stats(bs[:, 6 * i:6 * i + 6], h[:, 512 * i:512 * i + 512]),
                             *self.h_tok[t])
        v = self.dve.put(lambda e: e.bn_aggr(mv, bs), v)
        v = self.rsqrt(rs, mv[:, 1:2], LN_EPS, v)
        v = self.dve.put(lambda e: e.tensor_scalar(h, h, mv[:, 0:1], rs, ALU.subtract, ALU.mult), v)
        v = self.dve.put(lambda e: e.tensor_tensor(h, h, gg[0][:, :], ALU.mult), v, gg[1])
        gg[0].free = gg[0].free + [v] if t else [v]
        v = self.dve.put(lambda e: e.tensor_tensor(h, h, gb[0][:, :], ALU.add), v, gb[1])
        gb[0].free = gb[0].free + [v] if t else [v]
        self.h_tok[t] = [v]
        return h, v

    def turn_x(self, t, x, v, wait=2, scale=False):
        def gen():
            for _ in range(wait):
                yield
            for half in range(2):
                tok = self.turn(self.X, 4 * half, t, [x[:, (4 * half + i) * P:(4 * half + i + 1) * P]
                                                      for i in range(4)], *v)
                yield
            if not scale:
                self.xn_free[t] = [tok]
            if scale:
                h = self.h[:, t, :]
                a = self.act.put(lambda e: e.activation(h, h, ACT.Copy, scale=ALPHA), tok, *self.h_tok[t])
                self.h_tok[t] = [a]
        for i in range(8):
            self.X.ready.pop((i, t), None)
        self.lanes[3 if t else 0].append(gen())

    def down(self, name, ix, k0, n_units, sizes, epi):
        u = 0
        for size in sizes:
            jobs = []
            for _ in range(size):
                jobs.append(dict(key=(name, ix, k0 + 2 * u * P, 2, 0, D), X=self.M, slots=[2 * u, 2 * u + 1],
                                 segs=[(0, 0, 512), (1, 512, 1024)], first=(u == 0), last=(u == n_units - 1),
                                 epi=epi))
                u += 1
            self.group(jobs)
        assert u == n_units

    def ffn1(self, l, pre, after):
        self.mix_to_ffn()
        gate, up, dn = pre + "_w_gate", pre + "_w_up", pre + "_w_down"
        for n0, chunks, sizes in ((0, (512, 512, 512), (2, 4)), (1536, (512, 512, 256), (1, 4))):
            self.M.ready.clear()
            slot = 0
            c0 = n0
            for n in chunks:
                jobs = []
                for b, name in ((0, gate), (1, up)):
                    parts = [(0, 4), (4, 4)] if n == 512 else [(0, 8)]
                    for i, (k, kt) in enumerate(parts):
                        jobs.append(dict(key=(name, (l,), k * P, kt, c0, n), X=self.X,
                                         slots=list(range(k, k + kt)), segs=[(b, 0, n)], first=(i == 0),
                                         last=(i == len(parts) - 1),
                                         epi=self.silu_epi(n) if b == 0 else self.up_epi(n, slot)))
                self.group(jobs)
                slot += n // P
                c0 += n
            half2 = n0 > 0
            self.down(dn, (l,), n0, sum(chunks) // 256, sizes,
                      lambda t, tok, half2=half2: (self.add(t, tok), after(t) if half2 else None))

    def silu_epi(self, n):
        def epi(t, tok):
            bank = self.main[t][0]
            a = self.act.put(lambda e: e.activation(self.sg[t][:, 0:n], bank[:, 0:n], ACT.Silu),
                             tok, *self.sg_free[t])
            bank.free = [a]
            self.sg_tok[t] = a
        return epi

    def up_epi(self, n, slot):
        def epi(t, tok):
            bank = self.main[t][1]
            v = self.dve.put(lambda e: e.tensor_tensor(self.mn[t][:, 0:n], bank[:, 0:n], self.sg[t][:, 0:n],
                                                       ALU.mult), tok, self.sg_tok[t], *self.mn_free[t])
            bank.free = [v]
            self.sg_free[t] = [v]
            self.later_turn(t, n, slot, v)
        return epi

    def later_turn(self, t, n, slot, v):
        def gen():
            yield
            tok = self.turn(self.M, slot, t, [self.mn[t][:, i * P:i * P + P] for i in range(n // P)], v)
            self.mn_free[t] = [tok]
        g = gen()
        self.lanes[1 + t].append(g)

    def ffn2(self, l, after):
        self.mix_to_ffn()
        for n0, n_chunks, sizes in ((0, 3, (2, 4)), (1536, 3, (2, 4)), (3072, 2, (4,))):
            self.M.ready.clear()
            for c in range(n_chunks):
                b = c % 2
                c0 = n0 + 512 * c
                self.group([dict(key=("w_ff1_2", (l,), 512 * i, 4, c0, 512), X=self.X,
                                 slots=list(range(4 * i, 4 * i + 4)), segs=[(b, 0, 512)], first=(i == 0),
                                 last=(i == 1), epi=self.relu_epi(b, 4 * c)) for i in range(2)])
            end = n0 == 3072
            self.down("w_ff2_2", (l,), n0, n_chunks * 2, sizes,
                      lambda t, tok, end=end: (self.add(t, tok, 1.0), after(t) if end else None))

    def relu_epi(self, b, slot):
        def epi(t, tok):
            bank = self.main[t][b]
            a = self.act.put(lambda e: e.activation(self.sg[t][:, :], bank[:, :], ACT.Relu),
                             tok, *self.sg_free[t])
            v = self.dve.put(lambda e: e.scalar_tensor_tensor(self.mn[t][:, :], bank[:, :], 0.0, self.sg[t][:, :],
                                                              ALU.max, ALU.mult), a, *self.mn_free[t])
            bank.free = [v]
            self.sg_free[t] = [v]
            self.later_turn(t, 512, slot, v)
        return epi

    def mix_to_ffn(self):
        f = self.fence()
        self.sg_free, self.sg_tok = [list(f), list(f)], {}
        self.mn_free = [list(f), list(f)]
        for s in range(12):
            for t in range(2):
                self.M.used[(s, t)] = list(f)

    def start(self):
        A = self.A
        for j in range(NRAW):
            self.fetch(j)
        x = A["x"]
        self.xn_free = [[], []]
        self.X = Turned("X", self.xh, self.xl)
        self.M = Turned("M", self.mh, self.ml)
        self.lane_free = [[], [], []]
        self.h_tok = [[self.ld(f"x{t}", self.h[:, t, :], x[0, t * P:t * P + P, :])] for t in range(2)]
        k = [self.ld("const", d, s) for d, s in (
            (self.ident[:, :], A["c_ident"]), (self.mask[:, :], A["c_mask"]), (self.freq[:, :], A["c_freq"]),
            (self.pos_i[:, :], A["pos_row"].partition_broadcast(P)), (self.pos_c[:, :], A["pos_col"]),
            (self.lams[:, :], A["lams"].partition_broadcast(P)), (self.scan[:, :], A["c_scan"]))][-1]
        V, C = self.dve.put, self.act.put
        m = self.pool.put(lambda e: e.memset(self.ones[:, :], 1.0 / P))
        m = self.pool.put(lambda e: e.memset(self.half_pi[:, :], math.pi / 2))
        m = self.pool.put(lambda e: e.memset(self.one[:, :], 1.0))
        m = self.pool.put(lambda e: e.memset(self.nhalf[:, :], -0.5))
        m = self.pool.put(lambda e: e.memset(self.kr[:, :, 0:64], 0.0))
        self.memset_tok = m
        ident_ready = k
        self.const_tok = k
        g = self.gain_load(A["ffn1_norm"][0])
        for t in range(2):
            x_, v = self.rms(t, g)
            self.turn_x(t, x_, [v, k], 0)
        self.drain()
        a = V(lambda e: e.tensor_copy(self.pos_f[:, :], self.pos_c[:, :]), k)
        b = V(lambda e: e.tensor_copy(self.pos_r[:, :], self.pos_i[:, :]), k)
        d0, d1 = self.dist[:, 0:128], self.dist[:, 128:384]
        a = V(lambda e: e.tensor_scalar(d0, self.pos_r[:, 0:128], self.pos_f[:, 0:1], None,
                                        ALU.subtract), a, b)
        a = V(lambda e: e.tensor_scalar(d1, self.pos_r[:, :], self.pos_f[:, 1:2], None,
                                        ALU.subtract), a)
        a = C(lambda e: e.activation(self.dist[:, :], self.dist[:, :], ACT.Abs), a)
        a = V(lambda e: e.scalar_tensor_tensor(self.dist[:, :], self.mask[:, :], -1e4, self.dist[:, :],
                                               ALU.mult, ALU.add), a)
        for i in range(4):
            a = V(lambda e, i=i: e.tensor_scalar(self.ang[:, 16 * i:16 * i + 16], self.freq[:, 16 * i:16 * i + 16],
                                                 self.pos_f[:, i:i + 1], None, ALU.mult), a)
        a = V(lambda e: e.tensor_scalar(self.angk[:, :], self.ang[:, :], 1 / (2 * math.pi), MAGIC, ALU.mult,
                                        ALU.add), a)
        a = V(lambda e: e.tensor_scalar(self.angk[:, :], self.angk[:, :], MAGIC, None, ALU.subtract), a)
        for c in TWO_PI:
            a = V(lambda e, c=c: e.scalar_tensor_tensor(self.ang[:, :], self.angk[:, :], -c, self.ang[:, :],
                                                        ALU.mult, ALU.add), a)
        lim = 3.1415925
        a = V(lambda e: e.tensor_scalar(self.ang[:, :], self.ang[:, :], lim, -lim, ALU.min, ALU.max), a)
        b = C(lambda e: e.activation(self.angk[:, :], self.ang[:, :], ACT.Abs), a)
        cs = self.cs[:, :, :, :, :].rearrange("p a b t k -> p a (b t k)")
        c1 = C(lambda e: e.activation(cs[:, 0, :], self.angk[:, :], ACT.Sin, bias=self.half_pi[:, :], scale=-1.0),
               b, self.memset_tok)
        c2 = C(lambda e: e.activation(cs[:, 1, :], self.ang[:, :], ACT.Sin), a)
        self.rope_tok = c2
        for l in range(L):
            o = 128 * l
            for i in range(2):
                q, kk = self.lams[:, o + 64 * i:o + 64 * i + 32], self.lams[:, o + 64 * i + 32:o + 64 * i + 64]
                v = V(lambda e, q=q, kk=kk: e.tensor_tensor(self.lamt[:, :], q, kk, ALU.mult), *([v] if l or i else [k]))
                v = V(lambda e, c=2 * l + i: e.tensor_reduce(self.epsc[:, c:c + 1], self.lamt[:, :], AXX, ALU.add), v)
        a = C(lambda e: e.activation(self.epsc[:, 4:8], self.epsc[:, 0:4], ACT.Exp), v)
        for l in range(L):
            li = 0.8 - 0.6 * math.exp(-0.3 * l)
            c = 4 + 2 * l
            v = V(lambda e, l=l, c=c: e.tensor_tensor(self.lam[:, l:l + 1], self.epsc[:, c + 1:c + 2],
                                                      self.epsc[:, c:c + 1], ALU.subtract), a)
            v = V(lambda e, l=l, li=li: e.tensor_scalar(self.lam[:, l:l + 1], self.lam[:, l:l + 1], -li, None,
                                                        ALU.add), v)
        self.lam_tok = v
        self.lane_free = [self.fence() for _ in range(3)]

    def rope(self, kind, x, heads, w, o, tmp, *waits):
        V = self.dve.put
        x1, x2 = x[:, :, :, o:o + 16], x[:, :, :, o + 16:o + 32]
        cos = self.cs[:, 0, kind, :, :].unsqueeze(2).broadcast_to([P, 2, heads, 16])
        sin = self.cs[:, 1, kind, :, :].unsqueeze(2).broadcast_to([P, 2, heads, 16])
        n = 2 * heads * 16
        t = [tmp[:, i * n:(i + 1) * n].rearrange("p (a b c) -> p a b c", a=2, b=heads) for i in range(2)]
        v = V(lambda e: e.tensor_tensor(t[0], x1, sin, ALU.mult), self.rope_tok, *waits)
        v = V(lambda e: e.tensor_tensor(t[1], x2, sin, ALU.mult), v)
        v = V(lambda e: e.tensor_tensor(x1, x1, cos, ALU.mult), v)
        v = V(lambda e: e.tensor_tensor(x2, x2, cos, ALU.mult), v)
        v = V(lambda e: e.tensor_tensor(x1, x1, t[1], ALU.subtract), v)
        v = V(lambda e: e.tensor_tensor(x2, x2, t[0], ALU.add), v)
        return v

    def scores(self, q, k, *waits):
        bank = self.side()
        self.pe.put(lambda e: e.matmul(bank[:, 0:128], q[0], k(128), start=True, stop=True), *waits, *bank.free,
                    inc=False)
        return bank, self.pe.put(lambda e: e.matmul(bank[:, 128:384], q[1], k(256), start=True, stop=True))

    def exps(self, Sb, st, c, scale, v):
        parts = (Sb[:, 0:128], Sb[:, 128:384])
        for i, p in enumerate(parts):
            r = self.dve.put(lambda e, i=i, p=p: e.tensor_reduce(st[:, c + i:c + i + 1], p, AXX, ALU.max), v)
        r = self.dve.put(lambda e: e.tensor_scalar(st[:, c:c + 2], st[:, c:c + 2], -scale, None, ALU.mult), r)
        for i, p in enumerate(parts):
            a = self.act.put(lambda e, i=i, p=p: e.activation(p, p, ACT.Exp, bias=st[:, c + i:c + i + 1], scale=scale,
                                                              accum_out=st[:, c + 4 + i:c + 5 + i]), r)
        return a

    def turn_probs(self, Sb, PT, v, *war):
        bank = self.side()
        for i in range(3):
            tok = self.pe.put(lambda e, i=i: e.transpose(bank[:, i * P:i * P + P], Sb[:, i * P:i * P + P],
                                                         self.ident[:, :]),
                              *([v] + bank.free if i == 0 else []), inc=(i == 2))
        a = self.act.put(lambda e: e.activation(PT[:, 0:384], bank[:, 0:384], ACT.Copy), tok, *war)
        bank.free = [a]
        return a

    def weigh(self, PT, v, n, outs, r, rt, a):
        bank = self.side()
        tok = self.pe.put(lambda e: e.matmul(bank[:, 0:n], PT[:, 0:128], v[0], start=True, stop=True), a, *bank.free)
        self.pe.put(lambda e: e.matmul(bank[:, n:2 * n], PT[:, 128:256], v[0], start=True, stop=False), inc=False)
        tok = self.pe.put(lambda e: e.matmul(bank[:, n:2 * n], PT[:, 256:384], v[1], start=False, stop=True))
        for t in range(2):
            d = self.dve.put(lambda e, t=t: e.tensor_scalar(outs[t], bank[:, t * n:t * n + n], r[:, t:t + 1], None,
                                                            ALU.mult), tok, rt)
        bank.free = [d]
        return d

    def diff_head(self, i, l, h):
        st = self.st[:, 16 * i:16 * i + 16]
        S0, S1 = self.lS[i]
        scale = 32 ** -0.5
        slope = 2.0 ** -(h + 1)
        f, o = h // 2, 64 * (h % 2)
        V = self.dve.put
        for m, Sb in enumerate((S0, S1)):
            p = o + 32 * m
            bank, tok = self.scores(
                [self.dqT[p:p + 32, f, t * P:t * P + P] for t in range(2)],
                lambda n, p=p: self.dkT[p:p + 32, f, 0:n], *self.dqk_tok)
            v = V(lambda e, Sb=Sb, bank=bank: e.scalar_tensor_tensor(
                Sb[:, :], self.dist[:, :], -slope / scale, bank[:, 0:384], ALU.mult, ALU.add),
                tok, *self.lane_free[i])
            bank.free = [v]
            a = self.exps(Sb, st, 2 * m, scale, v)
        v = V(lambda e: e.reciprocal(st[:, 8:12], st[:, 4:8]), a)
        v = V(lambda e: e.scalar_tensor_tensor(st[:, 12:14], st[:, 4:6], self.lam[:, l:l + 1], st[:, 10:12],
                                               ALU.mult, ALU.mult), v, self.lam_tok)
        for t, (c0, c1) in enumerate(((0, 128), (128, 384))):
            w = V(lambda e, t=t, c0=c0, c1=c1: e.scalar_tensor_tensor(
                S0[:, c0:c1], S1[:, c0:c1], st[:, 12 + t:13 + t], S0[:, c0:c1], ALU.mult, ALU.add), v)
        yield
        yield
        a = self.turn_probs(S0, S1, w)
        yield
        hs = slice(64 * h, 64 * h + 64)
        v = self.weigh(S1, [self.dv[:, t, hs] for t in range(2)], 64, [self.pin[:, t, hs] for t in range(2)],
                       st[:, 8:10], w, a)
        self.lane_free[i] = [v]
        self.diff_done.append(v)

    def plain_head(self, i, scale, turn_q, k, v, n, outs, done, turned=None, h=0):
        st = self.st[:, 16 * i:16 * i + 16]
        Sb, PT = self.lS[i]
        Q = self.lQ[i]
        bank = self.side()
        for j, x in enumerate(turn_q):
            w = x.shape[1]
            tok = self.pe.put(lambda e, j=j, x=x, w=w: e.transpose(bank[0:w, j * P:j * P + P], x, self.ident[:, :]),
                              *(self.qk_tok + bank.free if j == 0 else []), inc=(j == len(turn_q) - 1))
        if turned is not None:
            turned[h] = tok
        c = len(turn_q) * P
        a = self.act.put(lambda e: e.activation(Q[0:w, 0:c], bank[0:w, 0:c], ACT.Copy), tok, *self.lane_free[i])
        bank.free = [a]
        yield
        bank, tok = self.scores([Q[0:w, 0:P], Q[0:w, P:2 * P]], k, a, *self.qk_tok)
        d = self.dve.put(lambda e: e.tensor_tensor(Sb[:, :], bank[:, 0:384], self.mask[:, :], ALU.add), tok,
                         *self.lane_free[i])
        bank.free = [d]
        a = self.exps(Sb, st, 0, scale, d)
        r = self.dve.put(lambda e: e.reciprocal(st[:, 8:10], st[:, 4:6]), a)
        yield
        yield
        b = self.turn_probs(Sb, PT, a, tok)
        yield
        while turned is not None and len([x for x in turned if x < h]) < h:
            yield
        d = self.weigh(PT, v, n, outs, st[:, 8:10], r, b)
        self.lane_free[i] = [d]
        done.append(d)

    def gates(self, name, l, c0, slot):
        for j in range(2):
            def epi(t, tok, j=j):
                bank = self.main[t][j]
                a = self.act.put(lambda e: e.activation(self.G[slot][:, t, 512 * j:512 * j + 512], bank[:, :],
                                                        ACT.Tanh, scale=0.5), tok, *self.g_free[slot])
                bank.free = [a]
                self.g_tok[slot, t, j] = a
            self.group([dict(key=(name, (l,), 512 * i, 4, c0 + 512 * j, 512), X=self.X,
                             slots=list(range(4 * i, 4 * i + 4)), segs=[(j, 0, 512)], first=(i == 0), last=(i == 1),
                             epi=epi) for i in range(2)])

    def branch(self, name, l, n, Y, slots, slot, first, last, stay=None):
        self.g_free[slot] = []

        def epi(j):
            def f(t, tok):
                bank = self.main[t][j]
                G = self.G[slot][:, t, 512 * j:512 * j + 512]
                m = self.xn[:, t, 512 * j:512 * j + 512]
                o = m if first else G
                v = self.dve.put(lambda e: e.scalar_tensor_tensor(o, G, 1.0, bank[:, :], ALU.add, ALU.mult),
                                 tok, self.g_tok[slot, t, j], *(self.m_free if first else []))
                bank.free = [v]
                if not first:
                    v = self.dve.put(lambda e: e.tensor_tensor(m, m, G, ALU.add), v, *self.m_tok[t, j])
                self.m_tok[t, j] = [v]
                self.g_free[slot].append(v)
                if last:
                    def gen():
                        yield
                        tok = self.turn(self.M, 4 * j, t, [m[:, i * P:i * P + P] for i in range(4)], v)
                        self.xn_free[t] = [tok]
                    self.lanes[3 if t else 0].append(gen())
            return f
        self.group([dict(key=(name, (l, n), 0, 4, 512 * j, 512), X=Y, slots=slots, segs=[(j, 0, 512)], first=True,
                         last=True, epi=epi(j)) for j in range(2)])

    def way_out(self, name, l, after):
        self.group([dict(key=(name, (l,), 512 * i, 4, 512 * b, 512), X=self.M, slots=list(range(4 * i, 4 * i + 4)),
                         segs=[(b, 0, 512)], first=(i == 0), last=(i == 1),
                         epi=(lambda t, tok: (self.add(t, tok), after(t))) if (i, b) == (1, 1) else
                         (lambda t, tok: None)) for i in range(2) for b in range(2)])

    def merged_ready(self):
        f = self.fence()
        self.M.ready.clear()
        for s in range(8):
            for t in range(2):
                self.M.used[(s, t)] = list(f)

    def copy_epi(self, dst, b, n=512, toks=None, func=ACT.Copy):
        def epi(t, tok):
            bank = self.main[t][b]
            a = self.act.put(lambda e: e.activation(dst(t), bank[:, 0:n], func), tok, *self.r_free)
            bank.free = [a]
            toks.append(a)
        return epi

    def cols(self, name, l, c0, b, epi, n=512):
        return [dict(key=(name, (l,), 512 * i, 4, c0, n), X=self.X, slots=list(range(4 * i, 4 * i + 4)),
                     segs=[(b, 0, n)], first=(i == 0), last=(i == 1), epi=epi) for i in range(2)]

    def mixer1(self, l, after):
        A, V, C, T = self.A, self.dve.put, self.act.put, self.pe.put
        f = self.fence()
        self.r_free = f
        self.g_free, self.g_tok, self.m_tok = [list(f), list(f)], {}, {}
        self.lane_free = [list(f) for _ in range(3)]
        self.diff_done, self.mla_done = [], []
        W = "w_in"
        k_gq = self.ld("gq", self.gq[:, :], A["gq"][l].partition_broadcast(P), *f)
        k_sub = self.ld("sub", self.sub[:, :], A["diff_subln"][l].partition_broadcast(P), *f)
        k_pc = [self.ld("pc", self.pc[:, :], A["c_pool"], *f)]
        k_pw = [self.ld("pw", self.pw[:, :, :], A["pool_w"][l].rearrange("g c d -> c g d"), *f),
                self.ld("pbs", self.pbs[:, :], A["pbs"][l], *f)]
        C1 = Turned("C", self.ch, self.cl)
        xf = self.xn_free
        for s in range(3):
            for t in range(2):
                C1.used[(s, t)] = list(f)
        kr_toks, pin_toks, dv_toks = [], [], []

        def c_epi(t, tok):
            bank = self.main[t][0]
            ms = self.bn[:, t, 0:2]
            rs = self.bn[:, t, 2:4]
            tmp = self.lQ[t]
            a = C(lambda e: e.activation(tmp[:, 0:256], bank[:, 0:256], ACT.Square, scale=1 / 16,
                                         accum_out=ms[:, 0:1]), tok, *self.lane_free[t])
            a = C(lambda e: e.activation(tmp[:, 256:384], bank[:, 256:384], ACT.Square, scale=128 ** -0.5,
                                         accum_out=ms[:, 1:2]))
            b = C(lambda e: e.activation(self.kr[:, t, 64:96], bank[:, 384:416], ACT.Copy), *self.r_free)
            v = self.rsqrt(rs, ms, EPS, a)
            kr_toks.append(b)

            def gen():
                while (7, 1) not in self.X.ready or (7, 0) not in self.X.ready or (t and len(self.c_done) < 1):
                    yield
                xn_free = self.xn_free[0] + self.xn_free[1]
                for s in range(3):
                    C1.used[(s, t)] = f + xn_free
                for i, (c0, c1) in enumerate(((0, 256), (256, 384))):
                    d = V(lambda e, i=i, c0=c0, c1=c1: e.scalar_tensor_tensor(
                        self.cn[:, c0:c1], bank[:, c0:c1], rs[:, i:i + 1], self.gq[:, c0:c1], ALU.mult, ALU.mult),
                        v, k_gq, *self.cn_free, *xn_free)
                bank.free = [d, b]
                yield
                tok = self.turn(C1, 0, t, [self.cn[:, i * P:i * P + P] for i in range(3)], d)
                self.cn_free = [tok]
                self.c_done.append(t)
            self.lanes[2].append(gen())
            self.lane_free[t] = [a]

        self.c_done = []
        self.cn_free = list(f)
        j_c = self.cols(W, l, 0, 0, c_epi, 416)
        j_v = self.cols(W, l, 1440, 1, self.copy_epi(lambda t: self.dv[:, t, :], 1, 512, dv_toks))
        self.group(j_c + j_v)
        while len(self.c_done) < 2:
            self.pump()

        def qk_epi(dst, b, toks):
            def epi(tok):
                for i in range(2):
                    bank = self.main[i][b]
                    o = dst[:, 2 * i:2 * i + 2, :].rearrange("p a s -> p (a s)")
                    a = C(lambda e, o=o, bank=bank: e.activation(o, bank[:, :], ACT.Copy), tok, *f)
                    bank.free = [a]
                    toks.append(a)
            return epi
        qk = []
        self.turned_group(self.X, [(W, (l,), 512 * i, 4, 416, 512) for i in range(2)], 0, qk_epi(self.dqT, 0, qk))
        self.turned_group(self.X, [(W, (l,), 512 * i, 4, 928, 512) for i in range(2)], 1, qk_epi(self.dkT, 1, qk))
        self.dqk_tok = [qk[-1]]
        self.group(self.cols(W, l, 1952, 0, self.copy_epi(lambda t: self.pin[:, t, :], 0, 512, pin_toks)))

        Yp = Turned("Yp", self.yph, self.ypl)
        pool_done = []

        def pool():
            yield
            for i in range(2):
                bank = self.side()
                for g in (2 * i, 2 * i + 1):
                    o = (g % 2) * S
                    gs = slice(g * P, g * P + P)
                    T(lambda e, g=g, o=o, gs=gs, bank=bank: e.matmul(
                        bank[:, o:o + 256], self.pin[:, 0, gs], self.pc[:, 256 * g:256 * g + 256],
                        start=True, stop=False, skip_group_check=True), *pin_toks, *k_pc,
                        *(bank.free if g % 2 == 0 else []), inc=False)
                    tok = T(lambda e, g=g, o=o, gs=gs, bank=bank: e.matmul(
                        bank[:, o + 128:o + 256], self.pin[:, 1, gs], self.pc[:, 1024 + P * g:1024 + P * g + P],
                        start=False, stop=True, skip_group_check=True))
                a = C(lambda e, i=i, bank=bank: e.activation(
                    self.pT[:, 2 * i:2 * i + 2, :].rearrange("p a s -> p (a s)"), bank[:, :], ACT.Copy), tok, *f)
                bank.free = [a]
                self.pin_free = [tok]
                yield
            for i in range(2):
                bank = self.side()
                for g in (2 * i, 2 * i + 1):
                    o = (g % 2) * S
                    tok = T(lambda e, g=g, o=o, bank=bank: e.matmul(
                        bank[:, o:o + 256], self.pw[:, g, :], self.pT[:, g, :], start=True, stop=True), a, *k_pw,
                        *(bank.free if g % 2 == 0 else []))
                for g in (2 * i, 2 * i + 1):
                    o = (g % 2) * S
                    v = V(lambda e, g=g, o=o, bank=bank: e.tensor_scalar(
                        self.pT[:, g, :], bank[:, o:o + 256], self.pbs[:, g:g + 1], self.pbs[:, 4 + g:5 + g],
                        ALU.add, ALU.mult), tok)
                bank.free = [v]
                yield
            pT = self.pT[:, :, :].rearrange("p a s -> p (a s)")
            a = C(lambda e: e.activation(self.yph[:, :, :].rearrange("p a s -> p (a s)"), pT, ACT.Copy), v, *f)
            v = V(lambda e: e.tensor_tensor(self.ypl[:, :, :].rearrange("p a s -> p (a s)"), pT,
                                            self.yph[:, :, :].rearrange("p a s -> p (a s)").bitcast(F32),
                                            ALU.subtract), a, *f)
            for s in range(4):
                for t in range(2):
                    Yp.ready[(s, t)] = [a, v]
            pool_done.append(v)
            self.g_free[1] = [v]
            self.kt_free = [tok]

        self.lanes[3].append(pool())

        def diff_lane(i):
            while not pool_done:
                yield
            for h in range(i, 8, 3):
                yield from self.diff_head(i, l, h)
        for i in range(3):
            self.lanes[i].append(diff_lane(i))
        self.gates(W, l, 2464 + 2048, 0)
        while not pool_done:
            self.pump()

        q_toks = []

        def q_epi(t, tok):
            for b in range(2):
                bank = self.main[t][b]
                a = C(lambda e, b=b, bank=bank: e.activation(
                    self.q[:, t, 4 * b:4 * b + 4, :], bank[:, 0:384].rearrange("p (h n) -> p h n", n=96), ACT.Copy),
                    tok, *f)
                bank.free = [a]
            q_toks.append(a)
        self.group([dict(key=("mla_w_uq", (l,), 0, 2, 0, 768), X=C1, slots=[0, 1],
                         segs=[(0, 0, 384), (1, 384, 768)], first=True, last=True, epi=q_epi)])
        self.latent_kv(l, C1, kr_toks, q_toks, f)
        self.m_free = self.fence()
        self.branch("w_branch", l, 2, Yp, [0, 1, 2, 3], 0, True, False)

        X = self.X

        yo = self.q[:, :, :, :].rearrange("p t h n -> p t (h n)")
        turned = {}

        def mla_lane(i):
            for h in range(i, 8, 3):
                hs = slice(64 * h, 64 * h + 64)
                yield from self.plain_head(
                    i, 96 ** -0.5, [self.q[:, t, h, :] for t in range(2)],
                    lambda n, h=h: self.kT[0:96, h, 0:n], [self.v[:, t, hs] for t in range(2)], 64,
                    [yo[:, t, hs] for t in range(2)], self.mla_done, turned, h)

        def diff_end():
            while len(self.diff_done) < 8 or not self.gates_done:
                yield
            li = 0.8 - 0.6 * math.exp(-0.3 * l)
            for t in range(2):
                y = self.pin[:, t, :].rearrange("p (h n) -> p h n", n=64)
                sq = self.sq[:, t, :].rearrange("p (h n) -> p h n", n=64)
                v = V(lambda e: e.tensor_tensor(sq, y, y, ALU.mult), *self.diff_done, *self.tmp_free)
                v = V(lambda e: e.tensor_reduce(self.bn[:, t, 0:8], sq, AXX, ALU.add), v)
                v = V(lambda e: e.tensor_scalar(self.bn[:, t, 0:8], self.bn[:, t, 0:8], 1 / 64, None, ALU.mult), v)
                v = self.rsqrt(self.bn[:, t, 0:8], self.bn[:, t, 0:8], EPS, v)
                v = V(lambda e: e.tensor_scalar(self.bn[:, t, 0:8], self.bn[:, t, 0:8], 1 - li, None, ALU.mult), v)
                v = V(lambda e: e.tensor_tensor(y, y, self.bn[:, t, 0:8].unsqueeze(2).broadcast_to([P, 8, 64]),
                                                ALU.mult), v)
                v = V(lambda e: e.tensor_tensor(y, y, self.sub[:, :].unsqueeze(1).broadcast_to([P, 8, 64]),
                                                ALU.mult), v, k_sub)
                self.turn(X, 4, t, [self.pin[:, t, i * P:i * P + P] for i in range(4)], v)
                yield

        def mla_end():
            while len(self.mla_done) < 8 or not self.gates_done:
                yield
            for t in range(2):
                self.turn(X, 0, t, [yo[:, t, P * i:P * i + P] for i in range(4)], *self.mla_done)
                yield
        self.gates_done = False
        for i in range(3):
            self.lanes[i].append(mla_lane(i))
        self.gates(W, l, 2464 + 1024, 1)
        self.gates(W, l, 2464, 0)
        self.gates_done = True
        X.ready.clear()
        while len(self.diff_done) < 8:
            self.pump()
        self.lanes[3].append(diff_end())
        self.lanes[3].append(mla_end())
        self.tmp_free = self.fence()
        self.branch("w_branch", l, 1, X, [4, 5, 6, 7], 1, False, False)
        while len(self.mla_done) < 8:
            self.pump()
        self.merged_ready()
        self.branch("w_branch", l, 0, X, [0, 1, 2, 3], 0, False, True)
        self.way_out("w_out", l, after)

    def latent_kv(self, l, C1, kr_toks, q_toks, f):
        V, C, T = self.dve.put, self.act.put, self.pe.put
        j = self.take(("mla_w_ukv", (l,), 0, 1, 0, 1024))
        tmp = self.cn
        dry = self.plan is None
        if not dry:
            wh, wl = self.weights(j)
            waits = list(self.split_tok[j]) + self.need(C1, [2], [0, 1])
        banks = [self.main[0][0], self.main[0][1], self.main[1][0], self.main[1][1]]
        sides = [self.side(), self.side()]
        toks = []
        if not dry:
            for t in range(2):
                bank = sides[t]
                for n, (x, w) in enumerate(((C1.h, wl), (C1.h, wh), (C1.l, wh))):
                    tok = T(lambda e, bank=bank, x=x[:, 2, t * P:t * P + P],
                            w=w[:, 0, :].rearrange("p (h n) -> p h n", n=128)[:, :, 64:128], n=n:
                            e.matmul(bank[:, :], x, w, start=(n == 0), stop=(n == 2)),
                            *(waits + bank.free if n == 0 else []), inc=(n == 2))
                toks.append(tok)
            for i, bank in enumerate(banks):
                for h in (2 * i, 2 * i + 1):
                    for n, (w, x) in enumerate(((wl, C1.h), (wh, C1.h), (wh, C1.l))):
                        tok = T(lambda e, bank=bank, h=h, w=w[:, 0, h * P:h * P + P], x=x[:, 2, :], n=n: e.matmul(
                            bank[:, (h % 2) * S:(h % 2) * S + S], w, x, start=(n == 0), stop=(n == 2),
                            skip_group_check=True),
                            *(bank.free if n == 0 and h % 2 == 0 else []), inc=(n == 2))
                toks.append(tok)
            self.done_tok[j] = [tok]
        else:
            toks = [(self.pe.sem, 0)] * 6
        for t in range(2):
            a = C(lambda e, t=t: e.activation(self.v[:, t, :], sides[t][:, :], ACT.Copy), toks[t], *f)
            sides[t].free = [a]
        for i, bank in enumerate(banks):
            k = V(lambda e, i=i, bank=bank: e.tensor_copy(
                self.kT[0:64, 2 * i:2 * i + 2, :], bank[0:64, :].rearrange("p (a s) -> p a s", s=S)), toks[2 + i],
                *self.kt_free)
            bank.free = [k]
        c1_used = [(self.pe.sem, self.pe.count)]
        v = self.rope(0, self.kr[:, :, :].unsqueeze(2), 1, 96, 64, tmp, *kr_toks, *self.cn_free)
        bank = self.side()
        for t in range(2):
            tok = T(lambda e, t=t, bank=bank: e.transpose(bank[0:96, t * P:t * P + P], self.kr[:, t, :],
                                                          self.ident[:, :]),
                    *([v, self.memset_tok] + bank.free if t == 0 else []), inc=(t == 1))
        kr = bank[64:96, 0:256].unsqueeze(1).broadcast_to([32, 4, S])
        a = C(lambda e: e.activation(self.kT[64:96, 0:4, :], kr, ACT.Copy), tok, *self.kt_free)
        b = C(lambda e: e.activation(self.kT[64:96, 4:8, :], kr, ACT.Copy))
        bank.free = [b]
        v = self.rope(0, self.q, 8, 96, 64, self.rope_tmp, *q_toks, v, *c1_used)
        self.qk_tok = [v, b, a, k]
        self.advance()
        self.pump()

    def mixer2(self, l, after):
        A, V, C, T = self.A, self.dve.put, self.act.put, self.pe.put
        f = self.fence()
        self.r_free = f
        self.g_free, self.g_tok, self.m_tok = [list(f), list(f)], {}, {}
        self.lane_free = [list(f) for _ in range(3)]
        self.gates_done = False
        W, X = "w_in_2", self.X
        k_lng = self.ld("lng", self.lng[:, :, :], A["lng"][l].partition_broadcast(P), *f)
        k_ws = self.ld("ws", self.ws[:, :, :], A["gmlp_w_s_2"][l].rearrange("g t s -> t g s"), *f)
        k_tril = self.ld("tril", self.tril[:, :], A["c_tril"][:, 0:P], *f)
        k_gp = self.ld("gp", self.gp[:, :], A["gp"][l], *f)
        k_wgu = self.ld("wgu", self.wgu[0:16, :], A["w_gate_up_2"][l], *f)

        Yg = Turned("Yg", self.yph, self.ypl)
        for s in range(4):
            for t in range(2):
                Yg.used[(s, t)] = list(f)
        gm_done = []
        zv_tok, zu_toks = {}, {}

        def wst():
            bank = self.side()
            for g in range(4):
                tok = T(lambda e: e.transpose(bank[:, g * P:g * P + P], self.ws[:, g, :], self.ident[:, :]),
                        *([k_ws] + bank.free if g == 0 else []), inc=(g == 3))
            v = V(lambda e: e.tensor_tensor(self.wsT[:, :, :], bank[:, :].rearrange("p (g t) -> p g t", g=4),
                                            self.tril[:, :].unsqueeze(1).broadcast_to([P, 4, P]), ALU.mult),
                  tok, k_tril, *f)
            bank.free = [v]
            self.ws_tok = v
        wst()

        def gelu_epi(b, dst, toks):
            def epi(t, tok):
                bank = self.main[t][b]
                a = C(lambda e: e.activation(dst[:, t, :], bank[:, :], ACT.Gelu), tok, *f, *self.xn_free[0],
                      *self.xn_free[1])
                bank.free = [a]
                toks[t] = a
                if b == 1:
                    self.lanes[2].append(gmlp(t))
            return epi

        def gmlp(t):
            bn = self.bn[:, t, :]
            z = self.zv[:, t, :]
            v = V(lambda e: e.bn_stats(bn[:, 0:6], z), zv_tok[t], *self.h_tok[t])
            v = V(lambda e: e.bn_aggr(bn[:, 12:14], bn[:, 0:6]), v)
            v = self.rsqrt(bn[:, 14:15], bn[:, 13:14], LN_EPS, v)
            v = V(lambda e: e.tensor_scalar(z, z, bn[:, 12:13], bn[:, 14:15], ALU.subtract, ALU.mult), v)
            v = V(lambda e: e.tensor_tensor(z, z, self.lng[:, 0, :], ALU.mult), v, k_lng)
            v = V(lambda e: e.tensor_tensor(z, z, self.lng[:, 1, :], ALU.add), v)
            yield
            bank = self.side()
            for g in range(4):
                tok = T(lambda e: e.matmul(bank[:, g * P:g * P + P], self.wsT[:, g, :],
                                           self.zv[:, t, g * P:g * P + P], start=True, stop=True),
                        *([v, self.ws_tok] + bank.free if g == 0 else []), inc=(g == 3))
            for g in range(4):
                u = self.zu[:, t, g * P:g * P + P]
                v = V(lambda e: e.scalar_tensor_tensor(u, bank[:, g * P:g * P + P], self.gp[:, 5 + g:6 + g], u,
                                                       ALU.add, ALU.mult), tok, zu_toks[t], k_gp)
            bank.free = [v]
            yield
            tok = self.turn(Yg, 0, t, [self.zu[:, t, g * P:g * P + P] for g in range(4)], v)
            gm_done.append(tok)

        self.group(self.cols(W, l, 2576, 0, gelu_epi(0, self.zv, zv_tok)) +
                   self.cols(W, l, 2064, 1, gelu_epi(1, self.zu, zu_toks)))
        mv_t, mq_t, mk_t, gv_t, gq_t, gk_t, gg_t, lr_t = ([] for _ in range(8))
        flat = lambda x, t: x[:, t, :, :].rearrange("p h n -> p (h n)")
        self.group(self.cols(W, l, 4112, 0, self.copy_epi(lambda t: self.mv[:, t, :], 0, 512, mv_t)) +
                   self.cols(W, l, 3088, 1, self.copy_epi(lambda t: flat(self.mq, t), 1, 512, mq_t)))
        self.group(self.cols(W, l, 3600, 0, self.copy_epi(lambda t: flat(self.mk, t), 0, 512, mk_t)))
        while len(gm_done) < 2:
            self.pump()
        v = self.rope(1, self.mq, 4, 128, 0, self.lG[0][:, :, :].rearrange("p a b -> p (a b)"), *mq_t,
                      *self.lane_free[0])
        v = self.rope(1, self.mk, 4, 128, 0, self.lG[0][:, :, :].rearrange("p a b -> p (a b)"), *mk_t, v)
        self.lane_free[0] = [v]
        self.qk_tok = [v]
        moba_done, gla_done = [], []

        def moba_lane(i, heads):
            for h in heads:
                yield from self.plain_head(
                    i, 128 ** -0.5, [x[:, t, h, :] for x in (self.mq, self.mk) for t in range(2)],
                    lambda n, i=i: self.lQ[i][:, 256:256 + n], [self.mv[:, t, h * P:h * P + P] for t in range(2)],
                    128, [self.mq[:, t, h, :] for t in range(2)], moba_done)
        for i, heads in enumerate(((0, 3), (1,), (2,))):
            self.lanes[i].append(moba_lane(i, heads))

        def t_epi(dst, b, toks, silu=False):
            def epi(tok):
                for i in range(2):
                    bank = self.main[i][b]
                    o = dst[:, 2 * i:2 * i + 2, :].rearrange("p a s -> p (a s)")
                    if silu:
                        a = C(lambda e: e.activation(o, bank[:, :], ACT.Tanh, scale=0.5), tok, *f)
                        a = V(lambda e: e.scalar_tensor_tensor(o, o, 1.0, bank[:, :], ALU.add, ALU.mult), a)
                    else:
                        a = C(lambda e: e.activation(o, bank[:, :], ACT.Copy), tok, *f)
                    bank.free = [a]
                    toks.append(a)
            return epi
        wide = lambda c0: [(W, (l,), 512 * i, 4, c0, 512) for i in range(2)]

        def lr_epi(t, tok):
            bank = self.main[t][1]
            a = C(lambda e: e.activation(self.lr[:, t, :], bank[:, 0:16], ACT.Copy), tok, *f)
            bank.free = [a]
            lr_t.append(a)
        self.group([dict(key=(W, (l,), 0, 8, 2048, 16), X=X, slots=list(range(8)), segs=[(1, 0, 16)], first=True,
                         last=True, epi=lr_epi)])
        wt = self.ws_tok

        def decay():
            bank = self.side()
            for t in range(2):
                tok = T(lambda e: e.transpose(bank[0:16, t * P:t * P + P], self.lr[:, t, :], self.ident[:, :]),
                        *(lr_t + bank.free if t == 0 else []), inc=(t == 1))
            a = C(lambda e: e.activation(self.lrT[0:16, :], bank[0:16, 0:256], ACT.Copy), tok, *gm_done)
            bank.free = [a]
            yield
            for i in range(2):
                bank = self.side()
                for h in (2 * i, 2 * i + 1):
                    tok = T(lambda e: e.matmul(bank[:, (h % 2) * S:(h % 2) * S + S], self.wgu[0:16, h * P:h * P + P],
                                               self.lrT[0:16, :], start=True, stop=True), a, k_wgu,
                            *(bank.free if h % 2 == 0 else []))
                for h in (2 * i, 2 * i + 1):
                    s = bank[:, (h % 2) * S:(h % 2) * S + S]
                    b = C(lambda e: e.activation(self.bigE[:, h, :], s, ACT.Abs, bias=self.gp[:, h:h + 1]), tok,
                          k_gp, wt, *gm_done)
                for h in (2 * i, 2 * i + 1):
                    s = bank[:, (h % 2) * S:(h % 2) * S + S]
                    v = V(lambda e: e.tensor_scalar(self.bigL[:, h, :], s, self.gp[:, h:h + 1], 0.0, ALU.add,
                                                    ALU.min), b)
                bank.free = [v, b]
            a = C(lambda e: e.activation(self.bigE[:, :, :], self.bigE[:, :, :], ACT.Exp, scale=-1.0), v)
            a = C(lambda e: e.activation(self.bigE[:, :, :], self.bigE[:, :, :], ACT.Ln, bias=self.one[:, :]), a,
                  self.memset_tok)
            v = V(lambda e: e.tensor_tensor(self.bigL[:, :, :], self.bigL[:, :, :], self.bigE[:, :, :],
                                            ALU.subtract), a)
            self.decay_tok = [v]
        self.decay_tok = []
        self.lanes[3].append(decay())
        self.turned_group(X, wide(0), 0, t_epi(self.gqT, 0, gq_t))
        self.turned_group(X, wide(512), 1, t_epi(self.gkT, 1, gk_t))
        self.group(self.cols(W, l, 1024, 0, self.copy_epi(lambda t: self.gv[:, t, :], 0, 512, gv_t)))
        self.turned_group(X, wide(1536), 1, t_epi(self.ggT, 1, gg_t, True))
        while not self.decay_tok:
            self.pump()

        def gla_lane(i, heads):
            for h in heads:
                yield from self.gla_head(i, h, gq_t + gk_t, gv_t, gg_t, gla_done)
        for i, heads in enumerate(((0, 3), (1,), (2,))):
            self.lanes[i].append(gla_lane(i, heads))

        def moba_end():
            while len(moba_done) < 4 or not self.gates_done:
                yield
            for t in range(2):
                self.turn(X, 0, t, [self.mq[:, t, h, :] for h in range(4)], *moba_done)
                yield

        def gla_end():
            while len(gla_done) < 4 or not self.gates_done:
                yield
            hi, lo = X.h[:, 4:8, :], X.l[:, 4:8, :]
            war = [x for s in range(4, 8) for t in range(2) for x in X.used[(s, t)]]
            a = C(lambda e: e.activation(hi, self.ggT[:, :, :], ACT.Copy), *gla_done, *war)
            v = V(lambda e: e.tensor_tensor(lo, self.ggT[:, :, :], hi.bitcast(F32), ALU.subtract), a)
            for s in range(4, 8):
                for t in range(2):
                    X.ready[(s, t)] = [a, v]
        G0 = 4624
        self.gates(W, l, G0 + 1024, 0)
        self.gates(W, l, G0 + 2048, 1)
        self.m_free = self.fence()
        self.branch("w_branch_2", l, 1, Yg, [0, 1, 2, 3], 0, True, False)
        self.gates(W, l, G0, 0)
        self.gates_done = True
        X.ready.clear()
        while len(moba_done) < 4:
            self.pump()
        self.lanes[3].append(moba_end())
        self.lanes[3].append(gla_end())
        self.branch("w_branch_2", l, 2, X, [0, 1, 2, 3], 1, False, False)
        while len(gla_done) < 4 or (7, 1) not in X.ready:
            self.pump()
        self.merged_ready()
        self.branch("w_branch_2", l, 0, X, [4, 5, 6, 7], 0, False, True)
        self.way_out("w_out_2", l, after)

    def gla_head(self, i, h, qk_t, gv_t, gg_t, done):
        V, C, T = self.dve.put, self.act.put, self.pe.put
        G = self.lG[i]
        flat = G[:, :, :].rearrange("p a b -> p (a b)")
        eb, kd, enb = flat[:, 0:256], flat[:, 256:512], flat[:, 512:768]
        kdn, at = G[:, 2:4, :], G[:, 4:6, :]
        S1, S2, S3 = self.bigL[:, h, 0:128], self.bigL[:, h, 128:256], G[:, 6, :]
        st = self.st[:, 16 * i:16 * i + 4]
        bc, E = self.bigL[:, h, :], self.bigE[:, h, :]
        gq, gk, gg = self.gqT[:, h, :], self.gkT[:, h, :], self.ggT[:, h, :]
        gv = [self.gv[:, t, h * P:h * P + P] for t in range(2)]
        free = self.lane_free[i]
        v = V(lambda e: e.tensor_tensor_scan(E, self.scan[:, :], bc, 0.0, ALU.mult, ALU.add), *self.decay_tok)
        w = V(lambda e: e.tensor_scalar(st, E[:, 63:256:64], 1 / 16, None, ALU.mult), v, *free)
        a = C(lambda e: e.activation(eb, E, ACT.Exp, scale=1 / 16), v, *free)
        a = C(lambda e: e.activation(enb, E, ACT.Exp, scale=-1 / 16))
        for c in range(3):
            b = C(lambda e: e.activation(kd[:, 64 * c:64 * c + 64], E[:, 64 * c:64 * c + 64], ACT.Exp,
                                         bias=st[:, c:c + 1], scale=-1 / 16), w)
        kdv = V(lambda e: e.tensor_tensor(kd[:, 0:192], kd[:, 0:192], gk[:, 0:192], ALU.mult), b, *qk_t)
        qd = V(lambda e: e.scalar_tensor_tensor(gq, gq, 128 ** -0.5, eb, ALU.mult, ALU.mult), a)
        ki = V(lambda e: e.tensor_tensor(gk, gk, enb, ALU.mult), a, kdv)
        z = V(lambda e: e.memset(at, 0.0), ki)
        yield
        yield
        bank = self.side()
        T(lambda e: e.transpose(bank[:, 0:128], kd[:, 0:128], self.ident[:, :]), kdv, *bank.free, inc=False)
        t1 = T(lambda e: e.transpose(bank[0:64, 128:256], kd[:, 128:192], self.ident[:, :]))
        bank2 = self.side()
        for t in range(2):
            ts = slice(t * P, t * P + P)
            t2 = T(lambda e: e.matmul(bank2[:, ts], gk[:, ts], gq[:, ts], start=True, stop=True), qd, ki,
                   *bank2.free)
        a = C(lambda e: e.activation(kdn[:, 0, :], bank[:, 0:128], ACT.Copy), t1)
        a = C(lambda e: e.activation(kdn[0:64, 1, :], bank[0:64, 128:256], ACT.Copy), t1)
        bank.free = [a]
        for t in range(2):
            m = V(lambda e: e.copy_predicated(at[:, t, :], self.chunk[:, :], bank2[:, t * P:t * P + P]), t2, z,
                  self.chunk_tok)
        bank2.free = [m]
        yield
        yield
        bank, bank2 = self.side(), self.side()
        T(lambda e: e.matmul(bank[:, 0:128], kdn[0:64, 0, :], gv[0][0:64, :], start=True, stop=True), a, *gv_t,
          *bank.free, inc=False)
        t1 = T(lambda e: e.matmul(bank[:, 128:256], kdn[0:64, 1, :], gv[1][0:64, :], start=True, stop=True))
        t2 = T(lambda e: e.matmul(bank2[:, 0:128], kdn[64:128, 0, :], gv[0][64:128, :], start=True, stop=True),
               *bank2.free)
        v = V(lambda e: e.tensor_copy(S1, bank[:, 0:128]), t1, v)
        v = V(lambda e: e.scalar_tensor_tensor(S2, S1, eb[:, 127:128], bank2[:, 0:128], ALU.mult, ALU.add), v, t2)
        bank2.free = [v]
        v = V(lambda e: e.scalar_tensor_tensor(S3, S2, eb[:, 191:192], bank[:, 128:256], ALU.mult, ALU.add), v)
        bank.free = [v]
        yield
        bank = self.side()
        w = [v, m] + bank.free
        for t in range(2):
            T(lambda e: e.matmul(bank[:, t * P:t * P + P], gv[t], at[:, t, :], start=(t == 0), stop=False,
                                 skip_group_check=True), *w, inc=False)
        for c, s in ((1, S1), (2, S2), (3, S3)):
            tok = T(lambda e: e.matmul(bank[:, 64 * c:64 * c + 64], s, gq[:, 64 * c:64 * c + 64], start=False,
                                       stop=True, skip_group_check=True))
        a = C(lambda e: e.activation(E, bank[:, 0:256], ACT.Square), tok)
        o = kd
        b = C(lambda e: e.activation(o, bank[:, 0:256], ACT.Copy), tok)
        bank.free = [b]
        yield
        bank = self.side()
        w = [a, self.memset_tok] + bank.free
        for t in range(2):
            tok = T(lambda e: e.matmul(bank[:, t:t + 1], E[:, t * P:t * P + P], self.ones[:, 0:1], start=True,
                                       stop=True), *w, inc=(t == 1))
        v = V(lambda e: e.tensor_scalar(st[:, 0:2], bank[:, 0:2], EPS, None, ALU.add), tok)
        bank.free = [v]
        half = self.nhalf[:, :].broadcast_to([P, 2])
        p = self.pool.put(lambda e: e.tensor_tensor(st[:, 0:2], st[:, 0:2], half, ALU.pow), v)
        yield
        bank = self.side()
        w = [p] + bank.free
        for t in range(2):
            tok = T(lambda e: e.matmul(bank[:, t * P:t * P + P], st[:, t:t + 1].broadcast_to([P, P]),
                                       self.ident[:, :], start=True, stop=True), *w, inc=(t == 1))
        v = V(lambda e: e.scalar_tensor_tensor(o, o, self.gp[:, 4:5], bank[:, 0:256], ALU.mult, ALU.mult), b, tok)
        bank.free = [v]
        v = V(lambda e: e.scalar_tensor_tensor(gg, o, 0.5, gg, ALU.mult, ALU.mult), v, *gg_t)
        self.lane_free[i] = [v]
        done.append(v)

    def run(self):
        A = self.A
        self.start()
        for l in range(L):
            g = self.gain_load(A["mix_norm"][l])
            self.ffn1(l, "ffn1", self.to_rms(g))
            g2 = lambda l=l: self.gain_load(A["ffn2_norm"][l])
            self.mixer1(l, self.lazy_rms(g2))
            if l + 1 < L:
                self.ffn1(l, "ffn2", self.lazy_rms(lambda l=l: self.gain_load(A["ffn1_norm"][l + 1])))
            else:
                self.ffn1(l, "ffn2", self.lazy_rms(lambda: self.gain_load(A["final_norm"]), True))
        self.chunk_load()
        for l in range(L):
            self.mixer2(l, self.lazy_ln(A["ln1_g_2"][l], A["ln1_b_2"][l]))
            last = l == L - 1
            self.ffn2(l, self.lazy_ln(A["ln2_g_2"][l], A["ln2_b_2"][l], last))

    def chunk_load(self):
        self.chunk_tok = self.ld("chunk", self.chunk[:, :], self.A["c_chunk"])

    def to_rms(self, g, final=False):
        def after(t):
            x, v = self.rms(t, g, final)
            self.turn_x(t, x, [v], scale=final)
        return after

    def lazy_rms(self, load, final=False):
        g = []

        def after(t):
            if not g:
                g.append(load())
            x, v = self.rms(t, g[0], final)
            self.turn_x(t, x, [v], scale=final)
        return after

    def lazy_ln(self, gvec, bvec, last=False):
        g = []

        def after(t):
            if not g:
                g.extend([self.gain_load(gvec), self.gain_load(bvec)])
            h, v = self.layer_norm(t, *g)
            if last:
                self.sp.dma(self.out[0, t * P:t * P + P, :], h, self.s_out, 0, v)
            else:
                self.turn_x(t, h, [v], scale=True)
        return after


_INS = ["x", "ffn1_norm", "ffn1_w_gate", "ffn1_w_up", "ffn1_w_down", "mix_norm", "w_in", "mla_w_uq", "mla_w_ukv",
        "diff_subln", "pool_w", "w_branch", "w_out", "ffn2_norm", "ffn2_w_gate", "ffn2_w_up", "ffn2_w_down",
        "final_norm", "w_in_2", "w_gate_up_2", "gmlp_w_s_2", "w_branch_2", "w_out_2", "ln1_g_2", "ln1_b_2",
        "w_ff1_2", "w_ff2_2", "ln2_g_2", "ln2_b_2"]


def layouts(inp):
    a = {k: np.ascontiguousarray(inp[k]) for k in _INS}
    g = {k: np.asarray(v) for k, v in inp.items()}
    a["gq"] = np.concatenate([g["mla_q_norm"], g["mla_kv_norm"]], 1)
    a["pbs"] = np.concatenate([g["pool_b"].transpose(0, 2, 1),
                               g["pool_scale"].reshape(L, 4, P).transpose(0, 2, 1)], 2)
    a["lams"] = np.stack([g["diff_lambda_q1"], g["diff_lambda_k1"], g["diff_lambda_q2"], g["diff_lambda_k2"]],
                         1).reshape(L * 128)
    a["lng"] = np.stack([g["gmlp_ln_g_2"], g["gmlp_ln_b_2"]], 1)
    a["gp"] = np.concatenate([g["b_gate_2"].reshape(L, 4, P).transpose(0, 2, 1), g["gla_norm_w_2"][:, :, None],
                              g["gmlp_b_s_2"].transpose(0, 2, 1)], 2)
    p1, p2 = g["positions"][0], g["positions_2"][0]
    a["pos_row"] = p1
    a["pos_col"] = np.stack([p1[0:P], p1[P:], p2[0:P], p2[P:]], 1)
    a.update(constants())
    a["c_chunk"] = a["c_tril"][:, P:].astype(np.uint32)
    a["c_tril"] = a["c_tril"][:, :P]
    return {k: np.ascontiguousarray(v) for k, v in a.items()}


def build(nc, A, out):
    with ExitStack() as ctx:
        net = Net(nc, A, out, ctx)
        net.reset(None)
        net.run()
        plan = net.units
        net.reset(plan)
        net.run()
        assert net.units == plan and net.n_split == len(plan)
        block = ctx.enter_context(nc.Block())

        @block.sync
        def _(eng):
            net.sp.issue(eng)
            eng.wait_ge(net.s_out, 32)

        @block.gpsimd
        def _(eng):
            net.pool.issue(eng)

        @block.scalar
        def _(eng):
            net.act.issue(eng)

        @block.vector
        def _(eng):
            net.dve.issue(eng)

        @block.tensor
        def _(eng):
            net.pe.issue(eng)
    return net


def kernel(**inputs):
    import concourse.bacc as _bacc
    from concourse.bass_utils import run_bass_kernel_spmd as _run

    nc = _bacc.Bacc("TRN2", target_bir_lowering=False, num_devices=1)
    arrays, args = {}, {}
    for name, a in layouts(inputs).items():
        arrays[f"in_{name}_dram"] = a
        args[name] = nc.dram_tensor(f"in_{name}_dram", a.shape, mybir.dt.from_np(a.dtype), kind="ExternalInput").ap()
    out = nc.dram_tensor("out_0_dram", (1, S, D), F32, kind="ExternalOutput").ap()
    build(nc, args, out)
    r = _run(nc, [arrays], core_ids=[0])
    return r.results[0]["out_0_dram"]
```

```python
import math
from collections import deque
from contextlib import ExitStack

import numpy as np
import concourse.bass as bass
from concourse import mybir

F32 = mybir.dt.float32
F32R = mybir.dt.float32r
I32 = mybir.dt.int32
U32 = mybir.dt.uint32
ALU = mybir.AluOpType
ACT = mybir.ActivationFunctionType
AXX = mybir.AxisListType.X

P = 128
D = 1024
S = 256
L = 2
FF1 = 2816
FF2 = 4096
IN1 = 5536
IN2 = 7696
EPS = 1e-6
LN_EPS = 1e-5
ALPHA = (2 * L) ** 0.25
BIG = 1e30
TWO_PI = (6.28125, 0.0019350051879882812, 3.0199158306745e-07)
MAGIC = 12582912.0

NRAW, NW = 3, 4
UCOLS = 2048
STAGGER = 2


class Ops:

    def activation(self, *a, **k):
        return lambda e: e.activation(*a, **k)

    def matmul(self, *a, **k):
        return lambda e: e.matmul(*a, **k)

    def transpose(self, *a, **k):
        return lambda e: e.transpose(*a, **k)

    def memset(self, *a, **k):
        return lambda e: e.memset(*a, **k)

    def tensor_copy(self, *a, **k):
        return lambda e: e.tensor_copy(*a, **k)

    def tensor_tensor(self, *a, **k):
        return lambda e: e.tensor_tensor(*a, **k)

    def tensor_scalar(self, *a, **k):
        return lambda e: e.tensor_scalar(*a, **k)

    def scalar_tensor_tensor(self, *a, **k):
        return lambda e: e.scalar_tensor_tensor(*a, **k)

    def tensor_tensor_scan(self, *a, **k):
        return lambda e: e.tensor_tensor_scan(*a, **k)

    def tensor_reduce(self, *a, **k):
        return lambda e: e.tensor_reduce(*a, **k)

    def reciprocal(self, *a, **k):
        return lambda e: e.reciprocal(*a, **k)

    def copy_predicated(self, *a, **k):
        return lambda e: e.copy_predicated(*a, **k)

    def bn_stats(self, *a, **k):
        return lambda e: e.bn_stats(*a, **k)

    def bn_aggr(self, *a, **k):
        return lambda e: e.bn_aggr(*a, **k)

    def dma_start(self, *a, **k):
        return lambda e: e.dma_start(*a, **k)


OPS = Ops()


class Queue:

    def __init__(self, sem):
        self.sem, self.count, self.items = sem, 0, []

    def put(self, fn, *waits, inc=True):
        self.count += inc
        self.items.append((waits, fn(OPS), self.sem if inc else None, 1))
        return (self.sem, self.count)

    def dma(self, out, in_, sem, value, *waits):
        self.items.append((waits, OPS.dma_start(out, in_), sem, 16))
        return (sem, value)

    def last(self):
        return (self.sem, self.count)

    def issue(self, eng):
        seen = {}
        for waits, ins, sem, by in self.items:
            for s, v in waits:
                if v > seen.get(s.name, 0):
                    eng.wait_ge(s, v)
                    seen[s.name] = v
            r = ins(eng)
            if sem is not None:
                r.then_inc(sem, by)


class Buf:

    def __init__(self, ap):
        self.ap, self.free = ap, []

    def __getitem__(self, k):
        return self.ap[k]


def constants():
    ident = np.eye(P, dtype=np.float32)
    q = np.arange(P)
    mask = np.zeros((P, 384), np.float32)
    mask[:, 0:128] = np.where(np.arange(128)[None] <= q[:, None], 0.0, -BIG)
    mask[:, 128:384] = np.where(np.arange(256)[None] <= q[:, None] + 128, 0.0, -BIG)
    half = np.arange(16, dtype=np.float64)
    f1 = (10000.0 ** (-half / 16)).astype(np.float32)
    f2 = (1.0 / (500000.0 ** (half * (2.0 / 32)))).astype(np.float32)
    freq = np.broadcast_to(np.stack([f1, f1, f2, f2]).reshape(1, 64), (P, 64))
    pool = np.zeros((256, 4, 256), np.float64)
    for g, w in enumerate((2, 4, 8, 16)):
        for t in range(256):
            lo = max(0, t - w + 1)
            pool[lo:t + 1, g, t] += 1.0 / (t + 1 - lo)
            pool[t, g, t] -= 1.0
    pool = pool.astype(np.float32)
    p0 = pool[0:128].reshape(P, 1024)
    p1 = pool[128:256, :, 128:256].reshape(P, 512)
    s = q[:, None]
    t = q[None, :]
    tril = (s <= t).astype(np.float32)
    chunk = ((s <= t) & (s // 64 == t // 64)).astype(np.float32)
    scan = np.broadcast_to((np.arange(S) % 64 != 0).astype(np.float32), (P, S))
    return {
        "c_ident": ident, "c_mask": mask, "c_freq": np.ascontiguousarray(freq),
        "c_pool": np.ascontiguousarray(np.concatenate([p0, p1], 1)),
        "c_tril": np.concatenate([tril, chunk], 1),
        "c_scan": np.ascontiguousarray(scan),
    }


class Turned:

    def __init__(self, name, h, l):
        self.name, self.h, self.l, self.ready, self.used = name, h, l, {}, {}


class Net:
    def __init__(self, nc, A, out, ctx):
        self.nc, self.A, self.out, self.ctx = nc, A, out, ctx
        self.s_eng = [self.sem(n) for n in ("s_pe", "s_act", "s_dve", "s_pool", "s_sp")]
        self.s_raw = [self.sem(f"s_raw{i}") for i in range(NRAW)]
        self.s_out = self.sem("s_out")
        self.s_ld = {}
        self.memory()

    def reset(self, plan):
        self.plan = plan
        self.units = []
        self.pe, self.act, self.dve, self.pool, self.sp = (Queue(s) for s in self.s_eng)
        for e in self.s_ld.values():
            e[1] = 0
        for b in self.pb + self.gain:
            b.free = []
        self.gain_n = self.n_side = self.n_split = 0
        self.split_tok, self.raw_free, self.done_tok = {}, {}, {}
        self.lanes = [deque() for _ in range(4)]

    def sem(self, name):
        return self.ctx.enter_context(self.nc.semaphore(name))

    def at(self, name, off, shape, dt=F32):
        n = 1
        for x in shape[1:]:
            n *= x
        assert off + 4 * n <= self.top, name
        return self.nc.alloc_sbuf_tensor_at(name, shape, dt, offset=off)

    def memory(self):
        nc = self.nc
        base = (nc.sbuf_base + 63) // 64 * 64
        self.top = nc.sbuf_usable_end
        off = [base]

        def take(nbytes):
            o = off[0]
            off[0] += (nbytes + 31) // 32 * 32
            assert off[0] <= self.top, (off[0], self.top)
            return o

        A = self.at
        self.h = A("h", take(8192), [P, 2, D])
        o_xn = take(8192)
        self.xn = A("xn", o_xn, [P, 2, D])
        self.xh = A("xh", take(8192), [P, 8, S], F32R)
        self.xl = A("xl", take(8192), [P, 8, S], F32R)
        o_m = take(24576)
        self.mh = A("mh", o_m, [P, 12, S], F32R)
        self.ml = A("ml", o_m + 12288, [P, 12, S], F32R)
        self.raw = [A(f"raw{i}", take(8192), [P, UCOLS]) for i in range(NRAW)]
        self.wh = [A(f"wh{i}", take(8192), [P, UCOLS], F32R) for i in range(NW)]
        self.wl = [A(f"wl{i}", take(8192), [P, UCOLS], F32R) for i in range(NW)]
        self.gain = [Buf(A(f"gain{i}", take(4096), [P, D])) for i in range(2)]
        self.ident = A("ident", take(512), [P, P])
        self.ones = A("ones", take(512), [P, P])
        self.mask = A("mask", take(1536), [P, 384])
        o_dist = take(1536)
        self.dist = A("dist", o_dist, [P, 384])
        self.cs = A("cs", take(512), [P, 2, 2, 2, 16])
        self.half_pi = A("half_pi", take(4), [P, 1])
        self.one = A("one", take(4), [P, 1])
        self.nhalf = A("nhalf", take(4), [P, 1])
        self.lam = A("lam", take(8), [P, 2])
        self.bn = A("bn", take(128), [P, 2, 16])
        self.epsc = A("epsc", take(32), [P, 8])
        self.st = A("st", take(256), [P, 64])
        self.ssq = A("ssq", take(64), [P, 2, 8])
        o_ck = take(512)
        o_r = take(0)
        r = [o_r]

        def rt(nbytes):
            o = r[0]
            r[0] += (nbytes + 31) // 32 * 32
            assert r[0] <= self.top, (r[0] - self.top)
            return o

        self.sg = [A(f"sg{t}", rt(2048), [P, 512]) for t in range(2)]
        self.mn = [A(f"mn{t}", rt(2048), [P, 512]) for t in range(2)]
        r[0] = o_r
        o_g = [rt(8192), rt(8192)]
        self.G = [A(f"G{i}", o_g[i], [P, 2, D]) for i in range(2)]
        o_lane = [rt(3584) for _ in range(3)]
        self.lS = [[A(f"lS{i}{j}", o_lane[i] + 1536 * j, [P, 384]) for j in range(2)] for i in range(3)]
        self.lQ = [A(f"lQ{i}", o_lane[i] + 1536, [P, 512]) for i in range(3)]
        self.lG = [A(f"lG{i}", o_lane[i], [P, 7, P]) for i in range(3)]
        self.pos_i = A("pos_i", o_lane[1], [P, S], I32)
        self.pos_c = A("pos_c", o_lane[1] + 1024, [P, 4], I32)
        self.pos_f = A("pos_f", o_lane[1] + 1088, [P, 4])
        self.pos_r = A("pos_r", o_lane[1] + 1536, [P, S])
        self.lams = A("lams", o_lane[0], [P, 2 * 128])
        self.lamt = A("lamt", o_lane[0] + 1024, [P, 32])
        self.ang = A("ang", o_lane[2], [P, 64])
        self.angk = A("angk", o_lane[2] + 256, [P, 64])
        self.freq = A("freq", o_lane[2] + 512, [P, 64])
        self.tril = A("tril", o_g[1] + 4096, [P, P])
        self.lane_free = [[] for _ in range(3)]
        self.scan = A("scan", rt(1024), [P, S])
        o_r2 = r[0]
        self.dqT = A("dqT", o_m, [P, 4, S])
        self.dkT = A("dkT", o_m + 4096, [P, 4, S])
        self.dv = A("dv", o_m + 8192, [P, 2, 512])
        self.v = A("v", o_m + 12288, [P, 2, 512])
        self.yph = A("yph", o_m + 16384, [P, 4, S], F32R)
        self.ypl = A("ypl", o_m + 20480, [P, 4, S], F32R)
        self.pin = A("pin", rt(4096), [P, 2, 512])
        o_q = rt(6144)
        self.q = A("q", o_q, [P, 2, 8, 96])
        self.cn = A("cn", o_q, [P, 2, 384])
        o_kt = rt(8192)
        self.kT = A("kT", o_kt, [P, 8, S])
        self.pc = A("pc", o_kt, [P, 1536])
        self.pw = A("pw", o_kt + 6144, [P, 4, P])
        self.rope_tmp = A("rope_tmp", o_xn, [P, 512])
        self.ch = A("ch", o_xn, [P, 3, S], F32R)
        self.cl = A("cl", o_xn + 3072, [P, 3, S], F32R)
        self.pT = A("pT", o_g[1], [P, 4, S])
        self.gq = A("gq", rt(1536), [P, 384])
        self.sub = A("sub", rt(256), [P, 64])
        self.kr = A("kr", rt(768), [P, 2, 96])
        self.pbs = A("pbs", rt(32), [P, 8])
        r[0] = o_r2
        self.gqT = A("gqT", o_m, [P, 4, S])
        self.gkT = A("gkT", o_m + 4096, [P, 4, S])
        self.ggT = A("ggT", o_m + 8192, [P, 4, S])
        self.gv = A("gv", o_m + 12288, [P, 2, 512])
        o_bl, o_be = rt(4096), rt(4096)
        self.bigL = A("bigL", o_bl, [P, 4, S])
        self.bigE = A("bigE", o_be, [P, 4, S])
        self.lng = A("lng", o_bl, [P, 2, 512])
        self.ws = A("ws", o_be, [P, 4, P])
        self.wsT = A("wsT", o_be + 2048, [P, 4, P])
        self.zu = A("zu", o_xn, [P, 2, 512])
        self.zv = A("zv", o_xn + 4096, [P, 2, 512])
        self.mq = A("mq", rt(4096), [P, 2, 4, P])
        self.mk = A("mk", rt(4096), [P, 2, 4, P])
        self.mv = A("mv", rt(4096), [P, 2, 512])
        self.wgu = A("wgu", rt(2048), [P, 512])
        self.gp = A("gp", rt(64), [P, 9])
        self.chunk = A("chunk", o_ck, [P, P], U32)
        self.lrT = A("lrT", o_dist, [P, S])
        self.pb = [Buf(self.ctx.enter_context(nc.psum_tensor(f"pb{i}", [P, 512], F32))) for i in range(8)]
        self.main = [[self.pb[0], self.pb[1]], [self.pb[2], self.pb[3]]]

    def fetch(self, j):
        if self.plan is None or j >= len(self.plan):
            return
        name, ix, k0, kt, n0, n = self.plan[j]
        src = self.A[name]
        for i in ix:
            src = src[i]
        src = src[k0:k0 + P * kt, n0:n0 + n].rearrange("(k p) n -> p k n", p=P)
        dst = self.raw[j % NRAW][:, 0:kt * n].rearrange("p (k n) -> p k n", n=n)
        self.sp.dma(dst, src, self.s_raw[j % NRAW], None, *self.raw_free.get(j - NRAW, []))

    def split(self, j):
        name, ix, k0, kt, n0, n = self.plan[j]
        c = kt * n
        raw = self.raw[j % NRAW][:, 0:c]
        hi, lo = self.wh[j % NW], self.wl[j % NW]
        landed = (self.s_raw[j % NRAW], 16 * (j // NRAW + 1))
        free = self.done_tok.get(j - NW, [])
        a = self.act.put(lambda e: e.activation(hi[:, 0:c], raw, ACT.Copy), landed, *free)
        v = self.dve.put(lambda e: e.tensor_tensor(lo[:, 0:c], raw, hi[:, 0:c].bitcast(F32), ALU.subtract),
                         a, *free)
        self.split_tok[j] = [a, v]
        self.raw_free[j] = [a, v]
        self.fetch(j + NRAW)

    def advance(self):
        if self.plan is None:
            return
        while self.n_split < len(self.plan) and (self.n_split < NW or self.n_split - NW in self.done_tok):
            self.split(self.n_split)
            self.n_split += 1

    def take(self, key):
        self.units.append(key)
        return len(self.units) - 1

    def weights(self, j):
        _, _, _, kt, _, n = self.plan[j]
        hi, lo = self.wh[j % NW], self.wl[j % NW]
        self.advance()
        assert j < self.n_split
        return tuple(w[:, 0:kt * n].rearrange("p (k n) -> p k n", n=n) for w in (hi, lo))

    def pump(self):
        for lane in self.lanes:
            if lane:
                try:
                    next(lane[0])
                except StopIteration:
                    lane.popleft()

    def drain(self, n=None):
        lanes = self.lanes if n is None else [self.lanes[n]]
        while any(lanes):
            for lane in lanes:
                if lane:
                    try:
                        next(lane[0])
                    except StopIteration:
                        lane.popleft()

    def tick(self):
        self.advance()
        self.pump()

    def side(self):
        self.n_side += 1
        return self.pb[4 + self.n_side % 4]

    def fence(self):
        return [self.pe.last(), self.act.last(), self.dve.last()]

    def ld(self, key, dst, src, *waits, queue=None):
        if key not in self.s_ld:
            self.s_ld[key] = [self.sem("s_" + key), 0]
        e = self.s_ld[key]
        e[1] += 16
        return (queue or self.pool).dma(dst, src, e[0], e[1], *waits)

    def need(self, X, slots, ts):
        out = []
        for s in slots:
            for t in ts:
                while (s, t) not in X.ready:
                    assert any(self.lanes), (X.name, s, t)
                    self.pump()
                out += X.ready[(s, t)]
        return out

    def group(self, jobs):
        idx = [self.take(j["key"]) for j in jobs]
        if self.plan is None:
            return self.dry(jobs)
        for t in range(2):
            for j, job in zip(idx, jobs):
                X, slots = job["X"], job["slots"]
                wh, wl = self.weights(j)
                waits = list(self.split_tok[j]) + self.need(X, slots, [t])
                if job["first"]:
                    for b, _, _ in job["segs"]:
                        waits += self.main[t][b].free
                cols = slice(t * P, t * P + P)
                n = 0
                total = len(slots) * len(job["segs"]) * 3
                for k, slot in enumerate(slots):
                    for x, w in ((X.h, wl), (X.h, wh), (X.l, wh)):
                        for b, c0, c1 in job["segs"]:
                            n += 1
                            tok = self.pe.put(
                                lambda e, o=self.main[t][b][:, 0:c1 - c0], x=x[:, slot, cols],
                                w=w[:, k, c0:c1], st=(job["first"] and k == 0 and x is X.h and w is wl),
                                sp=(job["last"] and n > total - len(job["segs"])):
                                e.matmul(o, x, w, start=st, stop=sp),
                                *waits, inc=(n == total))
                            waits = []
                for s in slots:
                    X.used[(s, t)] = [tok]
                if t == 1:
                    self.done_tok[j] = [tok]
                if job["last"]:
                    job["epi"](t, tok)
                self.tick()

    def dry(self, jobs):
        for t in range(2):
            for job in jobs:
                for s in job["slots"]:
                    job["X"].used[(s, t)] = []
                if job["last"]:
                    job["epi"](t, (self.pe.sem, 0))
                self.pump()

    def turned_group(self, X, keys, b, epi):
        idx = [self.take(k) for k in keys]
        if self.plan is None:
            epi((self.pe.sem, 0))
            return
        banks = [self.main[0][b], self.main[1][b]]
        kk = 0
        for u, j in enumerate(idx):
            kt = keys[u][3]
            wh, wl = self.weights(j)
            slots = list(range(kk, kk + kt))
            waits = list(self.split_tok[j]) + self.need(X, slots, [0, 1])
            if u == 0:
                waits += banks[0].free + banks[1].free
            for k in range(kt):
                if k == 2:
                    self.tick()
                for f in range(4):
                    fs = slice(f * P, f * P + P)
                    o = banks[f // 2][:, (f % 2) * S:(f % 2) * S + S]
                    for n, (w, x) in enumerate(((wl, X.h), (wh, X.h), (wh, X.l))):
                        end = k == kt - 1 and f == 3 and n == 2
                        tok = self.pe.put(
                            lambda e, o=o, w=w[:, k, fs], x=x[:, kk + k, :],
                            st=(u == 0 and k == 0 and n == 0 and f % 2 == 0),
                            sp=(u == len(idx) - 1 and k == kt - 1 and n == 2):
                            e.matmul(o, w, x, start=st, stop=sp, skip_group_check=True),
                            *waits, inc=end)
                        waits = []
            for s in slots:
                X.used[(s, 0)] = X.used[(s, 1)] = [tok]
            self.done_tok[j] = [tok]
            if u < len(idx) - 1:
                self.tick()
            kk += kt
        epi(tok)
        self.tick()

    def turn(self, X, slot0, t, srcs, *waits):
        n = len(srcs)
        bank = self.side()
        w = list(waits) + bank.free
        for i, s in enumerate(srcs):
            tok = self.pe.put(lambda e, i=i, s=s: e.transpose(bank[:, i * P:i * P + P], s, self.ident[:, :]),
                              *(w if i == 0 else []), inc=(i == n - 1))
        war = [x for i in range(n) for x in X.used.get((slot0 + i, t), [])]
        hi = X.h[:, slot0:slot0 + n, t * P:t * P + P]
        lo = X.l[:, slot0:slot0 + n, t * P:t * P + P]
        src = bank[:, 0:n * P].rearrange("p (k n) -> p k n", n=P)
        a = self.act.put(lambda e: e.activation(hi, src, ACT.Copy), tok, *war)
        v = self.dve.put(lambda e: e.tensor_tensor(lo, src, hi.bitcast(F32), ALU.subtract), a)
        bank.free = [a, v]
        for i in range(n):
            X.ready[(slot0 + i, t)] = [a, v]
        return tok

    def rsqrt(self, out, x, eps, *waits):
        p = self.pool.put(lambda e: e.tensor_scalar(out, x, eps, None, ALU.add), *waits)
        half = self.nhalf[:, :].broadcast_to([P, out.shape[1]])
        return self.pool.put(lambda e: e.tensor_tensor(out, out, half, ALU.pow), p, self.memset_tok)

    def gain_load(self, vec):
        g = self.gain[self.gain_n % 2]
        self.gain_n += 1
        tok = self.ld(f"gain{(self.gain_n - 1) % 2}", g[:, :], vec.partition_broadcast(P), *g.free)
        return g, tok

    def add(self, t, tok, coef=0.5):
        for b in range(2):
            o = self.h[:, t, b * 512:b * 512 + 512]
            v = self.dve.put(lambda e, b=b, o=o: e.scalar_tensor_tensor(
                o, self.main[t][b][:, :], coef, o, ALU.mult, ALU.add), tok, *self.h_tok[t])
            self.main[t][b].free = [v]
        self.h_tok[t] = [v]

    def rms(self, t, gain, final=False):
        g, gt = gain
        ms, rs = self.st[:, 48 + 2 * t:49 + 2 * t], self.st[:, 49 + 2 * t:50 + 2 * t]
        x, h = self.xn[:, t, :], self.h[:, t, :]
        a = self.act.put(lambda e: e.activation(x, h, ACT.Square, scale=1.0 / 32, accum_out=ms),
                         *self.h_tok[t], *self.xn_free[t])
        v = self.rsqrt(rs, ms, EPS, a)
        o = h if final else x
        halves = []
        for i in range(2):
            c = slice(512 * i, 512 * i + 512)
            halves.append(self.dve.put(lambda e: e.scalar_tensor_tensor(o[:, c], h[:, c], rs, g[:, c], ALU.mult,
                                                                        ALU.mult), v, gt))
        v = halves[1]
        g.free = g.free + [v] if t else [v]
        self.xn_free[t] = [v]
        if final:
            self.h_tok[t] = [v]
        return o, halves

    def layer_norm(self, t, gg, gb):
        bs = self.bn[:, t, 0:12]
        mv = self.bn[:, t, 12:14]
        rs = self.bn[:, t, 14:15]
        h = self.h[:, t, :]
        for i in range(2):
            v = self.dve.put(lambda e, i=i: e.bn_stats(bs[:, 6 * i:6 * i + 6], h[:, 512 * i:512 * i + 512]),
                             *self.h_tok[t])
        v = self.dve.put(lambda e: e.bn_aggr(mv, bs), v)
        v = self.rsqrt(rs, mv[:, 1:2], LN_EPS, v)
        shift = self.bn[:, t, 15:16]
        v = self.pool.put(lambda e: e.tensor_tensor(shift, mv[:, 0:1], rs, ALU.mult), v)
        v = self.pool.put(lambda e: e.tensor_scalar(shift, shift, -1.0, None, ALU.mult), v)
        halves = []
        for i in range(2):
            c = slice(512 * i, 512 * i + 512)
            w = self.act.put(lambda e: e.activation(h[:, c], h[:, c], ACT.Identity, bias=shift, scale=rs), v)
            w = self.dve.put(lambda e: e.tensor_tensor(h[:, c], h[:, c], gg[0][:, c], ALU.mult), w, gg[1])
            gg[0].free = gg[0].free + [w] if t or i else [w]
            w = self.dve.put(lambda e: e.tensor_tensor(h[:, c], h[:, c], gb[0][:, c], ALU.add), w, gb[1])
            gb[0].free = gb[0].free + [w] if t or i else [w]
            halves.append(w)
        self.h_tok[t] = [w]
        return h, halves

    def turn_x(self, t, x, v, wait=3, scale=False):
        def gen():
            for _ in range(wait):
                yield
            for half in range(2):
                tok = self.turn(self.X, 4 * half, t, [x[:, (4 * half + i) * P:(4 * half + i + 1) * P]
                                                      for i in range(4)], v[half])
            if not scale:
                self.xn_free[t] = [tok]
            if scale:
                h = self.h[:, t, :]
                a = self.act.put(lambda e: e.activation(h, h, ACT.Copy, scale=ALPHA), tok, *self.h_tok[t])
                self.h_tok[t] = [a]
        for i in range(8):
            self.X.ready.pop((i, t), None)
        self.lanes[3 if t else 0].append(gen())

    def down(self, name, ix, k0, n_units, sizes, epi):
        u = 0
        for size in sizes:
            jobs = []
            for _ in range(size):
                jobs.append(dict(key=(name, ix, k0 + 2 * u * P, 2, 0, D), X=self.M, slots=[2 * u, 2 * u + 1],
                                 segs=[(0, 0, 512), (1, 512, 1024)], first=(u == 0), last=(u == n_units - 1),
                                 epi=epi))
                u += 1
            self.group(jobs)
        assert u == n_units

    def ffn1(self, l, pre, after, loads):
        self.mix_to_ffn()
        self.loads = loads()
        gate, up, dn = pre + "_w_gate", pre + "_w_up", pre + "_w_down"
        for n0, chunks, sizes in ((0, (512, 512, 512), (2, 4)), (1536, (512, 512, 256), (1, 4))):
            self.M.ready.clear()
            slot = 0
            c0 = n0
            for n in chunks:
                jobs = []
                for b, name in ((0, gate), (1, up)):
                    parts = [(0, 4), (4, 4)] if n == 512 else [(0, 8)]
                    for i, (k, kt) in enumerate(parts):
                        jobs.append(dict(key=(name, (l,), k * P, kt, c0, n), X=self.X,
                                         slots=list(range(k, k + kt)), segs=[(b, 0, n)], first=(i == 0),
                                         last=(i == len(parts) - 1),
                                         epi=self.silu_epi(n) if b == 0 else self.up_epi(n, slot)))
                self.group(jobs)
                slot += n // P
                c0 += n
            half2 = n0 > 0
            self.down(dn, (l,), n0, sum(chunks) // 256, sizes,
                      lambda t, tok, half2=half2: (self.add(t, tok), after(t) if half2 else None))

    def silu_epi(self, n):
        def epi(t, tok):
            bank = self.main[t][0]
            a = self.act.put(lambda e: e.activation(self.sg[t][:, 0:n], bank[:, 0:n], ACT.Silu),
                             tok, *self.sg_free[t])
            bank.free = [a]
            self.sg_tok[t] = a
        return epi

    def up_epi(self, n, slot):
        def epi(t, tok):
            bank = self.main[t][1]
            v = self.dve.put(lambda e: e.tensor_tensor(self.mn[t][:, 0:n], bank[:, 0:n], self.sg[t][:, 0:n],
                                                       ALU.mult), tok, self.sg_tok[t], *self.mn_free[t])
            bank.free = [v]
            self.sg_free[t] = [v]
            self.later_turn(t, n, slot, v)
        return epi

    def later_turn(self, t, n, slot, v):
        def gen():
            yield
            tok = self.turn(self.M, slot, t, [self.mn[t][:, i * P:i * P + P] for i in range(n // P)], v)
            self.mn_free[t] = [tok]
        g = gen()
        self.lanes[1 + t].append(g)

    def ffn2(self, l, after, loads):
        self.mix_to_ffn()
        self.loads = loads()
        for n0, n_chunks, sizes in ((0, 3, (2, 4)), (1536, 2, (2, 2)), (2560, 3, (2, 4))):
            self.M.ready.clear()
            for c in range(n_chunks):
                b = c % 2
                c0 = n0 + 512 * c
                self.group([dict(key=("w_ff1_2", (l,), 512 * i, 4, c0, 512), X=self.X,
                                 slots=list(range(4 * i, 4 * i + 4)), segs=[(b, 0, 512)], first=(i == 0),
                                 last=(i == 1), epi=self.relu_epi(b, 4 * c)) for i in range(2)])
            end = n0 == 2560
            self.down("w_ff2_2", (l,), n0, n_chunks * 2, sizes,
                      lambda t, tok, end=end: (self.add(t, tok, 1.0), after(t) if end else None))

    def relu_epi(self, b, slot):
        def epi(t, tok):
            bank = self.main[t][b]
            a = self.act.put(lambda e: e.activation(self.sg[t][:, :], bank[:, :], ACT.Relu),
                             tok, *self.sg_free[t])
            v = self.dve.put(lambda e: e.scalar_tensor_tensor(self.mn[t][:, :], bank[:, :], 0.0, self.sg[t][:, :],
                                                              ALU.max, ALU.mult), a, *self.mn_free[t])
            bank.free = [v]
            self.sg_free[t] = [v]
            self.later_turn(t, 512, slot, v)
        return epi

    def mix_to_ffn(self):
        f = self.ffn_fence = self.fence()
        self.sg_free, self.sg_tok = [list(f), list(f)], {}
        self.mn_free = [list(f), list(f)]
        for s in range(12):
            for t in range(2):
                self.M.used[(s, t)] = list(f)

    def start(self):
        A = self.A
        x = A["x"]
        self.xn_free = [[], []]
        self.X = Turned("X", self.xh, self.xl)
        self.M = Turned("M", self.mh, self.ml)
        self.lane_free = [[], [], []]
        V, C = self.dve.put, self.act.put
        self.h_tok = [[self.ld(f"x{t}", self.h[:, t, :], x[0, t * P:t * P + P, :], queue=self.sp)] for t in range(2)]
        k_ident = self.ld("ident", self.ident[:, :], A["c_ident"], queue=self.sp)
        for j in range(NRAW):
            self.fetch(j)
        m = self.pool.put(lambda e: e.memset(self.nhalf[:, :], -0.5))
        self.memset_tok = m
        g = self.gain_load(A["ffn1_norm"][0])
        k = [self.ld("const", d, s) for d, s in (
            (self.mask[:, :], A["c_mask"]), (self.freq[:, :], A["c_freq"]),
            (self.pos_i[:, :], A["pos_row"].partition_broadcast(P)), (self.pos_c[:, :], A["pos_col"]),
            (self.lams[:, :], A["lams"].partition_broadcast(P)), (self.scan[:, :], A["c_scan"]))][-1]
        self.pe.put(lambda e: e.transpose(self.pb[4][:, 0:P], self.ident[:, :], self.ident[:, :]), k_ident)
        for t in range(2):
            x_, v = self.rms(t, g)
            self.turn_x(t, x_, v, 0)
        m = self.pool.put(lambda e: e.memset(self.ones[:, :], 1.0 / P))
        m = self.pool.put(lambda e: e.memset(self.half_pi[:, :], math.pi / 2))
        m = self.pool.put(lambda e: e.memset(self.one[:, :], 1.0))
        m = self.pool.put(lambda e: e.memset(self.kr[:, :, 0:64], 0.0))
        self.memset_tok = m
        self.drain()
        self.lanes[0].append(self.tables(k))

    def tables(self, k):
        V, C = self.dve.put, self.act.put
        for _ in range(4):
            yield
        a = V(lambda e: e.tensor_copy(self.pos_f[:, :], self.pos_c[:, :]), k)
        b = V(lambda e: e.tensor_copy(self.pos_r[:, :], self.pos_i[:, :]), k)
        d0, d1 = self.dist[:, 0:128], self.dist[:, 128:384]
        a = V(lambda e: e.tensor_scalar(d0, self.pos_r[:, 0:128], self.pos_f[:, 0:1], None,
                                        ALU.subtract), a, b)
        a = V(lambda e: e.tensor_scalar(d1, self.pos_r[:, :], self.pos_f[:, 1:2], None,
                                        ALU.subtract), a)
        yield
        a = C(lambda e: e.activation(self.dist[:, :], self.dist[:, :], ACT.Abs), a)
        yield
        a = V(lambda e: e.scalar_tensor_tensor(self.dist[:, :], self.mask[:, :], -1e4, self.dist[:, :],
                                               ALU.mult, ALU.add), a)
        yield
        for i in range(4):
            a = V(lambda e, i=i: e.tensor_scalar(self.ang[:, 16 * i:16 * i + 16], self.freq[:, 16 * i:16 * i + 16],
                                                 self.pos_f[:, i:i + 1], None, ALU.mult), a)
        a = V(lambda e: e.tensor_scalar(self.angk[:, :], self.ang[:, :], 1 / (2 * math.pi), MAGIC, ALU.mult,
                                        ALU.add), a)
        a = V(lambda e: e.tensor_scalar(self.angk[:, :], self.angk[:, :], MAGIC, None, ALU.subtract), a)
        yield
        for c in TWO_PI:
            a = V(lambda e, c=c: e.scalar_tensor_tensor(self.ang[:, :], self.angk[:, :], -c, self.ang[:, :],
                                                        ALU.mult, ALU.add), a)
        lim = 3.1415925
        a = V(lambda e: e.tensor_scalar(self.ang[:, :], self.ang[:, :], lim, -lim, ALU.min, ALU.max), a)
        yield
        b = C(lambda e: e.activation(self.angk[:, :], self.ang[:, :], ACT.Abs), a)
        cs = self.cs[:, :, :, :, :].rearrange("p a b t k -> p a (b t k)")
        C(lambda e: e.activation(cs[:, 0, :], self.angk[:, :], ACT.Sin, bias=self.half_pi[:, :], scale=-1.0),
          b, self.memset_tok)
        self.rope_tok = C(lambda e: e.activation(cs[:, 1, :], self.ang[:, :], ACT.Sin), a)
        yield
        v = k
        for l in range(L):
            o = 128 * l
            for i in range(2):
                q, kk = self.lams[:, o + 64 * i:o + 64 * i + 32], self.lams[:, o + 64 * i + 32:o + 64 * i + 64]
                v = V(lambda e, q=q, kk=kk: e.tensor_tensor(self.lamt[:, :], q, kk, ALU.mult), v)
                v = V(lambda e, c=2 * l + i: e.tensor_reduce(self.epsc[:, c:c + 1], self.lamt[:, :], AXX, ALU.add), v)
            yield
        a = C(lambda e: e.activation(self.epsc[:, 4:8], self.epsc[:, 0:4], ACT.Exp), v)
        yield
        for l in range(L):
            li = 0.8 - 0.6 * math.exp(-0.3 * l)
            c = 4 + 2 * l
            v = V(lambda e, l=l, c=c: e.tensor_tensor(self.lam[:, l:l + 1], self.epsc[:, c + 1:c + 2],
                                                      self.epsc[:, c:c + 1], ALU.subtract), a)
            v = V(lambda e, l=l, li=li: e.tensor_scalar(self.lam[:, l:l + 1], self.lam[:, l:l + 1], -li, None,
                                                        ALU.add), v)
        self.lam_tok = v

    def rope(self, kind, x, heads, w, o, tmp, *waits):
        V = self.dve.put
        x1, x2 = x[:, :, :, o:o + 16], x[:, :, :, o + 16:o + 32]
        cos = self.cs[:, 0, kind, :, :].unsqueeze(2).broadcast_to([P, 2, heads, 16])
        sin = self.cs[:, 1, kind, :, :].unsqueeze(2).broadcast_to([P, 2, heads, 16])
        n = 2 * heads * 16
        t = [tmp[:, i * n:(i + 1) * n].rearrange("p (a b c) -> p a b c", a=2, b=heads) for i in range(2)]
        v = V(lambda e: e.tensor_tensor(t[0], x1, sin, ALU.mult), self.rope_tok, *waits)
        v = V(lambda e: e.tensor_tensor(t[1], x2, sin, ALU.mult), v)
        v = V(lambda e: e.tensor_tensor(x1, x1, cos, ALU.mult), v)
        v = V(lambda e: e.tensor_tensor(x2, x2, cos, ALU.mult), v)
        v = V(lambda e: e.tensor_tensor(x1, x1, t[1], ALU.subtract), v)
        v = V(lambda e: e.tensor_tensor(x2, x2, t[0], ALU.add), v)
        return v

    def scores(self, q, k, *waits):
        bank = self.side()
        self.pe.put(lambda e: e.matmul(bank[:, 0:128], q[0], k(128), start=True, stop=True), *waits, *bank.free,
                    inc=False)
        return bank, self.pe.put(lambda e: e.matmul(bank[:, 128:384], q[1], k(256), start=True, stop=True))

    def exps(self, Sb, st, c, scale, v):
        parts = (Sb[:, 0:128], Sb[:, 128:384])
        for i, p in enumerate(parts):
            r = self.dve.put(lambda e, i=i, p=p: e.tensor_reduce(st[:, c + i:c + i + 1], p, AXX, ALU.max), v)
        r = self.dve.put(lambda e: e.tensor_scalar(st[:, c:c + 2], st[:, c:c + 2], -scale, None, ALU.mult), r)
        for i, p in enumerate(parts):
            a = self.act.put(lambda e, i=i, p=p: e.activation(p, p, ACT.Exp, bias=st[:, c + i:c + i + 1], scale=scale,
                                                              accum_out=st[:, c + 4 + i:c + 5 + i]), r)
        return a

    def turn_probs(self, Sb, PT, v, *war):
        bank = self.side()
        for i in range(3):
            tok = self.pe.put(lambda e, i=i: e.transpose(bank[:, i * P:i * P + P], Sb[:, i * P:i * P + P],
                                                         self.ident[:, :]),
                              *([v] + bank.free if i == 0 else []), inc=(i == 2))
        a = self.act.put(lambda e: e.activation(PT[:, 0:384], bank[:, 0:384], ACT.Copy), tok, *war)
        bank.free = [a]
        return a

    def weigh(self, PT, v, n, outs, r, rt, a, squares=None):
        bank = self.side()
        self.pe.put(lambda e: e.matmul(bank[:, 0:n], PT[:, 0:128], v[0], start=True, stop=True), *a, *bank.free,
                    inc=False)
        self.pe.put(lambda e: e.matmul(bank[:, n:2 * n], PT[:, 128:256], v[0], start=True, stop=False), inc=False)
        tok = self.pe.put(lambda e: e.matmul(bank[:, n:2 * n], PT[:, 256:384], v[1], start=False, stop=True))
        for t in range(2):
            d = self.act.put(lambda e, t=t: e.activation(outs[t], bank[:, t * n:t * n + n], ACT.Copy,
                                                         scale=r[:, t:t + 1]), tok, *rt)
            if squares:
                d = self.act.put(lambda e, t=t: e.activation(PT[:, t * n:t * n + n], bank[:, t * n:t * n + n],
                                                             ACT.Square, scale=r[:, t:t + 1],
                                                             accum_out=squares[t]))
        bank.free = [d]
        return d

    def diff_head(self, i, l, h):
        st = self.st[:, 16 * i:16 * i + 16]
        S0, S1 = self.lS[i]
        scale = 32 ** -0.5
        slope = 2.0 ** -(h + 1)
        f, o = h // 2, 64 * (h % 2)
        V = self.dve.put
        for m, Sb in enumerate((S0, S1)):
            p = o + 32 * m
            bank, tok = self.scores(
                [self.dqT[p:p + 32, f, t * P:t * P + P] for t in range(2)],
                lambda n, p=p: self.dkT[p:p + 32, f, 0:n], *self.dqk_tok)
            v = V(lambda e, Sb=Sb, bank=bank: e.scalar_tensor_tensor(
                Sb[:, :], self.dist[:, :], -slope / scale, bank[:, 0:384], ALU.mult, ALU.add),
                tok, *self.lane_free[i])
            bank.free = [v]
            a = self.exps(Sb, st, 2 * m, scale, v)
            yield
        v = V(lambda e: e.reciprocal(st[:, 8:12], st[:, 4:8]), a)
        v = V(lambda e: e.scalar_tensor_tensor(st[:, 12:14], st[:, 4:6], self.lam[:, l:l + 1], st[:, 10:12],
                                               ALU.mult, ALU.mult), v, self.lam_tok)
        for t, (c0, c1) in enumerate(((0, 128), (128, 384))):
            w = V(lambda e, t=t, c0=c0, c1=c1: e.scalar_tensor_tensor(
                S0[:, c0:c1], S1[:, c0:c1], st[:, 12 + t:13 + t], S0[:, c0:c1], ALU.mult, ALU.add), v)
        yield
        yield
        a = self.turn_probs(S0, S1, w)
        yield
        yield
        while not self.pin_free or len(self.dv_toks) < 2:
            yield
        hs = slice(64 * h, 64 * h + 64)
        v = self.weigh(S1, [self.dv[:, t, hs] for t in range(2)], 64, [self.pin[:, t, hs] for t in range(2)],
                       st[:, 8:10], [w] + self.pin_free, [a] + self.dv_toks,
                       [self.ssq[:, t, h:h + 1] for t in range(2)])
        self.lane_free[i] = [v]
        self.diff_done.append(v)

    def plain_head(self, i, scale, turn_q, k, v, n, outs, done, turned=None, h=0):
        st = self.st[:, 16 * i:16 * i + 16]
        Sb, PT = self.lS[i]
        Q = self.lQ[i]
        bank = self.side()
        for j, x in enumerate(turn_q):
            w = x.shape[1]
            tok = self.pe.put(lambda e, j=j, x=x, w=w: e.transpose(bank[0:w, j * P:j * P + P], x, self.ident[:, :]),
                              *(self.qk_tok + bank.free if j == 0 else []), inc=(j == len(turn_q) - 1))
        if turned is not None:
            turned[h] = tok
        c = len(turn_q) * P
        a = self.act.put(lambda e: e.activation(Q[0:w, 0:c], bank[0:w, 0:c], ACT.Copy), tok, *self.lane_free[i])
        bank.free = [a]
        yield
        bank, tok = self.scores([Q[0:w, 0:P], Q[0:w, P:2 * P]], k, a, *self.qk_tok)
        d = self.dve.put(lambda e: e.tensor_tensor(Sb[:, :], bank[:, 0:384], self.mask[:, :], ALU.add), tok,
                         *self.lane_free[i])
        bank.free = [d]
        a = self.exps(Sb, st, 0, scale, d)
        r = self.dve.put(lambda e: e.reciprocal(st[:, 8:10], st[:, 4:6]), a)
        yield
        yield
        b = self.turn_probs(Sb, PT, a, tok)
        yield
        yield
        while turned is not None and len([x for x in turned if x < h]) < h:
            yield
        war = list(turned.values()) if turned is not None else [tok]
        d = self.weigh(PT, v, n, outs, st[:, 8:10], [r] + war, [b])
        self.lane_free[i] = [d]
        done.append(d)

    def gates(self, name, l, c0, slot):
        for j in range(2):
            def epi(t, tok, j=j):
                bank = self.main[t][j]
                a = self.act.put(lambda e: e.activation(self.G[slot][:, t, 512 * j:512 * j + 512], bank[:, :],
                                                        ACT.Tanh, scale=0.5), tok, *self.g_free[slot])
                bank.free = [a]
                self.g_tok[slot, t, j] = a
            self.group([dict(key=(name, (l,), 512 * i, 4, c0 + 512 * j, 512), X=self.X,
                             slots=list(range(4 * i, 4 * i + 4)), segs=[(j, 0, 512)], first=(i == 0), last=(i == 1),
                             epi=epi) for i in range(2)])

    def branch(self, name, l, n, Y, slots, slot, first, last, stay=None):
        self.g_free[slot] = []

        def epi(j):
            def f(t, tok):
                bank = self.main[t][j]
                G = self.G[slot][:, t, 512 * j:512 * j + 512]
                m = self.xn[:, t, 512 * j:512 * j + 512]
                o = m if first else G
                v = self.dve.put(lambda e: e.scalar_tensor_tensor(o, G, 1.0, bank[:, :], ALU.add, ALU.mult),
                                 tok, self.g_tok[slot, t, j], *(self.m_free if first else []))
                bank.free = [v]
                if not first:
                    v = self.dve.put(lambda e: e.tensor_tensor(m, m, G, ALU.add), v, *self.m_tok[t, j])
                self.m_tok[t, j] = [v]
                self.g_free[slot].append(v)
                if last:
                    def gen():
                        yield
                        tok = self.turn(self.M, 4 * j, t, [m[:, i * P:i * P + P] for i in range(4)], v)
                        self.xn_free[t] = [tok]
                    self.lanes[3 if t else 0].append(gen())
            return f
        self.group([dict(key=(name, (l, n), 0, 4, 512 * j, 512), X=Y, slots=slots, segs=[(j, 0, 512)], first=True,
                         last=True, epi=epi(j)) for j in range(2)])

    def way_out(self, name, l, after):
        self.group([dict(key=(name, (l,), 512 * i, 4, 512 * b, 512), X=self.M, slots=list(range(4 * i, 4 * i + 4)),
                         segs=[(b, 0, 512)], first=(i == 0), last=(i == 1),
                         epi=(lambda t, tok: (self.add(t, tok), after(t))) if (i, b) == (1, 1) else
                         (lambda t, tok: None)) for i in range(2) for b in range(2)])

    def merged_ready(self):
        f = self.fence()
        self.M.ready.clear()
        for s in range(8):
            for t in range(2):
                self.M.used[(s, t)] = list(f)

    def copy_epi(self, dst, b, n=512, toks=None, func=ACT.Copy):
        def epi(t, tok):
            bank = self.main[t][b]
            a = self.act.put(lambda e: e.activation(dst(t), bank[:, 0:n], func), tok, *self.r_free)
            bank.free = [a]
            toks.append(a)
        return epi

    def cols(self, name, l, c0, b, epi, n=512):
        return [dict(key=(name, (l,), 512 * i, 4, c0, n), X=self.X, slots=list(range(4 * i, 4 * i + 4)),
                     segs=[(b, 0, n)], first=(i == 0), last=(i == 1), epi=epi) for i in range(2)]

    def loads1(self, l):
        A, f = self.A, self.ffn_fence
        return (self.ld("gq", self.gq[:, :], A["gq"][l].partition_broadcast(P), *f),
                self.ld("sub", self.sub[:, :], A["diff_subln"][l].partition_broadcast(P), *f),
                [self.ld("pc", self.pc[:, :], A["c_pool"], *f)],
                [self.ld("pw", self.pw[:, :, :], A["pool_w"][l].rearrange("g c d -> c g d"), *f),
                 self.ld("pbs", self.pbs[:, :], A["pbs"][l], *f)])

    def mixer1(self, l, after):
        A, V, C, T = self.A, self.dve.put, self.act.put, self.pe.put
        f = self.fence()
        self.r_free = f
        self.g_free, self.g_tok, self.m_tok = [list(f), list(f)], {}, {}
        self.lane_free = [list(f) for _ in range(3)]
        self.diff_done, self.mla_done = [], []
        W = "w_in"
        k_gq, k_sub, k_pc, k_pw = self.loads
        C1 = Turned("C", self.ch, self.cl)
        for s in range(3):
            for t in range(2):
                C1.used[(s, t)] = list(f)
        kr_toks, pin_toks, self.dv_toks, self.pin_free = [], [], [], []

        def c_epi(t, tok):
            bank = self.main[t][0]
            ms = self.bn[:, t, 0:2]
            rs = self.bn[:, t, 2:4]
            tmp = self.lQ[t]
            a = C(lambda e: e.activation(tmp[:, 0:256], bank[:, 0:256], ACT.Square, scale=1 / 16,
                                         accum_out=ms[:, 0:1]), tok, *self.lane_free[t])
            a = C(lambda e: e.activation(tmp[:, 256:384], bank[:, 256:384], ACT.Square, scale=128 ** -0.5,
                                         accum_out=ms[:, 1:2]))
            b = C(lambda e: e.activation(self.kr[:, t, 64:96], bank[:, 384:416], ACT.Copy), *self.r_free)
            v = self.rsqrt(rs, ms, EPS, a)
            kr_toks.append(b)

            def gen():
                yield
                for i, (c0, c1) in enumerate(((0, 256), (256, 384))):
                    d = V(lambda e, i=i, c0=c0, c1=c1: e.scalar_tensor_tensor(
                        self.cn[:, t, c0:c1], bank[:, c0:c1], rs[:, i:i + 1], self.gq[:, c0:c1], ALU.mult, ALU.mult),
                        v, b, k_gq, *f)
                bank.free = [d, b]
                c_scaled.append(t)
                yield
                while (7, 1) not in self.X.ready or (7, 0) not in self.X.ready:
                    yield
                yield
                for s in range(3):
                    C1.used[(s, t)] = f + self.xn_free[0] + self.xn_free[1]
                self.turn(C1, 0, t, [self.cn[:, t, i * P:i * P + P] for i in range(3)], d)
            self.lanes[t].append(gen())
            self.lane_free[t] = [a]

        c_scaled = []
        self.group(self.cols(W, l, 0, 0, c_epi, 416) +
                   self.cols(W, l, 1952, 1, self.copy_epi(lambda t: self.pin[:, t, :], 1, 512, pin_toks)))
        while len(c_scaled) < 2:
            self.pump()

        def qk_epi(dst, b, toks):
            def epi(tok):
                for i in range(2):
                    bank = self.main[i][b]
                    o = dst[:, 2 * i:2 * i + 2, :].rearrange("p a s -> p (a s)")
                    a = C(lambda e, o=o, bank=bank: e.activation(o, bank[:, :], ACT.Copy), tok, *f)
                    bank.free = [a]
                    toks.append(a)
            return epi
        Yp = Turned("Yp", self.yph, self.ypl)
        pool_done = []

        def pool():
            yield
            yield
            for i in range(2):
                bank = self.side()
                for g in (2 * i, 2 * i + 1):
                    o = (g % 2) * S
                    gs = slice(g * P, g * P + P)
                    T(lambda e, g=g, o=o, gs=gs, bank=bank: e.matmul(
                        bank[:, o:o + 256], self.pin[:, 0, gs], self.pc[:, 256 * g:256 * g + 256],
                        start=True, stop=False, skip_group_check=True), *pin_toks, *k_pc,
                        *(bank.free if g % 2 == 0 else []), inc=False)
                    tok = T(lambda e, g=g, o=o, gs=gs, bank=bank: e.matmul(
                        bank[:, o + 128:o + 256], self.pin[:, 1, gs], self.pc[:, 1024 + P * g:1024 + P * g + P],
                        start=False, stop=True, skip_group_check=True))
                a = C(lambda e, i=i, bank=bank: e.activation(
                    self.pT[:, 2 * i:2 * i + 2, :].rearrange("p a s -> p (a s)"), bank[:, :], ACT.Copy), tok, *f)
                bank.free = [a]
                yield
            self.pin_free = [tok]
            for i in range(2):
                bank = self.side()
                for g in (2 * i, 2 * i + 1):
                    o = (g % 2) * S
                    tok = T(lambda e, g=g, o=o, bank=bank: e.matmul(
                        bank[:, o:o + 256], self.pw[:, g, :], self.pT[:, g, :], start=True, stop=True), a, *k_pw,
                        *(bank.free if g % 2 == 0 else []))
                for g in (2 * i, 2 * i + 1):
                    o = (g % 2) * S
                    v = V(lambda e, g=g, o=o, bank=bank: e.tensor_scalar(
                        self.pT[:, g, :], bank[:, o:o + 256], self.pbs[:, g:g + 1], self.pbs[:, 4 + g:5 + g],
                        ALU.add, ALU.mult), tok)
                bank.free = [v]
                yield
            pT = self.pT[:, :, :].rearrange("p a s -> p (a s)")
            a = C(lambda e: e.activation(self.yph[:, :, :].rearrange("p a s -> p (a s)"), pT, ACT.Copy), v, *f)
            v = V(lambda e: e.tensor_tensor(self.ypl[:, :, :].rearrange("p a s -> p (a s)"), pT,
                                            self.yph[:, :, :].rearrange("p a s -> p (a s)").bitcast(F32),
                                            ALU.subtract), a, *f)
            for s in range(4):
                for t in range(2):
                    Yp.ready[(s, t)] = [a, v]
            self.g_free[1] = [v]
            self.kt_free = [tok]
            pool_done.append(v)

        self.lanes[3].append(pool())
        qk = []
        self.turned_group(self.X, [(W, (l,), 512 * i, 4, 416, 512) for i in range(2)], 0, qk_epi(self.dqT, 0, qk))
        self.turned_group(self.X, [(W, (l,), 512 * i, 4, 928, 512) for i in range(2)], 1, qk_epi(self.dkT, 1, qk))
        self.dqk_tok = [qk[-1]]

        def diff_lane(i):
            for _ in range(STAGGER * i):
                yield
            for h in range(i, 8, 3):
                yield from self.diff_head(i, l, h)
        for i in range(3):
            self.lanes[i].append(diff_lane(i))
        self.group(self.cols(W, l, 1440, 0, self.copy_epi(lambda t: self.dv[:, t, :], 0, 512, self.dv_toks)))
        while not pool_done:
            self.pump()

        kr_tok = self.rope(0, self.kr[:, :, :].unsqueeze(2), 1, 96, 64, self.cn[:, 1, :], *kr_toks,
                           *C1.ready[(2, 0)], *C1.ready[(2, 1)])
        q_toks = []

        def q_epi(t, tok):
            for b in range(2):
                bank = self.main[t][b]
                a = C(lambda e, b=b, bank=bank: e.activation(
                    self.q[:, t, 4 * b:4 * b + 4, :], bank[:, 0:384].rearrange("p (h n) -> p h n", n=96), ACT.Copy),
                    tok, kr_tok, *f)
                bank.free = [a]
            q_toks.append(a)
        self.group([dict(key=("mla_w_uq", (l,), 0, 2, 0, 768), X=C1, slots=[0, 1],
                         segs=[(0, 0, 384), (1, 384, 768)], first=True, last=True, epi=q_epi)])
        self.latent_kv(l, C1, kr_tok, q_toks, f)
        X = self.X

        yo = self.q[:, :, :, :].rearrange("p t h n -> p t (h n)")
        turned = {}

        def mla_lane(i):
            for h in range(i, 8, 3):
                hs = slice(64 * h, 64 * h + 64)
                yield from self.plain_head(
                    i, 96 ** -0.5, [self.q[:, t, h, :] for t in range(2)],
                    lambda n, h=h: self.kT[0:96, h, 0:n], [self.v[:, t, hs] for t in range(2)], 64,
                    [yo[:, t, hs] for t in range(2)], self.mla_done, turned, h)

        Yd = Turned("Yd", self.yph, self.ypl)

        def diff_end():
            while len(self.diff_done) < 8:
                yield
            c = (1 - (0.8 - 0.6 * math.exp(-0.3 * l))) ** -2
            p = self.pool.put(lambda e: e.tensor_scalar(self.ssq[:, :, :], self.ssq[:, :, :], c / 64, c * EPS,
                                                        ALU.mult, ALU.add), *self.diff_done)
            p = self.pool.put(lambda e: e.tensor_tensor(
                self.ssq[:, :, :].rearrange("p a b -> p (a b)"), self.ssq[:, :, :].rearrange("p a b -> p (a b)"),
                self.nhalf[:, :].broadcast_to([P, 16]), ALU.pow), p)
            yield
            for t in range(2):
                y = self.pin[:, t, :].rearrange("p (h n) -> p h n", n=64)
                v = V(lambda e: e.tensor_tensor(y, y, self.ssq[:, t, :].unsqueeze(2).broadcast_to([P, 8, 64]),
                                                ALU.mult), p)
                v = V(lambda e: e.tensor_tensor(y, y, self.sub[:, :].unsqueeze(1).broadcast_to([P, 8, 64]),
                                                ALU.mult), v, k_sub)
                yield
            while not pooled:
                yield
            Yd.used = dict(Yp.used)
            for t in range(2):
                self.turn(Yd, 0, t, [self.pin[:, t, i * P:i * P + P] for i in range(4)], v)
                yield

        def mla_end():
            while len(self.mla_done) < 8:
                yield
            for t in range(2):
                self.turn(X, 0, t, [yo[:, t, P * i:P * i + P] for i in range(4)], *self.mla_done)
                yield
        for i in range(3):
            self.lanes[i].append(mla_lane(i))
        pooled = []
        self.lanes[3].append(diff_end())
        self.gates(W, l, 2464 + 2048, 0)
        self.m_free = self.fence()
        self.branch("w_branch", l, 2, Yp, [0, 1, 2, 3], 0, True, False)
        pooled.append(True)
        self.gates(W, l, 2464 + 1024, 1)
        self.gates(W, l, 2464, 0)
        X.ready.clear()
        self.lanes[3].append(mla_end())
        self.branch("w_branch", l, 1, Yd, [0, 1, 2, 3], 1, False, False)
        while (3, 1) not in X.ready:
            self.pump()
        self.merged_ready()
        self.branch("w_branch", l, 0, X, [0, 1, 2, 3], 0, False, True)
        self.way_out("w_out", l, after)

    def latent_kv(self, l, C1, kr_tok, q_toks, f):
        V, C, T = self.dve.put, self.act.put, self.pe.put
        j = self.take(("mla_w_ukv", (l,), 0, 1, 0, 1024))
        dry = self.plan is None
        if not dry:
            wh, wl = self.weights(j)
            waits = list(self.split_tok[j]) + self.need(C1, [2], [0, 1])
        banks = [self.main[0][0], self.main[0][1], self.main[1][0], self.main[1][1]]
        sides = [self.side(), self.side()]
        toks = []
        if not dry:
            for t in range(2):
                bank = sides[t]
                for n, (x, w) in enumerate(((C1.h, wl), (C1.h, wh), (C1.l, wh))):
                    tok = T(lambda e, bank=bank, x=x[:, 2, t * P:t * P + P],
                            w=w[:, 0, :].rearrange("p (h n) -> p h n", n=128)[:, :, 64:128], n=n:
                            e.matmul(bank[:, :], x, w, start=(n == 0), stop=(n == 2)),
                            *(waits + bank.free if n == 0 else []), inc=(n == 2))
                toks.append(tok)
            for i, bank in enumerate(banks):
                for h in (2 * i, 2 * i + 1):
                    for n, (w, x) in enumerate(((wl, C1.h), (wh, C1.h), (wh, C1.l))):
                        tok = T(lambda e, bank=bank, h=h, w=w[:, 0, h * P:h * P + P], x=x[:, 2, :], n=n: e.matmul(
                            bank[:, (h % 2) * S:(h % 2) * S + S], w, x, start=(n == 0), stop=(n == 2),
                            skip_group_check=True),
                            *(bank.free if n == 0 and h % 2 == 0 else []), inc=(n == 2))
                toks.append(tok)
            self.done_tok[j] = [tok]
        else:
            toks = [(self.pe.sem, 0)] * 6
        for t in range(2):
            a = C(lambda e, t=t: e.activation(self.v[:, t, :], sides[t][:, :], ACT.Copy), toks[t], *f)
            sides[t].free = [a]
        for i, bank in enumerate(banks):
            k = V(lambda e, i=i, bank=bank: e.tensor_copy(
                self.kT[0:64, 2 * i:2 * i + 2, :], bank[0:64, :].rearrange("p (a s) -> p a s", s=S)), toks[2 + i],
                *self.kt_free)
            bank.free = [k]
        v = kr_tok
        bank = self.side()
        for t in range(2):
            tok = T(lambda e, t=t, bank=bank: e.transpose(bank[0:96, t * P:t * P + P], self.kr[:, t, :],
                                                          self.ident[:, :]),
                    *([v, self.memset_tok] + bank.free if t == 0 else []), inc=(t == 1))
        kr = bank[64:96, 0:256].unsqueeze(1).broadcast_to([32, 4, S])
        a = C(lambda e: e.activation(self.kT[64:96, 0:4, :], kr, ACT.Copy), tok, *self.kt_free)
        b = C(lambda e: e.activation(self.kT[64:96, 4:8, :], kr, ACT.Copy))
        bank.free = [b]
        v = self.rope(0, self.q, 8, 96, 64, self.rope_tmp, *q_toks, v, self.pe.last())
        self.qk_tok = [v, b, a, k]
        self.advance()
        self.pump()

    def loads2(self, l):
        A, f = self.A, self.ffn_fence
        return (self.ld("ws", self.ws[:, :, :], A["gmlp_w_s_2"][l].rearrange("g t s -> t g s"), *f),
                self.ld("tril", self.tril[:, :], A["c_tril"][:, 0:P], *f),
                self.ld("lng", self.lng[:, :, :], A["lng"][l].partition_broadcast(P), *f),
                self.ld("gp", self.gp[:, :], A["gp"][l], *f),
                self.ld("wgu", self.wgu[0:16, :], A["w_gate_up_2"][l], *f))

    def mixer2(self, l, after):
        A, V, C, T = self.A, self.dve.put, self.act.put, self.pe.put
        f = self.fence()
        self.r_free = f
        self.g_free, self.g_tok, self.m_tok = [list(f), list(f)], {}, {}
        self.lane_free = [list(f) for _ in range(3)]
        W, X = "w_in_2", self.X
        k_ws, k_tril, k_lng, k_gp, k_wgu = self.loads

        Yg = Turned("Yg", self.yph, self.ypl)
        for s in range(4):
            for t in range(2):
                Yg.used[(s, t)] = list(f)
        gm_done = []
        zv_tok, zu_toks = {}, {}

        def wst():
            for _ in range(8):
                yield
            bank = self.side()
            for g in range(4):
                tok = T(lambda e: e.transpose(bank[:, g * P:g * P + P], self.ws[:, g, :], self.ident[:, :]),
                        *([k_ws] + bank.free if g == 0 else []), inc=(g == 3))
            v = V(lambda e: e.tensor_tensor(self.wsT[:, :, :], bank[:, :].rearrange("p (g t) -> p g t", g=4),
                                            self.tril[:, :].unsqueeze(1).broadcast_to([P, 4, P]), ALU.mult),
                  tok, k_tril, *f)
            bank.free = [v]
            self.ws_tok = v

        def gelu_epi(b, dst, toks):
            def epi(t, tok):
                bank = self.main[t][b]
                a = C(lambda e: e.activation(dst[:, t, :], bank[:, :], ACT.Gelu), tok, *f, *self.xn_free[0],
                      *self.xn_free[1])
                bank.free = [a]
                toks[t] = a
                if b == 1:
                    self.lanes[3].append(gmlp(t))
            return epi

        def gmlp(t):
            yield
            bn = self.bn[:, t, :]
            z = self.zv[:, t, :]
            v = V(lambda e: e.bn_stats(bn[:, 0:6], z), zv_tok[t], *self.h_tok[t])
            v = V(lambda e: e.bn_aggr(bn[:, 12:14], bn[:, 0:6]), v)
            v = self.rsqrt(bn[:, 14:15], bn[:, 13:14], LN_EPS, v)
            v = V(lambda e: e.tensor_scalar(z, z, bn[:, 12:13], bn[:, 14:15], ALU.subtract, ALU.mult), v)
            v = V(lambda e: e.tensor_tensor(z, z, self.lng[:, 0, :], ALU.mult), v, k_lng)
            v = V(lambda e: e.tensor_tensor(z, z, self.lng[:, 1, :], ALU.add), v)
            yield
            yield
            bank = self.side()
            for g in range(4):
                tok = T(lambda e: e.matmul(bank[:, g * P:g * P + P], self.wsT[:, g, :],
                                           self.zv[:, t, g * P:g * P + P], start=True, stop=True),
                        *([v, self.ws_tok] + bank.free if g == 0 else []), inc=(g == 3))
            for g in range(4):
                u = self.zu[:, t, g * P:g * P + P]
                v = V(lambda e: e.scalar_tensor_tensor(u, bank[:, g * P:g * P + P], self.gp[:, 5 + g:6 + g], u,
                                                       ALU.add, ALU.mult), tok, zu_toks[t], k_gp)
            bank.free = [v]
            yield
            yield
            tok = self.turn(Yg, 0, t, [self.zu[:, t, g * P:g * P + P] for g in range(4)], v)
            gm_done.append(tok)

        self.lanes[3].append(wst())
        mv_t, mq_t, mk_t, gv_t, gq_t, gk_t, gg_t = ([] for _ in range(7))
        flat = lambda x, t: x[:, t, :, :].rearrange("p h n -> p (h n)")
        self.group(self.cols(W, l, 4112, 0, self.copy_epi(lambda t: self.mv[:, t, :], 0, 512, mv_t)) +
                   self.cols(W, l, 3088, 1, self.copy_epi(lambda t: flat(self.mq, t), 1, 512, mq_t)))
        self.group(self.cols(W, l, 3600, 0, self.copy_epi(lambda t: flat(self.mk, t), 0, 512, mk_t)))
        v = self.rope(1, self.mq, 4, 128, 0, self.lG[0][:, :, :].rearrange("p a b -> p (a b)"), *mq_t,
                      *self.lane_free[0])
        v = self.rope(1, self.mk, 4, 128, 0, self.lG[0][:, :, :].rearrange("p a b -> p (a b)"), *mk_t, v)
        self.lane_free[0] = [v]
        self.qk_tok = [v]
        moba_done, gla_done = [], []

        def moba_lane(i, heads):
            for _ in range(1 + STAGGER * i):
                yield
            for h in heads:
                yield from self.plain_head(
                    i, 128 ** -0.5, [x[:, t, h, :] for x in (self.mq, self.mk) for t in range(2)],
                    lambda n, i=i: self.lQ[i][:, 256:256 + n], [self.mv[:, t, h * P:h * P + P] for t in range(2)],
                    128, [self.mq[:, t, h, :] for t in range(2)], moba_done)
        for i, heads in enumerate(((0, 3), (1,), (2,))):
            self.lanes[i].append(moba_lane(i, heads))
        self.group(self.cols(W, l, 2576, 0, gelu_epi(0, self.zv, zv_tok)) +
                   self.cols(W, l, 2064, 1, gelu_epi(1, self.zu, zu_toks)))

        def t_epi(dst, b, toks, silu=False):
            def epi(tok):
                for i in range(2):
                    bank = self.main[i][b]
                    o = dst[:, 2 * i:2 * i + 2, :].rearrange("p a s -> p (a s)")
                    if silu:
                        a = C(lambda e: e.activation(o, bank[:, :], ACT.Tanh, scale=0.5), tok, *f)
                        a = V(lambda e: e.scalar_tensor_tensor(o, o, 1.0, bank[:, :], ALU.add, ALU.mult), a)
                    else:
                        a = C(lambda e: e.activation(o, bank[:, :], ACT.Copy), tok, *f)
                    bank.free = [a]
                    toks.append(a)
            return epi
        wide = lambda c0: [(W, (l,), 512 * i, 4, c0, 512) for i in range(2)]

        def decay():
            while len(gm_done) < 2:
                yield
            wt, a = self.ws_tok, lr_t[0]
            for i in range(2):
                bank = self.side()
                for h in (2 * i, 2 * i + 1):
                    tok = T(lambda e: e.matmul(bank[:, (h % 2) * S:(h % 2) * S + S], self.wgu[0:16, h * P:h * P + P],
                                               self.lrT[0:16, :], start=True, stop=True), a, k_wgu,
                            *(bank.free if h % 2 == 0 else []))
                for h in (2 * i, 2 * i + 1):
                    s = bank[:, (h % 2) * S:(h % 2) * S + S]
                    b = C(lambda e: e.activation(self.bigE[:, h, :], s, ACT.Abs, bias=self.gp[:, h:h + 1]), tok,
                          k_gp, wt, *gm_done)
                for h in (2 * i, 2 * i + 1):
                    s = bank[:, (h % 2) * S:(h % 2) * S + S]
                    v = V(lambda e: e.tensor_scalar(self.bigL[:, h, :], s, self.gp[:, h:h + 1], 0.0, ALU.add,
                                                    ALU.min), b)
                bank.free = [v, b]
                yield
            a = C(lambda e: e.activation(self.bigE[:, :, :], self.bigE[:, :, :], ACT.Exp, scale=-1.0), v)
            a = C(lambda e: e.activation(self.bigE[:, :, :], self.bigE[:, :, :], ACT.Ln, bias=self.one[:, :]), a,
                  self.memset_tok)
            v = V(lambda e: e.tensor_tensor(self.bigL[:, :, :], self.bigL[:, :, :], self.bigE[:, :, :],
                                            ALU.subtract), a)
            self.decay_tok = [v]
        self.decay_tok, lr_t = [], []
        self.turned_group(X, wide(0), 0, t_epi(self.gqT, 0, gq_t))
        self.turned_group(X, wide(512), 1, t_epi(self.gkT, 1, gk_t))
        j = self.take((W, (l,), 0, 8, 2048, 16))
        tok = (self.pe.sem, 0)
        if self.plan is not None:
            wh, wl = self.weights(j)
            bank = self.main[0][1]
            waits = list(self.split_tok[j]) + self.need(X, range(8), [0, 1]) + bank.free
            for k in range(8):
                for n, (w, x) in enumerate(((wl, X.h), (wh, X.h), (wh, X.l))):
                    tok = T(lambda e, w=w[:, k, :], x=x[:, k, :], st=(k == 0 and n == 0), sp=(k == 7 and n == 2):
                            e.matmul(bank[0:16, 0:256], w, x, start=st, stop=sp), *waits, inc=(k == 7 and n == 2))
                    waits = []
            for k in range(8):
                X.used[(k, 0)] = X.used[(k, 1)] = [tok]
            self.done_tok[j] = [tok]
        bank = self.main[0][1]
        lr_t.append(C(lambda e: e.activation(self.lrT[0:16, :], bank[0:16, 0:256], ACT.Copy), tok, *f))
        bank.free = list(lr_t)

        self.lanes[3].append(decay())
        self.group(self.cols(W, l, 1024, 0, self.copy_epi(lambda t: self.gv[:, t, :], 0, 512, gv_t)))
        self.turned_group(X, wide(1536), 1, t_epi(self.ggT, 1, gg_t, True))
        while not self.decay_tok:
            self.pump()

        def gla_lane(i, heads):
            for _ in range(STAGGER * i):
                yield
            for h in heads:
                yield from self.gla_head(i, h, gq_t + gk_t, gv_t, gg_t, gla_done)
        for i, heads in enumerate(((0, 3), (1,), (2,))):
            self.lanes[i].append(gla_lane(i, heads))

        Ym = Turned("Ym", self.yph, self.ypl)

        def moba_end():
            while len(moba_done) < 4:
                yield
            for t in range(2):
                self.turn(Ym, 0, t, [self.mq[:, t, h, :] for h in range(4)], *moba_done)
                yield

        def gla_end():
            while len(gla_done) < 4:
                yield
            hi, lo = X.h[:, 4:8, :], X.l[:, 4:8, :]
            war = [x for s in range(4, 8) for t in range(2) for x in X.used[(s, t)]]
            a = C(lambda e: e.activation(hi, self.ggT[:, :, :], ACT.Copy), *gla_done, *war)
            v = V(lambda e: e.tensor_tensor(lo, self.ggT[:, :, :], hi.bitcast(F32), ALU.subtract), a)
            for s in range(4, 8):
                for t in range(2):
                    X.ready[(s, t)] = [a, v]
        G0 = 4624
        self.gates(W, l, G0 + 1024, 0)
        self.gates(W, l, G0 + 2048, 1)
        self.m_free = self.fence()
        self.branch("w_branch_2", l, 1, Yg, [0, 1, 2, 3], 0, True, False)
        Ym.used = dict(Yg.used)
        self.lanes[3].append(moba_end())
        self.gates(W, l, G0, 0)
        X.ready.clear()
        self.lanes[3].append(gla_end())
        self.branch("w_branch_2", l, 2, Ym, [0, 1, 2, 3], 1, False, False)
        while (7, 1) not in X.ready:
            self.pump()
        self.merged_ready()
        self.branch("w_branch_2", l, 0, X, [4, 5, 6, 7], 0, False, True)
        self.way_out("w_out_2", l, after)

    def gla_head(self, i, h, qk_t, gv_t, gg_t, done):
        V, C, T = self.dve.put, self.act.put, self.pe.put
        G = self.lG[i]
        flat = G[:, :, :].rearrange("p a b -> p (a b)")
        eb, kd, enb = flat[:, 0:256], flat[:, 256:512], flat[:, 512:768]
        kdn, at = G[:, 2:4, :], G[:, 4:6, :]
        S1, S2, S3 = self.bigL[:, h, 0:128], self.bigL[:, h, 128:256], G[:, 6, :]
        st = self.st[:, 16 * i:16 * i + 4]
        bc, E = self.bigL[:, h, :], self.bigE[:, h, :]
        gq, gk, gg = self.gqT[:, h, :], self.gkT[:, h, :], self.ggT[:, h, :]
        gv = [self.gv[:, t, h * P:h * P + P] for t in range(2)]
        free = self.lane_free[i]
        v = V(lambda e: e.tensor_tensor_scan(E, self.scan[:, :], bc, 0.0, ALU.mult, ALU.add), *self.decay_tok)
        w = V(lambda e: e.tensor_scalar(st, E[:, 63:256:64], 1 / 16, None, ALU.mult), v, *free)
        a = C(lambda e: e.activation(eb, E, ACT.Exp, scale=1 / 16), v, *free)
        a = C(lambda e: e.activation(enb, E, ACT.Exp, scale=-1 / 16))
        for c in range(3):
            b = C(lambda e: e.activation(kd[:, 64 * c:64 * c + 64], E[:, 64 * c:64 * c + 64], ACT.Exp,
                                         bias=st[:, c:c + 1], scale=-1 / 16), w)
        yield
        kdv = V(lambda e: e.tensor_tensor(kd[:, 0:192], kd[:, 0:192], gk[:, 0:192], ALU.mult), b, *qk_t)
        qd = V(lambda e: e.scalar_tensor_tensor(gq, gq, 128 ** -0.5, eb, ALU.mult, ALU.mult), a)
        ki = V(lambda e: e.tensor_tensor(gk, gk, enb, ALU.mult), a, kdv)
        z = V(lambda e: e.memset(at, 0.0), ki)
        yield
        yield
        bank = self.side()
        T(lambda e: e.transpose(bank[:, 0:128], kd[:, 0:128], self.ident[:, :]), kdv, *bank.free, inc=False)
        t1 = T(lambda e: e.transpose(bank[0:64, 128:256], kd[:, 128:192], self.ident[:, :]))
        bank2 = self.side()
        for t in range(2):
            ts = slice(t * P, t * P + P)
            t2 = T(lambda e: e.matmul(bank2[:, ts], gk[:, ts], gq[:, ts], start=True, stop=True), qd, ki,
                   *bank2.free)
        a = C(lambda e: e.activation(kdn[:, 0, :], bank[:, 0:128], ACT.Copy), t1)
        a = C(lambda e: e.activation(kdn[0:64, 1, :], bank[0:64, 128:256], ACT.Copy), t1)
        bank.free = [a]
        for t in range(2):
            m = V(lambda e: e.copy_predicated(at[:, t, :], self.chunk[:, :], bank2[:, t * P:t * P + P]), t2, z,
                  self.chunk_tok)
        bank2.free = [m]
        yield
        yield
        bank, bank2 = self.side(), self.side()
        T(lambda e: e.matmul(bank[:, 0:128], kdn[0:64, 0, :], gv[0][0:64, :], start=True, stop=True), a, *gv_t,
          *bank.free, inc=False)
        t1 = T(lambda e: e.matmul(bank[:, 128:256], kdn[0:64, 1, :], gv[1][0:64, :], start=True, stop=True))
        t2 = T(lambda e: e.matmul(bank2[:, 0:128], kdn[64:128, 0, :], gv[0][64:128, :], start=True, stop=True),
               *bank2.free)
        v = V(lambda e: e.tensor_copy(S1, bank[:, 0:128]), t1, v)
        v = V(lambda e: e.scalar_tensor_tensor(S2, S1, eb[:, 127:128], bank2[:, 0:128], ALU.mult, ALU.add), v, t2)
        bank2.free = [v]
        v = V(lambda e: e.scalar_tensor_tensor(S3, S2, eb[:, 191:192], bank[:, 128:256], ALU.mult, ALU.add), v)
        bank.free = [v]
        yield
        bank = self.side()
        w = [v, m] + bank.free
        for t in range(2):
            T(lambda e: e.matmul(bank[:, t * P:t * P + P], gv[t], at[:, t, :], start=(t == 0), stop=False,
                                 skip_group_check=True), *w, inc=False)
        for c, s in ((1, S1), (2, S2), (3, S3)):
            tok = T(lambda e: e.matmul(bank[:, 64 * c:64 * c + 64], s, gq[:, 64 * c:64 * c + 64], start=False,
                                       stop=True, skip_group_check=True))
        a = C(lambda e: e.activation(E, bank[:, 0:256], ACT.Square), tok)
        o = kd
        b = C(lambda e: e.activation(o, bank[:, 0:256], ACT.Copy), tok)
        bank.free = [b]
        yield
        bank = self.side()
        w = [a, self.memset_tok] + bank.free
        for t in range(2):
            tok = T(lambda e: e.matmul(bank[:, t:t + 1], E[:, t * P:t * P + P], self.ones[:, 0:1], start=True,
                                       stop=True), *w, inc=(t == 1))
        v = V(lambda e: e.tensor_scalar(st[:, 0:2], bank[:, 0:2], EPS, None, ALU.add), tok)
        bank.free = [v]
        half = self.nhalf[:, :].broadcast_to([P, 2])
        p = self.pool.put(lambda e: e.tensor_tensor(st[:, 0:2], st[:, 0:2], half, ALU.pow), v)
        yield
        bank = self.side()
        w = [p] + bank.free
        for t in range(2):
            tok = T(lambda e: e.matmul(bank[:, t * P:t * P + P], st[:, t:t + 1].broadcast_to([P, P]),
                                       self.ident[:, :], start=True, stop=True), *w, inc=(t == 1))
        v = V(lambda e: e.scalar_tensor_tensor(o, o, self.gp[:, 4:5], bank[:, 0:256], ALU.mult, ALU.mult), b, tok)
        bank.free = [v]
        v = V(lambda e: e.scalar_tensor_tensor(gg, o, 0.5, gg, ALU.mult, ALU.mult), v, *gg_t)
        self.lane_free[i] = [v]
        done.append(v)

    def run(self):
        A = self.A
        self.start()
        for l in range(L):
            self.ffn1(l, "ffn1", self.to_rms(A["mix_norm"][l]), lambda: self.loads1(l))
            self.mixer1(l, self.to_rms(A["ffn2_norm"][l]))
            last = l == L - 1
            self.ffn1(l, "ffn2", self.to_rms(A["final_norm"] if last else A["ffn1_norm"][l + 1], last),
                      lambda: self.loads2(0) if last else None)
        self.chunk_load()
        for l in range(L):
            self.mixer2(l, self.to_ln(A["ln1_g_2"][l], A["ln1_b_2"][l]))
            last = l == L - 1
            self.ffn2(l, self.to_ln(A["ln2_g_2"][l], A["ln2_b_2"][l], last),
                      lambda: None if last else self.loads2(l + 1))

    def chunk_load(self):
        self.chunk_tok = self.ld("chunk", self.chunk[:, :], self.A["c_chunk"])

    def to_rms(self, vec, final=False):
        g = self.gain_load(vec)

        def after(t):
            x, v = self.rms(t, g, final)
            self.turn_x(t, x, v, scale=final)
        return after

    def to_ln(self, gvec, bvec, last=False):
        g = [self.gain_load(gvec), self.gain_load(bvec)]

        def after(t):
            h, v = self.layer_norm(t, *g)
            if last:
                self.sp.dma(self.out[0, t * P:t * P + P, :], h, self.s_out, 0, v[1])
            else:
                self.turn_x(t, h, v, scale=True)
        return after


_INS = ["x", "ffn1_norm", "ffn1_w_gate", "ffn1_w_up", "ffn1_w_down", "mix_norm", "w_in", "mla_w_uq", "mla_w_ukv",
        "diff_subln", "pool_w", "w_branch", "w_out", "ffn2_norm", "ffn2_w_gate", "ffn2_w_up", "ffn2_w_down",
        "final_norm", "w_in_2", "w_gate_up_2", "gmlp_w_s_2", "w_branch_2", "w_out_2", "ln1_g_2", "ln1_b_2",
        "w_ff1_2", "w_ff2_2", "ln2_g_2", "ln2_b_2"]


def layouts(inp):
    a = {k: np.ascontiguousarray(inp[k]) for k in _INS}
    g = {k: np.asarray(v) for k, v in inp.items()}
    a["gq"] = np.concatenate([g["mla_q_norm"], g["mla_kv_norm"]], 1)
    a["pbs"] = np.concatenate([g["pool_b"].transpose(0, 2, 1),
                               g["pool_scale"].reshape(L, 4, P).transpose(0, 2, 1)], 2)
    a["lams"] = np.stack([g["diff_lambda_q1"], g["diff_lambda_k1"], g["diff_lambda_q2"], g["diff_lambda_k2"]],
                         1).reshape(L * 128)
    a["lng"] = np.stack([g["gmlp_ln_g_2"], g["gmlp_ln_b_2"]], 1)
    a["gp"] = np.concatenate([g["b_gate_2"].reshape(L, 4, P).transpose(0, 2, 1), g["gla_norm_w_2"][:, :, None],
                              g["gmlp_b_s_2"].transpose(0, 2, 1)], 2)
    p1, p2 = g["positions"][0], g["positions_2"][0]
    a["pos_row"] = p1
    a["pos_col"] = np.stack([p1[0:P], p1[P:], p2[0:P], p2[P:]], 1)
    a.update(constants())
    a["c_chunk"] = a["c_tril"][:, P:].astype(np.uint32)
    a["c_tril"] = a["c_tril"][:, :P]
    return {k: np.ascontiguousarray(v) for k, v in a.items()}


def build(nc, A, out):
    with ExitStack() as ctx:
        net = Net(nc, A, out, ctx)
        net.reset(None)
        net.run()
        plan = net.units
        net.reset(plan)
        net.run()
        assert net.units == plan and net.n_split == len(plan)
        block = ctx.enter_context(nc.Block())

        @block.sync
        def _(eng):
            net.sp.issue(eng)
            eng.wait_ge(net.s_out, 32)

        @block.gpsimd
        def _(eng):
            net.pool.issue(eng)

        @block.scalar
        def _(eng):
            net.act.issue(eng)

        @block.vector
        def _(eng):
            net.dve.issue(eng)

        @block.tensor
        def _(eng):
            net.pe.issue(eng)
    return net


def kernel(**inputs):
    import concourse.bacc as _bacc
    from concourse.bass_utils import run_bass_kernel_spmd as _run

    nc = _bacc.Bacc("TRN2", target_bir_lowering=False, num_devices=1)
    arrays, args = {}, {}
    for name, a in layouts(inputs).items():
        arrays[f"in_{name}_dram"] = a
        args[name] = nc.dram_tensor(f"in_{name}_dram", a.shape, mybir.dt.from_np(a.dtype), kind="ExternalInput").ap()
    out = nc.dram_tensor("out_0_dram", (1, S, D), F32, kind="ExternalOutput").ap()
    build(nc, args, out)
    r = _run(nc, [arrays], core_ids=[0])
    return r.results[0]["out_0_dram"]
```

```python
import math
from collections import deque
from contextlib import ExitStack

import numpy as np
import concourse.bass as bass
from concourse import mybir

F32 = mybir.dt.float32
F32R = mybir.dt.float32r
I32 = mybir.dt.int32
U32 = mybir.dt.uint32
ALU = mybir.AluOpType
ACT = mybir.ActivationFunctionType
AXX = mybir.AxisListType.X

P = 128
D = 1024
S = 256
L = 2
FF1 = 2816
FF2 = 4096
IN1 = 5536
IN2 = 7696
EPS = 1e-6
LN_EPS = 1e-5
ALPHA = (2 * L) ** 0.25
BIG = 1e30
TWO_PI = (6.28125, 0.0019350051879882812, 3.0199158306745e-07)
MAGIC = 12582912.0

NL, NH = 6, 5
UCOLS = 2048
STAGGER = 2
NORM_WAIT = 2


class Ops:

    def activation(self, *a, **k):
        return lambda e: e.activation(*a, **k)

    def matmul(self, *a, **k):
        return lambda e: e.matmul(*a, **k)

    def transpose(self, *a, **k):
        return lambda e: e.transpose(*a, **k)

    def memset(self, *a, **k):
        return lambda e: e.memset(*a, **k)

    def tensor_copy(self, *a, **k):
        return lambda e: e.tensor_copy(*a, **k)

    def tensor_tensor(self, *a, **k):
        return lambda e: e.tensor_tensor(*a, **k)

    def tensor_scalar(self, *a, **k):
        return lambda e: e.tensor_scalar(*a, **k)

    def scalar_tensor_tensor(self, *a, **k):
        return lambda e: e.scalar_tensor_tensor(*a, **k)

    def tensor_tensor_scan(self, *a, **k):
        return lambda e: e.tensor_tensor_scan(*a, **k)

    def tensor_reduce(self, *a, **k):
        return lambda e: e.tensor_reduce(*a, **k)

    def reciprocal(self, *a, **k):
        return lambda e: e.reciprocal(*a, **k)

    def copy_predicated(self, *a, **k):
        return lambda e: e.copy_predicated(*a, **k)

    def bn_stats(self, *a, **k):
        return lambda e: e.bn_stats(*a, **k)

    def bn_aggr(self, *a, **k):
        return lambda e: e.bn_aggr(*a, **k)

    def dma_start(self, *a, **k):
        return lambda e: e.dma_start(*a, **k)


OPS = Ops()


class Queue:

    def __init__(self, sem):
        self.sem, self.count, self.items = sem, 0, []

    def put(self, fn, *waits, inc=True):
        self.count += inc
        self.items.append((waits, fn(OPS), self.sem if inc else None, 1))
        return (self.sem, self.count)

    def dma(self, out, in_, sem, value, *waits):
        self.items.append((waits, OPS.dma_start(out, in_), sem, 16))
        return (sem, value)

    def last(self):
        return (self.sem, self.count)

    def issue(self, eng):
        seen = {}
        for waits, ins, sem, by in self.items:
            for s, v in waits:
                if v > seen.get(s.name, 0):
                    eng.wait_ge(s, v)
                    seen[s.name] = v
            r = ins(eng)
            if sem is not None:
                r.then_inc(sem, by)


class Buf:

    def __init__(self, ap):
        self.ap, self.free = ap, []

    def __getitem__(self, k):
        return self.ap[k]


def constants():
    ident = np.eye(P, dtype=np.float32)
    q = np.arange(P)
    mask = np.zeros((P, 384), np.float32)
    mask[:, 0:128] = np.where(np.arange(128)[None] <= q[:, None], 0.0, -BIG)
    mask[:, 128:384] = np.where(np.arange(256)[None] <= q[:, None] + 128, 0.0, -BIG)
    half = np.arange(16, dtype=np.float64)
    f1 = (10000.0 ** (-half / 16)).astype(np.float32)
    f2 = (1.0 / (500000.0 ** (half * (2.0 / 32)))).astype(np.float32)
    freq = np.broadcast_to(np.stack([f1, f1, f2, f2]).reshape(1, 64), (P, 64))
    pool = np.zeros((256, 4, 256), np.float64)
    for g, w in enumerate((2, 4, 8, 16)):
        for t in range(256):
            lo = max(0, t - w + 1)
            pool[lo:t + 1, g, t] += 1.0 / (t + 1 - lo)
            pool[t, g, t] -= 1.0
    pool = pool.astype(np.float32)
    p0 = pool[0:128].reshape(P, 1024)
    p1 = pool[128:256, :, 128:256].reshape(P, 512)
    s = q[:, None]
    t = q[None, :]
    tril = (s <= t).astype(np.float32)
    chunk = ((s <= t) & (s // 64 == t // 64)).astype(np.float32)
    scan = np.broadcast_to((np.arange(S) % 64 != 0).astype(np.float32), (P, S))
    return {
        "c_ident": ident, "c_mask": mask, "c_freq": np.ascontiguousarray(freq),
        "c_pool": np.ascontiguousarray(np.concatenate([p0, p1], 1)),
        "c_tril": np.concatenate([tril, chunk], 1),
        "c_scan": np.ascontiguousarray(scan),
    }


class Turned:

    def __init__(self, name, h, l):
        self.name, self.h, self.l, self.ready, self.used = name, h, l, {}, {}


class Net:
    def __init__(self, nc, A, out, ctx):
        self.nc, self.A, self.out, self.ctx = nc, A, out, ctx
        self.s_eng = [self.sem(n) for n in ("s_pe", "s_act", "s_dve", "s_pool", "s_sp")]
        self.s_raw = [self.sem(f"s_raw{i}") for i in range(NL)]
        self.s_out = self.sem("s_out")
        self.s_ld = {}
        self.memory()

    def reset(self, plan):
        self.plan = plan
        self.units = []
        self.pe, self.act, self.dve, self.pool, self.sp = (Queue(s) for s in self.s_eng)
        for e in self.s_ld.values():
            e[1] = 0
        for b in self.pb + self.gain:
            b.free = []
        self.gain_n = self.n_side = self.n_fetch = self.n_high = self.n_low = 0
        self.high_tok, self.split_tok, self.done_tok = {}, {}, {}
        self.later, self.now = [], []
        self.lanes = [deque() for _ in range(4)]

    def sem(self, name):
        return self.ctx.enter_context(self.nc.semaphore(name))

    def at(self, name, off, shape, dt=F32):
        n = 1
        for x in shape[1:]:
            n *= x
        assert off + 4 * n <= self.top, name
        return self.nc.alloc_sbuf_tensor_at(name, shape, dt, offset=off)

    def memory(self):
        nc = self.nc
        base = (nc.sbuf_base + 63) // 64 * 64
        self.top = nc.sbuf_usable_end
        off = [base]

        def take(nbytes):
            o = off[0]
            off[0] += (nbytes + 31) // 32 * 32
            assert off[0] <= self.top, (off[0], self.top)
            return o

        A = self.at
        self.h = A("h", take(8192), [P, 2, D])
        o_xn = take(8192)
        self.xn = A("xn", o_xn, [P, 2, D])
        self.mT = A("mT", o_xn, [P, 8 * S])
        self.xh = A("xh", take(8192), [P, 8, S], F32R)
        self.xl = A("xl", take(8192), [P, 8, S], F32R)
        o_m = take(24576)
        self.mh = A("mh", o_m, [P, 12, S], F32R)
        self.ml = A("ml", o_m + 12288, [P, 12, S], F32R)
        self.wh = [A(f"wh{i}", take(8192), [P, UCOLS], F32R) for i in range(NH)]
        o_wl = [take(8192) for _ in range(NL)]
        self.raw = [A(f"raw{i}", o_wl[i], [P, UCOLS]) for i in range(NL)]
        self.wl = [A(f"wl{i}", o_wl[i], [P, UCOLS], F32R) for i in range(NL)]
        self.gain = [Buf(A(f"gain{i}", take(4096), [P, D])) for i in range(2)]
        self.ident = A("ident", take(512), [P, P])
        self.ones = A("ones", take(512), [P, P])
        self.mask = A("mask", take(1536), [P, 384])
        o_dist = take(1536)
        self.dist = A("dist", o_dist, [P, 384])
        self.cs = A("cs", take(512), [P, 2, 2, 2, 16])
        self.half_pi = A("half_pi", take(4), [P, 1])
        self.one = A("one", take(4), [P, 1])
        self.nhalf = A("nhalf", take(4), [P, 1])
        self.lam = A("lam", take(8), [P, 2])
        self.bn = A("bn", take(128), [P, 2, 16])
        self.epsc = A("epsc", take(32), [P, 8])
        self.st = A("st", take(256), [P, 64])
        self.ssq = A("ssq", take(64), [P, 2, 8])
        o_ck = take(512)
        o_r = take(0)
        r = [o_r]

        def rt(nbytes):
            o = r[0]
            r[0] += (nbytes + 31) // 32 * 32
            assert r[0] <= self.top, (r[0] - self.top)
            return o

        self.sg = [A(f"sg{t}", rt(2048), [P, 512]) for t in range(2)]
        self.mn = [A(f"mn{t}", rt(2048), [P, 512]) for t in range(2)]
        r[0] = o_r
        o_g = [rt(8192), rt(8192)]
        self.GT = [A(f"G{i}", o_g[i], [P, 8 * S]) for i in range(2)]
        o_lane = [rt(3584) for _ in range(3)]
        self.lS = [[A(f"lS{i}{j}", o_lane[i] + 1536 * j, [P, 384]) for j in range(2)] for i in range(3)]
        self.lQ = [A(f"lQ{i}", o_lane[i] + 1536, [P, 512]) for i in range(3)]
        self.lG = [A(f"lG{i}", o_lane[i], [P, 7, P]) for i in range(3)]
        self.pos_i = A("pos_i", o_lane[1], [P, S], I32)
        self.pos_c = A("pos_c", o_lane[1] + 1024, [P, 4], I32)
        self.pos_f = A("pos_f", o_lane[1] + 1088, [P, 4])
        self.pos_r = A("pos_r", o_lane[1] + 1536, [P, S])
        self.lams = A("lams", o_lane[0], [P, 2 * 128])
        self.lamt = A("lamt", o_lane[0] + 1024, [P, 32])
        self.ang = A("ang", o_lane[2], [P, 64])
        self.angk = A("angk", o_lane[2] + 256, [P, 64])
        self.freq = A("freq", o_lane[2] + 512, [P, 64])
        self.tril = A("tril", o_g[1] + 4096, [P, P])
        self.lane_free = [[] for _ in range(3)]
        self.scan = A("scan", rt(1024), [P, S])
        o_r2 = r[0]
        self.dqT = A("dqT", o_m, [P, 4, S])
        self.dkT = A("dkT", o_m + 4096, [P, 4, S])
        self.dv = A("dv", o_m + 8192, [P, 2, 512])
        self.v = A("v", o_m + 12288, [P, 2, 512])
        self.yph = A("yph", o_m + 16384, [P, 4, S], F32R)
        self.ypl = A("ypl", o_m + 20480, [P, 4, S], F32R)
        self.pin = A("pin", rt(4096), [P, 2, 512])
        o_q = rt(6144)
        self.q = A("q", o_q, [P, 2, 8, 96])
        self.cn = A("cn", o_q, [P, 2, 384])
        o_kt = rt(8192)
        self.kT = A("kT", o_kt, [P, 8, S])
        self.pc = A("pc", o_kt, [P, 1536])
        self.pw = A("pw", o_kt + 6144, [P, 4, P])
        self.rope_tmp = A("rope_tmp", o_xn, [P, 512])
        self.ch = A("ch", o_xn, [P, 3, S], F32R)
        self.cl = A("cl", o_xn + 3072, [P, 3, S], F32R)
        self.pT = A("pT", o_g[1], [P, 4, S])
        self.gq = A("gq", rt(1536), [P, 384])
        self.sub = A("sub", rt(256), [P, 64])
        self.kr = A("kr", rt(768), [P, 2, 96])
        self.pbs = A("pbs", rt(32), [P, 8])
        r[0] = o_r2
        self.gqT = A("gqT", o_m, [P, 4, S])
        self.gkT = A("gkT", o_m + 4096, [P, 4, S])
        self.ggT = A("ggT", o_m + 8192, [P, 4, S])
        self.gv = A("gv", o_m + 12288, [P, 2, 512])
        o_bl, o_be = rt(4096), rt(4096)
        self.bigL = A("bigL", o_bl, [P, 4, S])
        self.bigE = A("bigE", o_be, [P, 4, S])
        self.lng = A("lng", o_bl, [P, 2, 512])
        self.ws = A("ws", o_be, [P, 4, P])
        self.wsT = A("wsT", o_be + 2048, [P, 4, P])
        self.zu = A("zu", o_xn, [P, 2, 512])
        self.zv = A("zv", o_xn + 4096, [P, 2, 512])
        self.mq = A("mq", rt(4096), [P, 2, 4, P])
        self.mk = A("mk", rt(4096), [P, 2, 4, P])
        self.mv = A("mv", rt(4096), [P, 2, 512])
        self.wgu = A("wgu", rt(2048), [P, 512])
        self.gp = A("gp", rt(64), [P, 9])
        self.chunk = A("chunk", o_ck, [P, P], U32)
        self.lrT = A("lrT", o_dist, [P, S])
        self.pb = [Buf(self.ctx.enter_context(nc.psum_tensor(f"pb{i}", [P, 512], F32))) for i in range(8)]
        self.main = [[self.pb[0], self.pb[1]], [self.pb[2], self.pb[3]]]

    def fetch(self, j):
        name, ix, k0, kt, n0, n = self.plan[j]
        src = self.A[name]
        for i in ix:
            src = src[i]
        src = src[k0:k0 + P * kt, n0:n0 + n].rearrange("(k p) n -> p k n", p=P)
        dst = self.raw[j % NL][:, 0:kt * n].rearrange("p (k n) -> p k n", n=n)
        self.sp.dma(dst, src, self.s_raw[j % NL], None, *self.done_tok.get(j - NL, []))

    def split_high(self, j):
        name, ix, k0, kt, n0, n = self.plan[j]
        c = kt * n
        self.high_tok[j] = self.act.put(
            lambda e: e.activation(self.wh[j % NH][:, 0:c], self.raw[j % NL][:, 0:c], ACT.Copy),
            (self.s_raw[j % NL], 16 * (j // NL + 1)), *self.done_tok.get(j - NH, []))

    def split_low(self, j):
        name, ix, k0, kt, n0, n = self.plan[j]
        c = kt * n
        raw, hi, lo = self.raw[j % NL][:, 0:c], self.wh[j % NH][:, 0:c], self.wl[j % NL][:, 0:c]
        a = self.high_tok[j]
        v = self.dve.put(lambda e: e.tensor_tensor(lo, raw, hi.bitcast(F32), ALU.subtract), a)
        self.split_tok[j] = [a, v]

    def advance(self, most=NL):
        if self.plan is None:
            return
        while self.n_fetch < len(self.plan) and (self.n_fetch < NL or self.n_fetch - NL in self.done_tok):
            self.fetch(self.n_fetch)
            self.n_fetch += 1
        while self.n_low < self.n_high:
            self.split_low(self.n_low)
            self.n_low += 1
        while self.n_high < len(self.plan) and (self.n_high < NH or self.n_high - NH in self.done_tok) \
                and self.n_high - self.n_low < most:
            self.split_high(self.n_high)
            self.n_high += 1

    def take(self, key):
        self.units.append(key)
        return len(self.units) - 1

    def weights(self, j):
        _, _, _, kt, _, n = self.plan[j]
        hi, lo = self.wh[j % NH], self.wl[j % NL]
        while j not in self.split_tok:
            self.advance()
        return tuple(w[:, 0:kt * n].rearrange("p (k n) -> p k n", n=n) for w in (hi, lo))

    def pump(self):
        for lane in self.lanes:
            if lane:
                try:
                    next(lane[0])
                except StopIteration:
                    lane.popleft()

    def drain(self, n=None):
        lanes = self.lanes if n is None else [self.lanes[n]]
        while any(lanes):
            for lane in lanes:
                if lane:
                    try:
                        next(lane[0])
                    except StopIteration:
                        lane.popleft()

    def flush(self):
        now, self.now, self.later = self.now, self.later, []
        for f in now:
            f()

    def tick(self):
        self.flush()
        self.pump()
        self.advance()

    def side(self):
        self.n_side += 1
        return self.pb[4 + self.n_side % 4]

    def fence(self):
        return [self.pe.last(), self.act.last(), self.dve.last()]

    def ld(self, key, dst, src, *waits, queue=None):
        if key not in self.s_ld:
            self.s_ld[key] = [self.sem("s_" + key), 0]
        e = self.s_ld[key]
        e[1] += 16
        return (queue or self.pool).dma(dst, src, e[0], e[1], *waits)

    def need(self, X, slots, ts):
        out = []
        for s in slots:
            for t in ts:
                while (s, t) not in X.ready:
                    assert any(self.lanes) or self.now or self.later, (X.name, s, t)
                    self.flush()
                    self.pump()
                out += X.ready[(s, t)]
        return out

    def visits(self, n, apart):
        if apart:
            return [(t, u) for t in range(2) for u in range(n)]
        return [(t, u) for u in range(n) for t in range(2)]

    def group(self, jobs, apart=False):
        idx = [self.take(j["key"]) for j in jobs]
        for t, u in self.visits(len(jobs), apart):
            if self.plan is None:
                tok = self.dry_visit(jobs[u], t)
            else:
                tok = self.visit(idx[u], jobs[u], t)
            if jobs[u]["last"]:
                jobs[u]["epi"](t, tok)
            self.tick()

    def dry_visit(self, job, t):
        for s in job["slots"]:
            job["X"].used[(s, t)] = []
        return (self.pe.sem, 0)

    def visit(self, j, job, t):
        X, slots, segs = job["X"], job["slots"], job["segs"]
        wh, wl = self.weights(j)
        waits = list(self.split_tok[j]) + self.need(X, slots, [t])
        if job["first"]:
            for b, _, _ in segs:
                waits += self.main[t][b].free
        cols = slice(t * P, t * P + P)
        n = 0
        total = len(slots) * len(segs) * 3
        for k, slot in enumerate(slots):
            for x, w in ((X.h, wl), (X.h, wh), (X.l, wh)):
                for b, c0, c1 in segs:
                    n += 1
                    tok = self.pe.put(
                        lambda e, o=self.main[t][b][:, 0:c1 - c0], x=x[:, slot, cols],
                        w=w[:, k, c0:c1], st=(job["first"] and k == 0 and x is X.h and w is wl),
                        sp=(job["last"] and n > total - len(segs)):
                        e.matmul(o, x, w, start=st, stop=sp),
                        *waits, inc=(n == total))
                    waits = []
        for s in slots:
            X.used[(s, t)] = [tok]
        if t == 1:
            self.done_tok[j] = [tok]
        return tok

    def turned_group(self, X, keys, b, epi, base=0, by_bank=False):
        idx = [self.take(k) for k in keys]
        if self.plan is None:
            for i in range(keys[0][5] // 256 if by_bank else 1):
                epi(*([i] if by_bank else []), (self.pe.sem, 0))
            return
        banks = b if isinstance(b, list) else self.pair(b)
        nf = keys[0][5] // P
        kk = base
        for u, j in enumerate(idx):
            kt = keys[u][3]
            wh, wl = self.weights(j)
            slots = list(range(kk, kk + kt))
            waits = list(self.split_tok[j]) + self.need(X, slots, [0, 1])
            for i in range(nf // 2):
                if i:
                    self.tick()
                if u == 0:
                    waits += banks[i].free
                n = 0
                for k in range(kt):
                    for f in (2 * i, 2 * i + 1):
                        o = banks[i][:, (f % 2) * S:(f % 2) * S + S]
                        for m, (w, x) in enumerate(((wl, X.h), (wh, X.h), (wh, X.l))):
                            n += 1
                            tok = self.pe.put(
                                lambda e, o=o, w=w[:, k, f * P:f * P + P], x=x[:, kk + k, :],
                                st=(u == 0 and k == 0 and m == 0 and f % 2 == 0),
                                sp=(u == len(idx) - 1 and k == kt - 1 and m == 2):
                                e.matmul(o, w, x, start=st, stop=sp, skip_group_check=True),
                                *waits, inc=(n == 6 * kt))
                            waits = []
                if u == len(idx) - 1 and by_bank:
                    epi(i, tok)
            for s in slots:
                X.used[(s, 0)] = X.used[(s, 1)] = [tok]
            self.done_tok[j] = [tok]
            if u < len(idx) - 1:
                self.tick()
            kk += kt
        if not by_bank:
            epi(tok)
        self.tick()

    def pair(self, b, side=False):
        return [self.pb[4 + 2 * b], self.pb[5 + 2 * b]] if side else [self.main[0][b], self.main[1][b]]

    def turn(self, X, slot0, t, srcs, *waits):
        n = len(srcs)
        bank = self.side()
        w = list(waits) + bank.free
        for i, s in enumerate(srcs):
            tok = self.pe.put(lambda e, i=i, s=s: e.transpose(bank[:, i * P:i * P + P], s, self.ident[:, :]),
                              *(w if i == 0 else []), inc=(i == n - 1))
        war = [x for i in range(n) for x in X.used.get((slot0 + i, t), [])]
        hi = X.h[:, slot0:slot0 + n, t * P:t * P + P]
        lo = X.l[:, slot0:slot0 + n, t * P:t * P + P]
        src = bank[:, 0:n * P].rearrange("p (k n) -> p k n", n=P)
        a = self.act.put(lambda e: e.activation(hi, src, ACT.Copy), tok, *war)
        v = self.dve.put(lambda e: e.tensor_tensor(lo, src, hi.bitcast(F32), ALU.subtract), a)
        bank.free = [a, v]
        for i in range(n):
            X.ready[(slot0 + i, t)] = [a, v]
        return tok

    def rsqrt(self, out, x, eps, *waits):
        p = self.pool.put(lambda e: e.tensor_scalar(out, x, eps, None, ALU.add), *waits)
        half = self.nhalf[:, :].broadcast_to([P, out.shape[1]])
        return self.pool.put(lambda e: e.tensor_tensor(out, out, half, ALU.pow), p, self.memset_tok)

    def gain_load(self, vec):
        g = self.gain[self.gain_n % 2]
        self.gain_n += 1
        tok = self.ld(f"gain{(self.gain_n - 1) % 2}", g[:, :], vec.partition_broadcast(P), *g.free)
        return g, tok

    def add(self, t, b, tok, coef=0.5):
        o = self.h[:, t, b * 512:b * 512 + 512]
        v = self.dve.put(lambda e: e.scalar_tensor_tensor(o, self.main[t][b][:, :], coef, o, ALU.mult, ALU.add),
                         tok, *self.h_tok[t])
        self.main[t][b].free = [v]
        self.h_half[t, b] = [v]
        if b:
            self.h_tok[t] = self.h_half[t, 0] + [v]

    def rms_half(self, t, b):
        c = slice(512 * b, 512 * b + 512)
        self.sq_tok[t, b] = self.act.put(
            lambda e: e.activation(self.xn[:, t, c], self.h[:, t, c], ACT.Square, scale=1.0 / 32,
                                   accum_out=self.st[:, 48 + 4 * t + b:49 + 4 * t + b]),
            *self.h_half[t, b], *self.xn_free[t])

    def rms(self, t, gain, final=False):
        g, gt = gain
        ms, rs = self.st[:, 48 + 4 * t:50 + 4 * t], self.st[:, 50 + 4 * t:51 + 4 * t]
        x, h = self.xn[:, t, :], self.h[:, t, :]
        v = self.pool.put(lambda e: e.tensor_scalar(rs, ms[:, 0:1], ms[:, 1:2], EPS, ALU.add, ALU.add),
                          self.sq_tok[t, 0], self.sq_tok[t, 1])
        v = self.pool.put(lambda e: e.tensor_tensor(rs, rs, self.nhalf[:, :], ALU.pow), v, self.memset_tok)
        o = h if final else x
        halves = []
        for i in range(2):
            c = slice(512 * i, 512 * i + 512)
            halves.append(self.dve.put(lambda e: e.scalar_tensor_tensor(o[:, c], h[:, c], rs, g[:, c], ALU.mult,
                                                                        ALU.mult), v, gt))
        v = halves[1]
        g.free = g.free + [v] if t else [v]
        self.xn_free[t] = [v]
        if final:
            self.h_tok[t] = [v]
        return o, halves

    def ln_half(self, t, b):
        self.sq_tok[t, b] = self.dve.put(
            lambda e: e.bn_stats(self.bn[:, t, 6 * b:6 * b + 6], self.h[:, t, 512 * b:512 * b + 512]),
            *self.h_half[t, b])

    def layer_norm(self, t, gg, gb):
        mv = self.bn[:, t, 12:14]
        rs = self.bn[:, t, 14:15]
        h = self.h[:, t, :]
        v = self.dve.put(lambda e: e.bn_aggr(mv, self.bn[:, t, 0:12]), self.sq_tok[t, 0], self.sq_tok[t, 1])
        v = self.rsqrt(rs, mv[:, 1:2], LN_EPS, v)
        shift = self.bn[:, t, 15:16]
        v = self.pool.put(lambda e: e.tensor_scalar(shift, mv[:, 0:1], rs, -1.0, ALU.mult, ALU.mult), v)
        halves = []
        for i in range(2):
            c = slice(512 * i, 512 * i + 512)
            w = self.act.put(lambda e: e.activation(h[:, c], h[:, c], ACT.Identity, bias=shift, scale=rs), v)
            w = self.dve.put(lambda e: e.tensor_tensor(h[:, c], h[:, c], gg[0][:, c], ALU.mult), w, gg[1])
            gg[0].free = gg[0].free + [w] if t or i else [w]
            w = self.dve.put(lambda e: e.tensor_tensor(h[:, c], h[:, c], gb[0][:, c], ALU.add), w, gb[1])
            gb[0].free = gb[0].free + [w] if t or i else [w]
            halves.append(w)
        self.h_tok[t] = [w]
        return h, halves

    def turn_x(self, t, x, v, wait=3, scale=False):
        def gen():
            for _ in range(wait):
                yield
            for half in range(2):
                tok = self.turn(self.X, 4 * half, t, [x[:, (4 * half + i) * P:(4 * half + i + 1) * P]
                                                      for i in range(4)], v[half])
            if not scale:
                self.xn_free[t] = [tok]
            if scale:
                h = self.h[:, t, :]
                a = self.act.put(lambda e: e.activation(h, h, ACT.Copy, scale=ALPHA), tok, *self.h_tok[t])
                self.h_tok[t] = [a]
        for i in range(8):
            self.X.ready.pop((i, t), None)
        self.lanes[3 if t else 0].append(gen())

    def down(self, name, ix, k0, n_units, sizes, coef, after):
        def epi(t, tok):
            for b in range(2):
                self.add(t, b, tok, coef)

        def half_epi(b):
            def f(t, tok):
                self.add(t, b, tok, coef)
                after(t, b)
            return f
        u = 0
        for size in sizes:
            first, last = u == 0, u + size == n_units
            if last and after:
                self.group([dict(key=(name, ix, k0 + (2 * u + 4 * i) * P, 4, 512 * b, 512), X=self.M,
                                 slots=[2 * u + 4 * i + k for k in range(4)], segs=[(b, 0, 512)],
                                 first=first and i == 0, last=(i == size // 2 - 1), epi=half_epi(b))
                            for b in range(2) for i in range(size // 2)], apart=True)
            else:
                self.group([dict(key=(name, ix, k0 + 2 * (u + i) * P, 2, 0, D), X=self.M,
                                 slots=[2 * (u + i), 2 * (u + i) + 1], segs=[(0, 0, 512), (1, 512, 1024)],
                                 first=first and i == 0, last=last and i == size - 1, epi=epi)
                            for i in range(size)])
            u += size
        assert u == n_units

    def ffn1(self, l, pre, after, loads):
        self.mix_to_ffn()
        self.loads = loads()
        gate, up, dn = pre + "_w_gate", pre + "_w_up", pre + "_w_down"
        for n0, chunks, sizes in ((0, (512, 512, 512), (2, 4)), (1536, (512, 512, 256), (1, 4))):
            self.M.ready.clear()
            slot = 0
            c0 = n0
            for n in chunks:
                if c0 > 0:
                    parts = [(0, 4), (4, 4)] if n == 512 else [(0, 8)]
                    for b, name in ((0, gate), (1, up)):
                        banks = self.pair(b, c0 > 512)
                        self.turned_group(self.X, [(name, (l,), k * P, kt, c0, n) for k, kt in parts], banks,
                                          self.silu_t(banks) if b == 0 else self.up_t(banks, slot), by_bank=True)
                else:
                    kt = 4
                    self.group([dict(key=(name, (l,), k * P, kt, c0, n), X=self.X, slots=list(range(k, k + kt)),
                                     segs=[(b, 0, n)], first=(k == 0), last=(k == 8 - kt),
                                     epi=self.silu_epi(n) if b == 0 else self.up_epi(n, slot))
                                for b, name in ((0, gate), (1, up)) for k in range(0, 8, kt)], apart=True)
                slot += n // P
                c0 += n
            half2 = n0 > 0
            self.down(dn, (l,), n0, sum(chunks) // 256, sizes, 0.5, after if half2 else None)

    def silu_t(self, banks):
        def epi(i, tok):
            a = self.act.put(lambda e: e.activation(self.sg[i][:, :], banks[i][:, :], ACT.Silu), tok,
                             *self.sg_free[i])
            banks[i].free = [a]
            self.sg_tok[i] = a
        return epi

    def up_t(self, banks, slot):
        def epi(i, tok):
            v = self.dve.put(lambda e: e.tensor_tensor(self.mn[i][:, :], banks[i][:, :], self.sg[i][:, :],
                                                       ALU.mult), tok, self.sg_tok[i], *self.mn_free[i])
            banks[i].free = [v]
            self.sg_free[i] = [v]
            self.mn_free[i] = []
            self.split_into(self.M, slot + 2 * i, self.mn[i][:, :], self.mn_free[i], v)
        return epi

    def relu_t(self, banks, slot):
        def epi(i, tok):
            a = self.act.put(lambda e: e.activation(self.sg[i][:, :], banks[i][:, :], ACT.Relu), tok,
                             *self.sg_free[i])
            v = self.dve.put(lambda e: e.scalar_tensor_tensor(self.mn[i][:, :], banks[i][:, :], 0.0,
                                                              self.sg[i][:, :], ALU.max, ALU.mult),
                             a, *self.mn_free[i])
            banks[i].free = [v]
            self.sg_free[i] = [v]
            self.mn_free[i] = []
            self.split_into(self.M, slot + 2 * i, self.mn[i][:, :], self.mn_free[i], v)
        return epi

    def silu_epi(self, n):
        def epi(t, tok):
            bank = self.main[t][0]
            a = self.act.put(lambda e: e.activation(self.sg[t][:, 0:n], bank[:, 0:n], ACT.Silu),
                             tok, *self.sg_free[t])
            bank.free = [a]
            self.sg_tok[t] = a
        return epi

    def up_epi(self, n, slot):
        def epi(t, tok):
            bank = self.main[t][1]
            v = self.dve.put(lambda e: e.tensor_tensor(self.mn[t][:, 0:n], bank[:, 0:n], self.sg[t][:, 0:n],
                                                       ALU.mult), tok, self.sg_tok[t], *self.mn_free[t])
            bank.free = [v]
            self.sg_free[t] = [v]
            self.later_turn(t, n, slot, v)
        return epi

    def later_turn(self, t, n, slot, v):
        def gen():
            yield
            tok = self.turn(self.M, slot, t, [self.mn[t][:, i * P:i * P + P] for i in range(n // P)], v)
            self.mn_free[t] = [tok]
        g = gen()
        self.lanes[1 + t].append(g)

    def ffn2(self, l, after, loads):
        self.mix_to_ffn()
        self.loads = loads()
        n_t = 0
        for n0, n_chunks, sizes in ((0, 3, (2, 4)), (1536, 2, (2, 2)), (2560, 3, (2, 4))):
            self.M.ready.clear()
            first = 2 if n0 == 0 else 0
            if first:
                self.group([dict(key=("w_ff1_2", (l,), 512 * i, 4, 512 * c, 512), X=self.X,
                                 slots=list(range(4 * i, 4 * i + 4)), segs=[(c, 0, 512)], first=(i == 0),
                                 last=(i == 1), epi=self.relu_epi(c, 4 * c)) for c in range(2) for i in range(2)],
                           apart=True)
            for c in range(first, n_chunks):
                banks = self.pair(n_t % 2, n_t > 0)
                n_t += 1
                self.turned_group(self.X, [("w_ff1_2", (l,), 512 * i, 4, n0 + 512 * c, 512) for i in range(2)],
                                  banks, self.relu_t(banks, 4 * c), by_bank=True)
            end = n0 == 2560
            self.down("w_ff2_2", (l,), n0, n_chunks * 2, sizes, 1.0, after if end else None)

    def relu_epi(self, b, slot):
        def epi(t, tok):
            bank = self.main[t][b]
            a = self.act.put(lambda e: e.activation(self.sg[t][:, :], bank[:, :], ACT.Relu),
                             tok, *self.sg_free[t])
            v = self.dve.put(lambda e: e.scalar_tensor_tensor(self.mn[t][:, :], bank[:, :], 0.0, self.sg[t][:, :],
                                                              ALU.max, ALU.mult), a, *self.mn_free[t])
            bank.free = [v]
            self.sg_free[t] = [v]
            self.later_turn(t, 512, slot, v)
        return epi

    def mix_to_ffn(self):
        f = self.ffn_fence = self.fence()
        self.sg_free, self.sg_tok = [list(f), list(f)], {}
        self.mn_free = [list(f), list(f)]
        for s in range(12):
            for t in range(2):
                self.M.used[(s, t)] = list(f)

    def start(self):
        A = self.A
        x = A["x"]
        self.xn_free = [[], []]
        self.X = Turned("X", self.xh, self.xl)
        self.M = Turned("M", self.mh, self.ml)
        self.lane_free = [[], [], []]
        V, C = self.dve.put, self.act.put
        load_x = lambda t: [self.ld(f"x{t}", self.h[:, t, :], x[0, t * P:t * P + P, :], queue=self.sp)]
        self.h_tok = [load_x(0)]
        g = self.gain_load(A["ffn1_norm"][0])
        k_ident = self.ld("ident", self.ident[:, :], A["c_ident"], queue=self.sp)
        if self.plan is not None:
            self.fetch(0)
            self.n_fetch = 1
        self.h_tok.append(load_x(1))
        self.advance(0)
        self.memset_tok = self.pool.put(lambda e: e.memset(self.nhalf[:, :], -0.5))
        self.pe.put(lambda e: e.transpose(self.pb[4][:, 0:P], self.ident[:, :], self.ident[:, :]), k_ident)
        self.h_half = {(t, b): self.h_tok[t] for t in range(2) for b in range(2)}
        self.sq_tok = {}
        for b in range(2):
            self.rms_half(0, b)
        x0, v0 = self.rms(0, g)
        self.turn_x(0, x0, v0, 0)
        self.drain()
        self.advance(1)
        for b in range(2):
            self.rms_half(1, b)
        self.advance(1)
        x1, v1 = self.rms(1, g)
        self.turn_x(1, x1, v1, 2)
        k = [self.ld("const", d, s) for d, s in (
            (self.mask[:, :], A["c_mask"]), (self.freq[:, :], A["c_freq"]),
            (self.pos_i[:, :], A["pos_row"].partition_broadcast(P)), (self.pos_c[:, :], A["pos_col"]),
            (self.lams[:, :], A["lams"].partition_broadcast(P)), (self.scan[:, :], A["c_scan"]))][-1]
        m = self.pool.put(lambda e: e.memset(self.ones[:, :], 1.0 / P))
        m = self.pool.put(lambda e: e.memset(self.half_pi[:, :], math.pi / 2))
        m = self.pool.put(lambda e: e.memset(self.one[:, :], 1.0))
        m = self.pool.put(lambda e: e.memset(self.kr[:, :, 0:64], 0.0))
        self.memset_tok = m
        self.lanes[0].append(self.tables(k))

    def tables(self, k):
        V, C = self.dve.put, self.act.put
        for _ in range(4):
            yield
        a = V(lambda e: e.tensor_copy(self.pos_f[:, :], self.pos_c[:, :]), k)
        b = V(lambda e: e.tensor_copy(self.pos_r[:, :], self.pos_i[:, :]), k)
        d0, d1 = self.dist[:, 0:128], self.dist[:, 128:384]
        a = V(lambda e: e.tensor_scalar(d0, self.pos_r[:, 0:128], self.pos_f[:, 0:1], None,
                                        ALU.subtract), a, b)
        a = V(lambda e: e.tensor_scalar(d1, self.pos_r[:, :], self.pos_f[:, 1:2], None,
                                        ALU.subtract), a)
        yield
        a = C(lambda e: e.activation(self.dist[:, :], self.dist[:, :], ACT.Abs), a)
        yield
        a = V(lambda e: e.scalar_tensor_tensor(self.dist[:, :], self.mask[:, :], -1e4, self.dist[:, :],
                                               ALU.mult, ALU.add), a)
        yield
        for i in range(4):
            a = V(lambda e, i=i: e.tensor_scalar(self.ang[:, 16 * i:16 * i + 16], self.freq[:, 16 * i:16 * i + 16],
                                                 self.pos_f[:, i:i + 1], None, ALU.mult), a)
        a = V(lambda e: e.tensor_scalar(self.angk[:, :], self.ang[:, :], 1 / (2 * math.pi), MAGIC, ALU.mult,
                                        ALU.add), a)
        a = V(lambda e: e.tensor_scalar(self.angk[:, :], self.angk[:, :], MAGIC, None, ALU.subtract), a)
        yield
        for c in TWO_PI:
            a = V(lambda e, c=c: e.scalar_tensor_tensor(self.ang[:, :], self.angk[:, :], -c, self.ang[:, :],
                                                        ALU.mult, ALU.add), a)
        lim = 3.1415925
        a = V(lambda e: e.tensor_scalar(self.ang[:, :], self.ang[:, :], lim, -lim, ALU.min, ALU.max), a)
        yield
        b = C(lambda e: e.activation(self.angk[:, :], self.ang[:, :], ACT.Abs), a)
        cs = self.cs[:, :, :, :, :].rearrange("p a b t k -> p a (b t k)")
        C(lambda e: e.activation(cs[:, 0, :], self.angk[:, :], ACT.Sin, bias=self.half_pi[:, :], scale=-1.0),
          b, self.memset_tok)
        self.rope_tok = C(lambda e: e.activation(cs[:, 1, :], self.ang[:, :], ACT.Sin), a)
        yield
        v = k
        for l in range(L):
            o = 128 * l
            for i in range(2):
                q, kk = self.lams[:, o + 64 * i:o + 64 * i + 32], self.lams[:, o + 64 * i + 32:o + 64 * i + 64]
                v = V(lambda e, q=q, kk=kk: e.tensor_tensor(self.lamt[:, :], q, kk, ALU.mult), v)
                v = V(lambda e, c=2 * l + i: e.tensor_reduce(self.epsc[:, c:c + 1], self.lamt[:, :], AXX, ALU.add), v)
            yield
        a = C(lambda e: e.activation(self.epsc[:, 4:8], self.epsc[:, 0:4], ACT.Exp), v)
        yield
        for l in range(L):
            li = 0.8 - 0.6 * math.exp(-0.3 * l)
            c = 4 + 2 * l
            v = V(lambda e, l=l, c=c: e.tensor_tensor(self.lam[:, l:l + 1], self.epsc[:, c + 1:c + 2],
                                                      self.epsc[:, c:c + 1], ALU.subtract), a)
            v = V(lambda e, l=l, li=li: e.tensor_scalar(self.lam[:, l:l + 1], self.lam[:, l:l + 1], -li, None,
                                                        ALU.add), v)
        self.lam_tok = v

    def rope(self, kind, x, heads, w, o, tmp, *waits):
        V = self.dve.put
        x1, x2 = x[:, :, :, o:o + 16], x[:, :, :, o + 16:o + 32]
        cos = self.cs[:, 0, kind, :, :].unsqueeze(2).broadcast_to([P, 2, heads, 16])
        sin = self.cs[:, 1, kind, :, :].unsqueeze(2).broadcast_to([P, 2, heads, 16])
        n = 2 * heads * 16
        t = [tmp[:, i * n:(i + 1) * n].rearrange("p (a b c) -> p a b c", a=2, b=heads) for i in range(2)]
        v = V(lambda e: e.tensor_tensor(t[0], x1, sin, ALU.mult), self.rope_tok, *waits)
        v = V(lambda e: e.tensor_tensor(t[1], x2, sin, ALU.mult), v)
        v = V(lambda e: e.tensor_tensor(x1, x1, cos, ALU.mult), v)
        v = V(lambda e: e.tensor_tensor(x2, x2, cos, ALU.mult), v)
        v = V(lambda e: e.tensor_tensor(x1, x1, t[1], ALU.subtract), v)
        v = V(lambda e: e.tensor_tensor(x2, x2, t[0], ALU.add), v)
        return v

    def scores(self, q, k, *waits):
        bank = self.side()
        self.pe.put(lambda e: e.matmul(bank[:, 0:128], q[0], k(128), start=True, stop=True), *waits, *bank.free,
                    inc=False)
        return bank, self.pe.put(lambda e: e.matmul(bank[:, 128:384], q[1], k(256), start=True, stop=True))

    def exps(self, Sb, st, c, scale, v):
        parts = (Sb[:, 0:128], Sb[:, 128:384])
        for i, p in enumerate(parts):
            r = self.dve.put(lambda e, i=i, p=p: e.tensor_reduce(st[:, c + i:c + i + 1], p, AXX, ALU.max), v)
        r = self.dve.put(lambda e: e.tensor_scalar(st[:, c:c + 2], st[:, c:c + 2], -scale, None, ALU.mult), r)
        for i, p in enumerate(parts):
            a = self.act.put(lambda e, i=i, p=p: e.activation(p, p, ACT.Exp, bias=st[:, c + i:c + i + 1], scale=scale,
                                                              accum_out=st[:, c + 4 + i:c + 5 + i]), r)
        return a

    def turn_probs(self, Sb, PT, v, *war):
        bank = self.side()
        for i in range(3):
            tok = self.pe.put(lambda e, i=i: e.transpose(bank[:, i * P:i * P + P], Sb[:, i * P:i * P + P],
                                                         self.ident[:, :]),
                              *([v] + bank.free if i == 0 else []), inc=(i == 2))
        a = self.act.put(lambda e: e.activation(PT[:, 0:384], bank[:, 0:384], ACT.Copy), tok, *war)
        bank.free = [a]
        return a

    def weigh(self, PT, v, n, outs, r, rt, a, squares=None):
        bank = self.side()
        self.pe.put(lambda e: e.matmul(bank[:, 0:n], PT[:, 0:128], v[0], start=True, stop=True), *a, *bank.free,
                    inc=False)
        self.pe.put(lambda e: e.matmul(bank[:, n:2 * n], PT[:, 128:256], v[0], start=True, stop=False), inc=False)
        tok = self.pe.put(lambda e: e.matmul(bank[:, n:2 * n], PT[:, 256:384], v[1], start=False, stop=True))
        for t in range(2):
            d = self.act.put(lambda e, t=t: e.activation(outs[t], bank[:, t * n:t * n + n], ACT.Copy,
                                                         scale=r[:, t:t + 1]), tok, *rt)
            if squares:
                d = self.act.put(lambda e, t=t: e.activation(PT[:, t * n:t * n + n], bank[:, t * n:t * n + n],
                                                             ACT.Square, scale=r[:, t:t + 1],
                                                             accum_out=squares[t]))
        bank.free = [d]
        return d

    def diff_head(self, i, l, h):
        st = self.st[:, 16 * i:16 * i + 16]
        S0, S1 = self.lS[i]
        scale = 32 ** -0.5
        slope = 2.0 ** -(h + 1)
        f, o = h // 2, 64 * (h % 2)
        V = self.dve.put
        for m, Sb in enumerate((S0, S1)):
            p = o + 32 * m
            bank, tok = self.scores(
                [self.dqT[p:p + 32, f, t * P:t * P + P] for t in range(2)],
                lambda n, p=p: self.dkT[p:p + 32, f, 0:n], *self.dqk_tok)
            v = V(lambda e, Sb=Sb, bank=bank: e.scalar_tensor_tensor(
                Sb[:, :], self.dist[:, :], -slope / scale, bank[:, 0:384], ALU.mult, ALU.add),
                tok, *self.lane_free[i])
            bank.free = [v]
            a = self.exps(Sb, st, 2 * m, scale, v)
            yield
        v = V(lambda e: e.reciprocal(st[:, 8:12], st[:, 4:8]), a)
        v = V(lambda e: e.scalar_tensor_tensor(st[:, 12:14], st[:, 4:6], self.lam[:, l:l + 1], st[:, 10:12],
                                               ALU.mult, ALU.mult), v, self.lam_tok)
        for t, (c0, c1) in enumerate(((0, 128), (128, 384))):
            w = V(lambda e, t=t, c0=c0, c1=c1: e.scalar_tensor_tensor(
                S0[:, c0:c1], S1[:, c0:c1], st[:, 12 + t:13 + t], S0[:, c0:c1], ALU.mult, ALU.add), v)
        yield
        yield
        a = self.turn_probs(S0, S1, w)
        yield
        yield
        while not self.pin_free or len(self.dv_toks) < 2:
            yield
        hs = slice(64 * h, 64 * h + 64)
        v = self.weigh(S1, [self.dv[:, t, hs] for t in range(2)], 64, [self.pin[:, t, hs] for t in range(2)],
                       st[:, 8:10], [w] + self.pin_free, [a] + self.dv_toks,
                       [self.ssq[:, t, h:h + 1] for t in range(2)])
        self.lane_free[i] = [v]
        self.diff_done.append(v)

    def plain_head(self, i, scale, turn_q, k, v, n, outs, done, turned=None, h=0):
        st = self.st[:, 16 * i:16 * i + 16]
        Sb, PT = self.lS[i]
        Q = self.lQ[i]
        bank = self.side()
        for j, x in enumerate(turn_q):
            w = x.shape[1]
            tok = self.pe.put(lambda e, j=j, x=x, w=w: e.transpose(bank[0:w, j * P:j * P + P], x, self.ident[:, :]),
                              *(self.qk_tok + bank.free if j == 0 else []), inc=(j == len(turn_q) - 1))
        if turned is not None:
            turned[h] = tok
        c = len(turn_q) * P
        a = self.act.put(lambda e: e.activation(Q[0:w, 0:c], bank[0:w, 0:c], ACT.Copy), tok, *self.lane_free[i])
        bank.free = [a]
        yield
        bank, tok = self.scores([Q[0:w, 0:P], Q[0:w, P:2 * P]], k, a, *self.qk_tok)
        d = self.dve.put(lambda e: e.tensor_tensor(Sb[:, :], bank[:, 0:384], self.mask[:, :], ALU.add), tok,
                         *self.lane_free[i])
        bank.free = [d]
        a = self.exps(Sb, st, 0, scale, d)
        r = self.dve.put(lambda e: e.reciprocal(st[:, 8:10], st[:, 4:6]), a)
        yield
        yield
        b = self.turn_probs(Sb, PT, a, tok)
        yield
        yield
        while turned is not None and len([x for x in turned if x < h]) < h:
            yield
        war = list(turned.values()) if turned is not None else [tok]
        d = self.weigh(PT, v, n, outs, st[:, 8:10], [r] + war, [b])
        self.lane_free[i] = [d]
        done.append(d)

    def gates(self, name, l, c0, slot):
        for j in range(2):
            def epi(i, tok, j=j):
                bank = self.main[i][j]
                f = 4 * j + 2 * i
                a = self.act.put(lambda e: e.activation(self.GT[slot][:, f * S:(f + 2) * S], bank[:, :],
                                                        ACT.Tanh, scale=0.5), tok, *self.g_free[slot])
                bank.free = [a]
                self.g_tok[slot, i, j] = a
            self.turned_group(self.X, [(name, (l,), 512 * i, 4, c0 + 512 * j, 512) for i in range(2)], j, epi,
                              by_bank=True)

    def branch(self, name, l, n, Y, base, slot, first, last):
        self.g_free[slot] = []
        ends = []

        def epi(j):
            def f(i, tok):
                bank = self.main[i][j]
                f = 4 * j + 2 * i
                G = self.GT[slot][:, f * S:(f + 2) * S]
                m = self.mT[:, f * S:(f + 2) * S]
                o = m if first else G
                v = self.dve.put(lambda e: e.scalar_tensor_tensor(o, G, 1.0, bank[:, :], ALU.add, ALU.mult),
                                 tok, self.g_tok[slot, i, j], *(self.m_free if first else []))
                bank.free = [v]
                if not first:
                    v = self.dve.put(lambda e: e.tensor_tensor(m, m, G, ALU.add), v, *self.m_tok[i, j])
                self.m_tok[i, j] = [v]
                self.g_free[slot].append(v)
                if last:
                    self.split_into(self.M, f, m, ends, v)
            return f
        for j in range(2):
            self.turned_group(Y, [(name, (l, n), 0, 4, 512 * j, 512)], j, epi(j), base, by_bank=True)
        if last:
            self.xn_free = [ends, ends]

    def split_into(self, X, slot, src, read, *waits):
        hi = X.h[:, slot:slot + 2, :].rearrange("p a s -> p (a s)")
        lo = X.l[:, slot:slot + 2, :].rearrange("p a s -> p (a s)")
        ks = [(s, t) for s in (slot, slot + 1) for t in range(2)]
        war = [x for k in ks for x in X.used.get(k, [])]
        a = self.act.put(lambda e: e.activation(hi, src, ACT.Copy), *waits, *war)

        def low():
            v = self.dve.put(lambda e: e.tensor_tensor(lo, src, hi.bitcast(F32), ALU.subtract), a)
            for k in ks:
                X.ready[k] = [a, v]
            read.extend([a, v])
        self.later.append(low)

    def way_out(self, name, l, after):
        def epi(b):
            def f(t, tok):
                self.add(t, b, tok)
                after(t, b)
            return f
        self.group([dict(key=(name, (l,), 512 * i, 4, 512 * b, 512), X=self.M, slots=list(range(4 * i, 4 * i + 4)),
                         segs=[(b, 0, 512)], first=(i == 0), last=(i == 1), epi=epi(b))
                    for i, b in ((0, 0), (0, 1), (1, 0), (1, 1))], apart=True)

    def merged_ready(self):
        f = self.fence()
        self.M.ready.clear()
        for s in range(8):
            for t in range(2):
                self.M.used[(s, t)] = list(f)

    def copy_epi(self, dst, b, n=512, toks=None, func=ACT.Copy):
        def epi(t, tok):
            bank = self.main[t][b]
            a = self.act.put(lambda e: e.activation(dst(t), bank[:, 0:n], func), tok, *self.r_free)
            bank.free = [a]
            toks.append(a)
        return epi

    def cols(self, name, l, c0, b, epi, n=512):
        return [dict(key=(name, (l,), 512 * i, 4, c0, n), X=self.X, slots=list(range(4 * i, 4 * i + 4)),
                     segs=[(b, 0, n)], first=(i == 0), last=(i == 1), epi=epi) for i in range(2)]

    def loads1(self, l):
        A, f = self.A, self.ffn_fence
        return (self.ld("gq", self.gq[:, :], A["gq"][l].partition_broadcast(P), *f),
                self.ld("sub", self.sub[:, :], A["diff_subln"][l].partition_broadcast(P), *f),
                [self.ld("pc", self.pc[:, :], A["c_pool"], *f)],
                [self.ld("pw", self.pw[:, :, :], A["pool_w"][l].rearrange("g c d -> c g d"), *f),
                 self.ld("pbs", self.pbs[:, :], A["pbs"][l], *f)])

    def mixer1(self, l, after):
        A, V, C, T = self.A, self.dve.put, self.act.put, self.pe.put
        f = self.fence()
        self.r_free = f
        self.g_free, self.g_tok, self.m_tok = [list(f), list(f)], {}, {}
        self.lane_free = [list(f) for _ in range(3)]
        self.diff_done, self.mla_done = [], []
        W = "w_in"
        k_gq, k_sub, k_pc, k_pw = self.loads
        C1 = Turned("C", self.ch, self.cl)
        for s in range(3):
            for t in range(2):
                C1.used[(s, t)] = list(f)
        kr_toks, pin_toks, self.dv_toks, self.pin_free = [], [], [], []

        def c_epi(t, tok):
            bank = self.main[t][0]
            ms = self.bn[:, t, 0:2]
            rs = self.bn[:, t, 2:4]
            tmp = self.lQ[t]
            a = C(lambda e: e.activation(tmp[:, 0:256], bank[:, 0:256], ACT.Square, scale=1 / 16,
                                         accum_out=ms[:, 0:1]), tok, *self.lane_free[t])
            a = C(lambda e: e.activation(tmp[:, 256:384], bank[:, 256:384], ACT.Square, scale=128 ** -0.5,
                                         accum_out=ms[:, 1:2]))
            b = C(lambda e: e.activation(self.kr[:, t, 64:96], bank[:, 384:416], ACT.Copy), *self.r_free)
            v = self.rsqrt(rs, ms, EPS, a)
            kr_toks.append(b)

            def gen():
                yield
                for i, (c0, c1) in enumerate(((0, 256), (256, 384))):
                    d = V(lambda e, i=i, c0=c0, c1=c1: e.scalar_tensor_tensor(
                        self.cn[:, t, c0:c1], bank[:, c0:c1], rs[:, i:i + 1], self.gq[:, c0:c1], ALU.mult, ALU.mult),
                        v, b, k_gq, *f)
                bank.free = [d, b]
                c_scaled.append(t)
                yield
                while (7, 1) not in self.X.ready or (7, 0) not in self.X.ready:
                    yield
                yield
                for s in range(3):
                    C1.used[(s, t)] = f + self.xn_free[0] + self.xn_free[1]
                self.turn(C1, 0, t, [self.cn[:, t, i * P:i * P + P] for i in range(3)], d)
            self.lanes[t].append(gen())
            self.lane_free[t] = [a]

        c_scaled = []
        self.group(self.cols(W, l, 0, 0, c_epi, 416) +
                   self.cols(W, l, 1952, 1, self.copy_epi(lambda t: self.pin[:, t, :], 1, 512, pin_toks)), apart=True)
        while len(c_scaled) < 2:
            self.pump()

        def qk_epi(dst, b, toks):
            def epi(tok):
                for i in range(2):
                    bank = self.main[i][b]
                    o = dst[:, 2 * i:2 * i + 2, :].rearrange("p a s -> p (a s)")
                    a = C(lambda e, o=o, bank=bank: e.activation(o, bank[:, :], ACT.Copy), tok, *f)
                    bank.free = [a]
                    toks.append(a)
            return epi
        Yp = Turned("Yp", self.yph, self.ypl)
        pool_done = []

        def pool():
            yield
            yield
            for i in range(2):
                bank = self.side()
                for g in (2 * i, 2 * i + 1):
                    o = (g % 2) * S
                    gs = slice(g * P, g * P + P)
                    T(lambda e, g=g, o=o, gs=gs, bank=bank: e.matmul(
                        bank[:, o:o + 256], self.pin[:, 0, gs], self.pc[:, 256 * g:256 * g + 256],
                        start=True, stop=False, skip_group_check=True), *pin_toks, *k_pc,
                        *(bank.free if g % 2 == 0 else []), inc=False)
                    tok = T(lambda e, g=g, o=o, gs=gs, bank=bank: e.matmul(
                        bank[:, o + 128:o + 256], self.pin[:, 1, gs], self.pc[:, 1024 + P * g:1024 + P * g + P],
                        start=False, stop=True, skip_group_check=True))
                a = C(lambda e, i=i, bank=bank: e.activation(
                    self.pT[:, 2 * i:2 * i + 2, :].rearrange("p a s -> p (a s)"), bank[:, :], ACT.Copy), tok, *f)
                bank.free = [a]
                yield
            self.pin_free = [tok]
            for i in range(2):
                bank = self.side()
                for g in (2 * i, 2 * i + 1):
                    o = (g % 2) * S
                    tok = T(lambda e, g=g, o=o, bank=bank: e.matmul(
                        bank[:, o:o + 256], self.pw[:, g, :], self.pT[:, g, :], start=True, stop=True), a, *k_pw,
                        *(bank.free if g % 2 == 0 else []))
                for g in (2 * i, 2 * i + 1):
                    o = (g % 2) * S
                    v = V(lambda e, g=g, o=o, bank=bank: e.tensor_scalar(
                        self.pT[:, g, :], bank[:, o:o + 256], self.pbs[:, g:g + 1], self.pbs[:, 4 + g:5 + g],
                        ALU.add, ALU.mult), tok)
                bank.free = [v]
                yield
            pT = self.pT[:, :, :].rearrange("p a s -> p (a s)")
            a = C(lambda e: e.activation(self.yph[:, :, :].rearrange("p a s -> p (a s)"), pT, ACT.Copy), v, *f)
            v = V(lambda e: e.tensor_tensor(self.ypl[:, :, :].rearrange("p a s -> p (a s)"), pT,
                                            self.yph[:, :, :].rearrange("p a s -> p (a s)").bitcast(F32),
                                            ALU.subtract), a, *f)
            for s in range(4):
                for t in range(2):
                    Yp.ready[(s, t)] = [a, v]
            self.g_free[1] = [v]
            self.kt_free = [tok]
            pool_done.append(v)

        self.lanes[3].append(pool())
        qk = []
        self.turned_group(self.X, [(W, (l,), 512 * i, 4, 416, 512) for i in range(2)], 0, qk_epi(self.dqT, 0, qk))
        self.turned_group(self.X, [(W, (l,), 512 * i, 4, 928, 512) for i in range(2)], 1, qk_epi(self.dkT, 1, qk))
        self.dqk_tok = [qk[-1]]

        def diff_lane(i):
            for _ in range(STAGGER * i):
                yield
            for h in range(i, 8, 3):
                yield from self.diff_head(i, l, h)
        for i in range(3):
            self.lanes[i].append(diff_lane(i))
        self.group(self.cols(W, l, 1440, 0, self.copy_epi(lambda t: self.dv[:, t, :], 0, 512, self.dv_toks)))
        while not pool_done:
            self.pump()

        kr_tok = self.rope(0, self.kr[:, :, :].unsqueeze(2), 1, 96, 64, self.cn[:, 1, :], *kr_toks,
                           *C1.ready[(2, 0)], *C1.ready[(2, 1)])
        q_toks = []

        def q_epi(t, tok):
            for b in range(2):
                bank = self.main[t][b]
                a = C(lambda e, b=b, bank=bank: e.activation(
                    self.q[:, t, 4 * b:4 * b + 4, :], bank[:, 0:384].rearrange("p (h n) -> p h n", n=96), ACT.Copy),
                    tok, kr_tok, *f)
                bank.free = [a]
            q_toks.append(a)
        self.group([dict(key=("mla_w_uq", (l,), 0, 2, 0, 768), X=C1, slots=[0, 1],
                         segs=[(0, 0, 384), (1, 384, 768)], first=True, last=True, epi=q_epi)])
        self.latent_kv(l, C1, kr_tok, q_toks, f)
        X = self.X

        yo = self.q[:, :, :, :].rearrange("p t h n -> p t (h n)")
        turned = {}

        def mla_lane(i):
            for h in range(i, 8, 3):
                hs = slice(64 * h, 64 * h + 64)
                yield from self.plain_head(
                    i, 96 ** -0.5, [self.q[:, t, h, :] for t in range(2)],
                    lambda n, h=h: self.kT[0:96, h, 0:n], [self.v[:, t, hs] for t in range(2)], 64,
                    [yo[:, t, hs] for t in range(2)], self.mla_done, turned, h)

        Yd = Turned("Yd", self.yph, self.ypl)

        def diff_end():
            while len(self.diff_done) < 8:
                yield
            c = (1 - (0.8 - 0.6 * math.exp(-0.3 * l))) ** -2
            p = self.pool.put(lambda e: e.tensor_scalar(self.ssq[:, :, :], self.ssq[:, :, :], c / 64, c * EPS,
                                                        ALU.mult, ALU.add), *self.diff_done)
            p = self.pool.put(lambda e: e.tensor_tensor(
                self.ssq[:, :, :].rearrange("p a b -> p (a b)"), self.ssq[:, :, :].rearrange("p a b -> p (a b)"),
                self.nhalf[:, :].broadcast_to([P, 16]), ALU.pow), p)
            yield
            yield
            yield
            for t in range(2):
                y = self.pin[:, t, :].rearrange("p (h n) -> p h n", n=64)
                v = V(lambda e: e.tensor_tensor(y, y, self.ssq[:, t, :].unsqueeze(2).broadcast_to([P, 8, 64]),
                                                ALU.mult), p)
                v = V(lambda e: e.tensor_tensor(y, y, self.sub[:, :].unsqueeze(1).broadcast_to([P, 8, 64]),
                                                ALU.mult), v, k_sub)
                yield
            while not pooled:
                yield
            Yd.used = dict(Yp.used)
            for t in range(2):
                self.turn(Yd, 0, t, [self.pin[:, t, i * P:i * P + P] for i in range(4)], v)
                yield

        def mla_end():
            while len(self.mla_done) < 8:
                yield
            for t in range(2):
                self.turn(X, 0, t, [yo[:, t, P * i:P * i + P] for i in range(4)], *self.mla_done)
                yield
        for i in range(3):
            self.lanes[i].append(mla_lane(i))
        pooled = []
        self.lanes[3].append(diff_end())
        self.gates(W, l, 2464 + 2048, 0)
        self.m_free = self.fence()
        self.branch("w_branch", l, 2, Yp, 0, 0, True, False)
        pooled.append(True)
        self.gates(W, l, 2464 + 1024, 1)
        self.gates(W, l, 2464, 0)
        X.ready.clear()
        self.lanes[3].append(mla_end())
        self.branch("w_branch", l, 1, Yd, 0, 1, False, False)
        while (3, 1) not in X.ready:
            self.pump()
        self.merged_ready()
        self.branch("w_branch", l, 0, X, 0, 0, False, True)
        self.way_out("w_out", l, after)

    def latent_kv(self, l, C1, kr_tok, q_toks, f):
        V, C, T = self.dve.put, self.act.put, self.pe.put
        j = self.take(("mla_w_ukv", (l,), 0, 1, 0, 1024))
        dry = self.plan is None
        if not dry:
            wh, wl = self.weights(j)
            waits = list(self.split_tok[j]) + self.need(C1, [2], [0, 1])
        banks = [self.main[0][0], self.main[0][1], self.main[1][0], self.main[1][1]]
        sides = [self.side(), self.side()]
        toks = []
        if not dry:
            for t in range(2):
                bank = sides[t]
                for n, (x, w) in enumerate(((C1.h, wl), (C1.h, wh), (C1.l, wh))):
                    tok = T(lambda e, bank=bank, x=x[:, 2, t * P:t * P + P],
                            w=w[:, 0, :].rearrange("p (h n) -> p h n", n=128)[:, :, 64:128], n=n:
                            e.matmul(bank[:, :], x, w, start=(n == 0), stop=(n == 2)),
                            *(waits + bank.free if n == 0 else []), inc=(n == 2))
                toks.append(tok)
            for i, bank in enumerate(banks):
                for h in (2 * i, 2 * i + 1):
                    for n, (w, x) in enumerate(((wl, C1.h), (wh, C1.h), (wh, C1.l))):
                        tok = T(lambda e, bank=bank, h=h, w=w[:, 0, h * P:h * P + P], x=x[:, 2, :], n=n: e.matmul(
                            bank[:, (h % 2) * S:(h % 2) * S + S], w, x, start=(n == 0), stop=(n == 2),
                            skip_group_check=True),
                            *(bank.free if n == 0 and h % 2 == 0 else []), inc=(n == 2))
                toks.append(tok)
            self.done_tok[j] = [tok]
        else:
            toks = [(self.pe.sem, 0)] * 6
        for t in range(2):
            a = C(lambda e, t=t: e.activation(self.v[:, t, :], sides[t][:, :], ACT.Copy), toks[t], *f)
            sides[t].free = [a]
        for i, bank in enumerate(banks):
            k = V(lambda e, i=i, bank=bank: e.tensor_copy(
                self.kT[0:64, 2 * i:2 * i + 2, :], bank[0:64, :].rearrange("p (a s) -> p a s", s=S)), toks[2 + i],
                *self.kt_free)
            bank.free = [k]
        v = kr_tok
        bank = self.side()
        for t in range(2):
            tok = T(lambda e, t=t, bank=bank: e.transpose(bank[0:96, t * P:t * P + P], self.kr[:, t, :],
                                                          self.ident[:, :]),
                    *([v, self.memset_tok] + bank.free if t == 0 else []), inc=(t == 1))
        kr = bank[64:96, 0:256].unsqueeze(1).broadcast_to([32, 4, S])
        a = C(lambda e: e.activation(self.kT[64:96, 0:4, :], kr, ACT.Copy), tok, *self.kt_free)
        b = C(lambda e: e.activation(self.kT[64:96, 4:8, :], kr, ACT.Copy))
        bank.free = [b]
        v = self.rope(0, self.q, 8, 96, 64, self.rope_tmp, *q_toks, v, self.pe.last())
        self.qk_tok = [v, b, a, k]
        self.tick()

    def loads2(self, l):
        A, f = self.A, self.ffn_fence
        return (self.ld("ws", self.ws[:, :, :], A["gmlp_w_s_2"][l].rearrange("g t s -> t g s"), *f),
                self.ld("tril", self.tril[:, :], A["c_tril"][:, 0:P], *f),
                self.ld("lng", self.lng[:, :, :], A["lng"][l].partition_broadcast(P), *f),
                self.ld("gp", self.gp[:, :], A["gp"][l], *f),
                self.ld("wgu", self.wgu[0:16, :], A["w_gate_up_2"][l], *f))

    def mixer2(self, l, after):
        A, V, C, T = self.A, self.dve.put, self.act.put, self.pe.put
        f = self.fence()
        self.r_free = f
        self.g_free, self.g_tok, self.m_tok = [list(f), list(f)], {}, {}
        self.lane_free = [list(f) for _ in range(3)]
        W, X = "w_in_2", self.X
        k_ws, k_tril, k_lng, k_gp, k_wgu = self.loads

        Yg = Turned("Yg", self.yph, self.ypl)
        for s in range(4):
            for t in range(2):
                Yg.used[(s, t)] = list(f)
        gm_done = []
        zv_tok, zu_toks = {}, {}

        def wst():
            for _ in range(8):
                yield
            bank = self.side()
            for g in range(4):
                tok = T(lambda e: e.transpose(bank[:, g * P:g * P + P], self.ws[:, g, :], self.ident[:, :]),
                        *([k_ws] + bank.free if g == 0 else []), inc=(g == 3))
            v = V(lambda e: e.tensor_tensor(self.wsT[:, :, :], bank[:, :].rearrange("p (g t) -> p g t", g=4),
                                            self.tril[:, :].unsqueeze(1).broadcast_to([P, 4, P]), ALU.mult),
                  tok, k_tril, *f)
            bank.free = [v]
            self.ws_tok = v

        def gelu_epi(b, dst, toks):
            def epi(t, tok):
                bank = self.main[t][b]
                a = C(lambda e: e.activation(dst[:, t, :], bank[:, :], ACT.Gelu), tok, *f, *self.xn_free[0],
                      *self.xn_free[1])
                bank.free = [a]
                toks[t] = a
                if b == 1:
                    self.lanes[3].append(gmlp(t))
            return epi

        def gmlp(t):
            yield
            bn = self.bn[:, t, :]
            z = self.zv[:, t, :]
            v = V(lambda e: e.bn_stats(bn[:, 0:6], z), zv_tok[t], *self.h_tok[t])
            v = V(lambda e: e.bn_aggr(bn[:, 12:14], bn[:, 0:6]), v)
            v = self.rsqrt(bn[:, 14:15], bn[:, 13:14], LN_EPS, v)
            v = V(lambda e: e.tensor_scalar(z, z, bn[:, 12:13], bn[:, 14:15], ALU.subtract, ALU.mult), v)
            v = V(lambda e: e.tensor_tensor(z, z, self.lng[:, 0, :], ALU.mult), v, k_lng)
            v = V(lambda e: e.tensor_tensor(z, z, self.lng[:, 1, :], ALU.add), v)
            yield
            yield
            bank = self.side()
            for g in range(4):
                tok = T(lambda e: e.matmul(bank[:, g * P:g * P + P], self.wsT[:, g, :],
                                           self.zv[:, t, g * P:g * P + P], start=True, stop=True),
                        *([v, self.ws_tok] + bank.free if g == 0 else []), inc=(g == 3))
            for g in range(4):
                u = self.zu[:, t, g * P:g * P + P]
                v = V(lambda e: e.scalar_tensor_tensor(u, bank[:, g * P:g * P + P], self.gp[:, 5 + g:6 + g], u,
                                                       ALU.add, ALU.mult), tok, zu_toks[t], k_gp)
            bank.free = [v]
            yield
            yield
            tok = self.turn(Yg, 0, t, [self.zu[:, t, g * P:g * P + P] for g in range(4)], v)
            gm_done.append(tok)

        self.lanes[3].append(wst())
        mv_t, mq_t, mk_t, gv_t, gq_t, gk_t, gg_t = ([] for _ in range(7))
        flat = lambda x, t: x[:, t, :, :].rearrange("p h n -> p (h n)")
        self.group(self.cols(W, l, 4112, 0, self.copy_epi(lambda t: self.mv[:, t, :], 0, 512, mv_t)) +
                   self.cols(W, l, 3088, 1, self.copy_epi(lambda t: flat(self.mq, t), 1, 512, mq_t)),
                   apart=True)
        self.group(self.cols(W, l, 3600, 0, self.copy_epi(lambda t: flat(self.mk, t), 0, 512, mk_t)))
        v = self.rope(1, self.mq, 4, 128, 0, self.lG[0][:, :, :].rearrange("p a b -> p (a b)"), *mq_t,
                      *self.lane_free[0])
        v = self.rope(1, self.mk, 4, 128, 0, self.lG[0][:, :, :].rearrange("p a b -> p (a b)"), *mk_t, v)
        self.lane_free[0] = [v]
        self.qk_tok = [v]
        moba_done, gla_done = [], []

        def moba_lane(i, heads):
            for _ in range(2 + STAGGER * i):
                yield
            for h in heads:
                yield from self.plain_head(
                    i, 128 ** -0.5, [x[:, t, h, :] for x in (self.mq, self.mk) for t in range(2)],
                    lambda n, i=i: self.lQ[i][:, 256:256 + n], [self.mv[:, t, h * P:h * P + P] for t in range(2)],
                    128, [self.mq[:, t, h, :] for t in range(2)], moba_done)
        for i, heads in enumerate(((0, 3), (1,), (2,))):
            self.lanes[i].append(moba_lane(i, heads))
        self.group(self.cols(W, l, 2576, 0, gelu_epi(0, self.zv, zv_tok)) +
                   self.cols(W, l, 2064, 1, gelu_epi(1, self.zu, zu_toks)))

        def t_epi(dst, b, toks, silu=False):
            def epi(tok):
                for i in range(2):
                    bank = self.main[i][b]
                    o = dst[:, 2 * i:2 * i + 2, :].rearrange("p a s -> p (a s)")
                    if silu:
                        a = C(lambda e: e.activation(o, bank[:, :], ACT.Tanh, scale=0.5), tok, *f)
                        a = V(lambda e: e.scalar_tensor_tensor(o, o, 1.0, bank[:, :], ALU.add, ALU.mult), a)
                    else:
                        a = C(lambda e: e.activation(o, bank[:, :], ACT.Copy), tok, *f)
                    bank.free = [a]
                    toks.append(a)
            return epi
        wide = lambda c0: [(W, (l,), 512 * i, 4, c0, 512) for i in range(2)]

        def decay():
            while len(gm_done) < 2:
                yield
            wt, a = self.ws_tok, lr_t[0]
            for i in range(2):
                bank = self.side()
                for h in (2 * i, 2 * i + 1):
                    tok = T(lambda e: e.matmul(bank[:, (h % 2) * S:(h % 2) * S + S], self.wgu[0:16, h * P:h * P + P],
                                               self.lrT[0:16, :], start=True, stop=True), a, k_wgu,
                            *(bank.free if h % 2 == 0 else []))
                for h in (2 * i, 2 * i + 1):
                    s = bank[:, (h % 2) * S:(h % 2) * S + S]
                    b = C(lambda e: e.activation(self.bigE[:, h, :], s, ACT.Abs, bias=self.gp[:, h:h + 1]), tok,
                          k_gp, wt, *gm_done)
                for h in (2 * i, 2 * i + 1):
                    s = bank[:, (h % 2) * S:(h % 2) * S + S]
                    v = V(lambda e: e.tensor_scalar(self.bigL[:, h, :], s, self.gp[:, h:h + 1], 0.0, ALU.add,
                                                    ALU.min), b)
                bank.free = [v, b]
                yield
            a = C(lambda e: e.activation(self.bigE[:, :, :], self.bigE[:, :, :], ACT.Exp, scale=-1.0), v)
            a = C(lambda e: e.activation(self.bigE[:, :, :], self.bigE[:, :, :], ACT.Ln, bias=self.one[:, :]), a,
                  self.memset_tok)
            v = V(lambda e: e.tensor_tensor(self.bigL[:, :, :], self.bigL[:, :, :], self.bigE[:, :, :],
                                            ALU.subtract), a)
            self.decay_tok = [v]
        self.decay_tok, lr_t = [], []
        self.turned_group(X, wide(0), 0, t_epi(self.gqT, 0, gq_t))
        self.turned_group(X, wide(512), 1, t_epi(self.gkT, 1, gk_t))
        j = self.take((W, (l,), 0, 8, 2048, 16))
        tok = (self.pe.sem, 0)
        if self.plan is not None:
            wh, wl = self.weights(j)
            bank = self.main[0][1]
            waits = list(self.split_tok[j]) + self.need(X, range(8), [0, 1]) + bank.free
            for k in range(8):
                for n, (w, x) in enumerate(((wl, X.h), (wh, X.h), (wh, X.l))):
                    tok = T(lambda e, w=w[:, k, :], x=x[:, k, :], st=(k == 0 and n == 0), sp=(k == 7 and n == 2):
                            e.matmul(bank[0:16, 0:256], w, x, start=st, stop=sp), *waits, inc=(k == 7 and n == 2))
                    waits = []
            for k in range(8):
                X.used[(k, 0)] = X.used[(k, 1)] = [tok]
            self.done_tok[j] = [tok]
        bank = self.main[0][1]
        lr_t.append(C(lambda e: e.activation(self.lrT[0:16, :], bank[0:16, 0:256], ACT.Copy), tok, *f))
        bank.free = list(lr_t)

        self.lanes[3].append(decay())
        self.group(self.cols(W, l, 1024, 0, self.copy_epi(lambda t: self.gv[:, t, :], 0, 512, gv_t)))
        self.turned_group(X, wide(1536), 1, t_epi(self.ggT, 1, gg_t, True))
        while not self.decay_tok:
            self.pump()

        def gla_lane(i, heads):
            for _ in range(STAGGER * i):
                yield
            for h in heads:
                yield from self.gla_head(i, h, gq_t + gk_t, gv_t, gg_t, gla_done)
        for i, heads in enumerate(((0, 3), (1,), (2,))):
            self.lanes[i].append(gla_lane(i, heads))

        Ym = Turned("Ym", self.yph, self.ypl)

        def moba_end():
            while len(moba_done) < 4:
                yield
            for t in range(2):
                self.turn(Ym, 0, t, [self.mq[:, t, h, :] for h in range(4)], *moba_done)
                yield

        def gla_end():
            while len(gla_done) < 4:
                yield
            hi, lo = X.h[:, 4:8, :], X.l[:, 4:8, :]
            war = [x for s in range(4, 8) for t in range(2) for x in X.used[(s, t)]]
            a = C(lambda e: e.activation(hi, self.ggT[:, :, :], ACT.Copy), *gla_done, *war)
            v = V(lambda e: e.tensor_tensor(lo, self.ggT[:, :, :], hi.bitcast(F32), ALU.subtract), a)
            for s in range(4, 8):
                for t in range(2):
                    X.ready[(s, t)] = [a, v]
        G0 = 4624
        self.gates(W, l, G0 + 1024, 0)
        self.gates(W, l, G0 + 2048, 1)
        self.m_free = self.fence()
        self.branch("w_branch_2", l, 1, Yg, 0, 0, True, False)
        Ym.used = dict(Yg.used)
        self.lanes[3].append(moba_end())
        self.gates(W, l, G0, 0)
        X.ready.clear()
        self.lanes[3].append(gla_end())
        self.branch("w_branch_2", l, 2, Ym, 0, 1, False, False)
        while (7, 1) not in X.ready:
            self.pump()
        self.merged_ready()
        self.branch("w_branch_2", l, 0, X, 4, 0, False, True)
        self.way_out("w_out_2", l, after)

    def gla_head(self, i, h, qk_t, gv_t, gg_t, done):
        V, C, T = self.dve.put, self.act.put, self.pe.put
        G = self.lG[i]
        flat = G[:, :, :].rearrange("p a b -> p (a b)")
        eb, kd, enb = flat[:, 0:256], flat[:, 256:512], flat[:, 512:768]
        kdn, at = G[:, 2:4, :], G[:, 4:6, :]
        S1, S2, S3 = self.bigL[:, h, 0:128], self.bigL[:, h, 128:256], G[:, 6, :]
        st = self.st[:, 16 * i:16 * i + 4]
        bc, E = self.bigL[:, h, :], self.bigE[:, h, :]
        gq, gk, gg = self.gqT[:, h, :], self.gkT[:, h, :], self.ggT[:, h, :]
        gv = [self.gv[:, t, h * P:h * P + P] for t in range(2)]
        free = self.lane_free[i]
        v = V(lambda e: e.tensor_tensor_scan(E, self.scan[:, :], bc, 0.0, ALU.mult, ALU.add), *self.decay_tok)
        w = V(lambda e: e.tensor_scalar(st, E[:, 63:256:64], 1 / 16, None, ALU.mult), v, *free)
        a = C(lambda e: e.activation(eb, E, ACT.Exp, scale=1 / 16), v, *free)
        a = C(lambda e: e.activation(enb, E, ACT.Exp, scale=-1 / 16))
        for c in range(3):
            b = C(lambda e: e.activation(kd[:, 64 * c:64 * c + 64], E[:, 64 * c:64 * c + 64], ACT.Exp,
                                         bias=st[:, c:c + 1], scale=-1 / 16), w)
        yield
        yield
        kdv = V(lambda e: e.tensor_tensor(kd[:, 0:192], kd[:, 0:192], gk[:, 0:192], ALU.mult), b, *qk_t)
        qd = V(lambda e: e.scalar_tensor_tensor(gq, gq, 128 ** -0.5, eb, ALU.mult, ALU.mult), a)
        ki = V(lambda e: e.tensor_tensor(gk, gk, enb, ALU.mult), a, kdv)
        z = V(lambda e: e.memset(at, 0.0), ki)
        yield
        yield
        bank = self.side()
        T(lambda e: e.transpose(bank[:, 0:128], kd[:, 0:128], self.ident[:, :]), kdv, *bank.free, inc=False)
        t1 = T(lambda e: e.transpose(bank[0:64, 128:256], kd[:, 128:192], self.ident[:, :]))
        bank2 = self.side()
        for t in range(2):
            ts = slice(t * P, t * P + P)
            t2 = T(lambda e: e.matmul(bank2[:, ts], gk[:, ts], gq[:, ts], start=True, stop=True), qd, ki,
                   *bank2.free)
        a = C(lambda e: e.activation(kdn[:, 0, :], bank[:, 0:128], ACT.Copy), t1)
        a = C(lambda e: e.activation(kdn[0:64, 1, :], bank[0:64, 128:256], ACT.Copy), t1)
        bank.free = [a]
        for t in range(2):
            m = V(lambda e: e.copy_predicated(at[:, t, :], self.chunk[:, :], bank2[:, t * P:t * P + P]), t2, z,
                  self.chunk_tok)
        bank2.free = [m]
        yield
        yield
        bank, bank2 = self.side(), self.side()
        T(lambda e: e.matmul(bank[:, 0:128], kdn[0:64, 0, :], gv[0][0:64, :], start=True, stop=True), a, *gv_t,
          *bank.free, inc=False)
        t1 = T(lambda e: e.matmul(bank[:, 128:256], kdn[0:64, 1, :], gv[1][0:64, :], start=True, stop=True))
        t2 = T(lambda e: e.matmul(bank2[:, 0:128], kdn[64:128, 0, :], gv[0][64:128, :], start=True, stop=True),
               *bank2.free)
        v = V(lambda e: e.tensor_copy(S1, bank[:, 0:128]), t1, v)
        v = V(lambda e: e.scalar_tensor_tensor(S2, S1, eb[:, 127:128], bank2[:, 0:128], ALU.mult, ALU.add), v, t2)
        bank2.free = [v]
        v = V(lambda e: e.scalar_tensor_tensor(S3, S2, eb[:, 191:192], bank[:, 128:256], ALU.mult, ALU.add), v)
        bank.free = [v]
        yield
        yield
        bank = self.side()
        w = [v, m] + bank.free
        for t in range(2):
            T(lambda e: e.matmul(bank[:, t * P:t * P + P], gv[t], at[:, t, :], start=(t == 0), stop=False,
                                 skip_group_check=True), *w, inc=False)
        for c, s in ((1, S1), (2, S2), (3, S3)):
            tok = T(lambda e: e.matmul(bank[:, 64 * c:64 * c + 64], s, gq[:, 64 * c:64 * c + 64], start=False,
                                       stop=True, skip_group_check=True))
        a = C(lambda e: e.activation(E, bank[:, 0:256], ACT.Square), tok)
        o = kd
        b = C(lambda e: e.activation(o, bank[:, 0:256], ACT.Copy), tok)
        bank.free = [b]
        yield
        yield
        bank = self.side()
        w = [a, self.memset_tok] + bank.free
        for t in range(2):
            tok = T(lambda e: e.matmul(bank[:, t:t + 1], E[:, t * P:t * P + P], self.ones[:, 0:1], start=True,
                                       stop=True), *w, inc=(t == 1))
        v = V(lambda e: e.tensor_scalar(st[:, 0:2], bank[:, 0:2], EPS, None, ALU.add), tok)
        bank.free = [v]
        half = self.nhalf[:, :].broadcast_to([P, 2])
        p = self.pool.put(lambda e: e.tensor_tensor(st[:, 0:2], st[:, 0:2], half, ALU.pow), v)
        yield
        yield
        bank = self.side()
        w = [p] + bank.free
        for t in range(2):
            tok = T(lambda e: e.matmul(bank[:, t * P:t * P + P], st[:, t:t + 1].broadcast_to([P, P]),
                                       self.ident[:, :], start=True, stop=True), *w, inc=(t == 1))
        v = V(lambda e: e.scalar_tensor_tensor(o, o, self.gp[:, 4:5], bank[:, 0:256], ALU.mult, ALU.mult), b, tok)
        bank.free = [v]
        v = V(lambda e: e.scalar_tensor_tensor(gg, o, 0.5, gg, ALU.mult, ALU.mult), v, *gg_t)
        self.lane_free[i] = [v]
        done.append(v)

    def run(self):
        A = self.A
        self.start()
        for l in range(L):
            self.ffn1(l, "ffn1", self.to_rms(A["mix_norm"][l]), lambda: self.loads1(l))
            self.mixer1(l, self.to_rms(A["ffn2_norm"][l]))
            last = l == L - 1
            self.ffn1(l, "ffn2", self.to_rms(A["final_norm"] if last else A["ffn1_norm"][l + 1], last),
                      lambda: self.loads2(0) if last else None)
        self.chunk_load()
        for l in range(L):
            self.mixer2(l, self.to_ln(A["ln1_g_2"][l], A["ln1_b_2"][l]))
            last = l == L - 1
            self.ffn2(l, self.to_ln(A["ln2_g_2"][l], A["ln2_b_2"][l], last),
                      lambda: None if last else self.loads2(l + 1))

    def chunk_load(self):
        self.chunk_tok = self.ld("chunk", self.chunk[:, :], self.A["c_chunk"])

    def to_rms(self, vec, final=False):
        g = self.gain_load(vec)

        def after(t, b):
            self.rms_half(t, b)
            if b:
                x, v = self.rms(t, g, final)
                self.turn_x(t, x, v, NORM_WAIT, scale=final)
        return after

    def to_ln(self, gvec, bvec, last=False):
        g = [self.gain_load(gvec), self.gain_load(bvec)]

        def after(t, b):
            self.ln_half(t, b)
            if b:
                h, v = self.layer_norm(t, *g)
                if last:
                    for i in range(2):
                        c = slice(512 * i, 512 * i + 512)
                        self.sp.dma(self.out[0, t * P:t * P + P, c], h[:, c], self.s_out, 0, v[i])
                else:
                    self.turn_x(t, h, v, NORM_WAIT, scale=True)
        return after


_INS = ["x", "ffn1_norm", "ffn1_w_gate", "ffn1_w_up", "ffn1_w_down", "mix_norm", "w_in", "mla_w_uq", "mla_w_ukv",
        "diff_subln", "pool_w", "w_branch", "w_out", "ffn2_norm", "ffn2_w_gate", "ffn2_w_up", "ffn2_w_down",
        "final_norm", "w_in_2", "w_gate_up_2", "gmlp_w_s_2", "w_branch_2", "w_out_2", "ln1_g_2", "ln1_b_2",
        "w_ff1_2", "w_ff2_2", "ln2_g_2", "ln2_b_2"]


def layouts(inp):
    a = {k: np.ascontiguousarray(inp[k]) for k in _INS}
    g = {k: np.asarray(v) for k, v in inp.items()}
    a["gq"] = np.concatenate([g["mla_q_norm"], g["mla_kv_norm"]], 1)
    a["pbs"] = np.concatenate([g["pool_b"].transpose(0, 2, 1),
                               g["pool_scale"].reshape(L, 4, P).transpose(0, 2, 1)], 2)
    a["lams"] = np.stack([g["diff_lambda_q1"], g["diff_lambda_k1"], g["diff_lambda_q2"], g["diff_lambda_k2"]],
                         1).reshape(L * 128)
    a["lng"] = np.stack([g["gmlp_ln_g_2"], g["gmlp_ln_b_2"]], 1)
    a["gp"] = np.concatenate([g["b_gate_2"].reshape(L, 4, P).transpose(0, 2, 1), g["gla_norm_w_2"][:, :, None],
                              g["gmlp_b_s_2"].transpose(0, 2, 1)], 2)
    p1, p2 = g["positions"][0], g["positions_2"][0]
    a["pos_row"] = p1
    a["pos_col"] = np.stack([p1[0:P], p1[P:], p2[0:P], p2[P:]], 1)
    a.update(constants())
    a["c_chunk"] = a["c_tril"][:, P:].astype(np.uint32)
    a["c_tril"] = a["c_tril"][:, :P]
    return {k: np.ascontiguousarray(v) for k, v in a.items()}


def build(nc, A, out):
    with ExitStack() as ctx:
        net = Net(nc, A, out, ctx)
        net.reset(None)
        net.run()
        plan = net.units
        net.reset(plan)
        net.run()
        assert net.units == plan and net.n_low == len(plan)
        block = ctx.enter_context(nc.Block())

        @block.sync
        def _(eng):
            net.sp.issue(eng)
            eng.wait_ge(net.s_out, 64)

        @block.gpsimd
        def _(eng):
            net.pool.issue(eng)

        @block.scalar
        def _(eng):
            net.act.issue(eng)

        @block.vector
        def _(eng):
            net.dve.issue(eng)

        @block.tensor
        def _(eng):
            net.pe.issue(eng)
    return net


def kernel(**inputs):
    import concourse.bacc as _bacc
    from concourse.bass_utils import run_bass_kernel_spmd as _run

    nc = _bacc.Bacc("TRN2", target_bir_lowering=False, num_devices=1)
    arrays, args = {}, {}
    for name, a in layouts(inputs).items():
        arrays[f"in_{name}_dram"] = a
        args[name] = nc.dram_tensor(f"in_{name}_dram", a.shape, mybir.dt.from_np(a.dtype), kind="ExternalInput").ap()
    out = nc.dram_tensor("out_0_dram", (1, S, D), F32, kind="ExternalOutput").ap()
    build(nc, args, out)
    r = _run(nc, [arrays], core_ids=[0])
    return r.results[0]["out_0_dram"]
```
